# Optimizing a Trainium2 kernel written in Bass

```python
import jax, jax.numpy as jnp
from jax import lax
import numpy as np

D_MODEL = 1024
BATCH = 1
SEQ = 1024
DEPTH = 1

HEAD_DIM = 64
SWA_Q_HEADS = 8
SWA_KV_HEADS = 2
SWA_GROUP = SWA_Q_HEADS // SWA_KV_HEADS
WINDOW = 128
BLOCK = 128
FOX_HEADS = 8
ROPE_THETA = 10000.0
SWA_Q_W = SWA_Q_HEADS * HEAD_DIM
SWA_KV_W = SWA_KV_HEADS * HEAD_DIM
FOX_W = FOX_HEADS * HEAD_DIM
MIX_WIDTH = SWA_Q_W + FOX_W
IN_PROJ_W = SWA_Q_W + 2 * SWA_KV_W + 3 * FOX_W + FOX_HEADS

PEER_HEADS = 8
PEER_N_KEYS = 128
PEER_N_EXPERTS = PEER_N_KEYS ** 2
PEER_QUERY_DIM = 256
PEER_HALF = PEER_QUERY_DIM // 2
PEER_TOPK = 16
PEER_CHUNK = 128

PLE_DIM = 256

RMS_EPS = 1e-6

kernel_name = "hymba_swa_fox_peer_layer"

def rmsnorm(x, g):
    xf = x.astype(jnp.float32)
    r = xf * lax.rsqrt(jnp.mean(xf * xf, axis=-1, keepdims=True) + RMS_EPS)
    return (r * g.astype(jnp.float32)).astype(x.dtype)

def rope_tables(seq):
    pos = jnp.arange(seq, dtype=jnp.float32)
    inv_freq = ROPE_THETA ** (-jnp.arange(0, HEAD_DIM, 2, dtype=jnp.float32) / HEAD_DIM)
    ang = pos[:, None] * inv_freq[None, :]
    ang = jnp.concatenate([ang, ang], axis=-1)
    return jnp.cos(ang), jnp.sin(ang)

def apply_rope(t, cos, sin):
    tf = t.astype(jnp.float32)
    t1, t2 = jnp.split(tf, 2, axis=-1)
    rot = jnp.concatenate([-t2, t1], axis=-1)
    out = tf * cos[None, :, None, :] + rot * sin[None, :, None, :]
    return out.astype(t.dtype)

def swa_sink_attention(q, k, v, sinks):
    B, S = q.shape[0], q.shape[1]
    nb = S // BLOCK
    qb = q.reshape(B, nb, BLOCK, SWA_KV_HEADS, SWA_GROUP, HEAD_DIM)

    def band(t):
        tb = t.reshape(B, nb, BLOCK, SWA_KV_HEADS, HEAD_DIM)
        prev = jnp.pad(tb[:, :-1], ((0, 0), (1, 0), (0, 0), (0, 0), (0, 0)))
        return jnp.concatenate([prev, tb], axis=2)

    kb, vb = band(k), band(v)
    s = jnp.einsum('bnqhgd,bnkhd->bnhgqk', qb, kb,
                   preferred_element_type=jnp.float32) * (HEAD_DIM ** -0.5)
    qi = jnp.arange(BLOCK)[:, None] + BLOCK
    ki = jnp.arange(2 * BLOCK)[None, :]
    rel = qi - ki
    in_window = (rel >= 0) & (rel < WINDOW)
    blk = jnp.arange(nb)
    real_key = (blk[:, None] > 0) | (ki >= BLOCK)
    mask = in_window[None] & real_key[:, None, :]
    s = jnp.where(mask[None, :, None, None], s, -jnp.inf)
    sk = sinks.astype(jnp.float32).reshape(1, 1, SWA_KV_HEADS, SWA_GROUP, 1, 1)
    m = jnp.maximum(jnp.max(s, axis=-1, keepdims=True), sk)
    e = jnp.exp(s - m)
    w = e / (jnp.sum(e, axis=-1, keepdims=True) + jnp.exp(sk - m))
    o = jnp.einsum('bnhgqk,bnkhd->bnqhgd', w.astype(v.dtype), vb)
    return o.reshape(B, S, SWA_Q_HEADS, HEAD_DIM)

def forgetting_attention(q, k, v, log_f):
    B, S, H, dh = q.shape
    nb = S // BLOCK
    c = jnp.cumsum(log_f, axis=1)
    c_keys = jnp.transpose(c, (0, 2, 1))
    qb = jnp.transpose(q.reshape(B, nb, BLOCK, H, dh), (1, 0, 2, 3, 4))
    cb = jnp.transpose(c.reshape(B, nb, BLOCK, H), (1, 0, 3, 2))
    kpos = jnp.arange(S)
    scale = dh ** -0.5

    def one_block(args):
        qi, ci, start = args
        s = jnp.einsum('bqhd,bkhd->bhqk', qi, k, preferred_element_type=jnp.float32) * scale
        s = s + ci[..., None] - c_keys[:, :, None, :]
        qpos = start + jnp.arange(BLOCK)
        s = jnp.where(qpos[:, None] >= kpos[None, :], s, -jnp.inf)
        w = jax.nn.softmax(s, axis=-1).astype(v.dtype)
        return jnp.einsum('bhqk,bkhd->bqhd', w, v)

    out = lax.map(one_block, (qb, cb, jnp.arange(nb) * BLOCK))
    return jnp.transpose(out, (1, 0, 2, 3, 4)).reshape(B, S, H, dh)

def peer(xn, w_query, sub_keys, expert_u, expert_v):
    B, S, D = xn.shape
    T = B * S
    K = PEER_TOPK
    xt = xn.reshape(T, D)
    q = (xt @ w_query).reshape(T, PEER_HEADS, 2, PEER_HALF)
    scores = jnp.einsum('thcd,ckd->thck', q, sub_keys,
                        preferred_element_type=jnp.float32)
    top_s, top_i = lax.top_k(scores, K)
    cand_s = (top_s[:, :, 0, :, None] + top_s[:, :, 1, None, :]).reshape(T, PEER_HEADS, K * K)
    cand_i = (top_i[:, :, 0, :, None] * PEER_N_KEYS + top_i[:, :, 1, None, :]).reshape(T, PEER_HEADS, K * K)
    best_s, best_pos = lax.top_k(cand_s, K)
    expert_idx = jnp.take_along_axis(cand_i, best_pos, axis=-1)
    gates = jax.nn.softmax(best_s, axis=-1)
    nc = T // PEER_CHUNK

    def one_chunk(args):
        xc, ic, gc = args
        u = jnp.take(expert_u, ic, axis=0)
        vv = jnp.take(expert_v, ic, axis=0)
        act = jax.nn.gelu(jnp.einsum('cd,chkd->chk', xc, u, preferred_element_type=jnp.float32),
                          approximate=False)
        coef = (gc * act).astype(xc.dtype)
        return jnp.einsum('chk,chkd->cd', coef, vv)

    y = lax.map(one_chunk, (xt.reshape(nc, PEER_CHUNK, D),
                            expert_idx.reshape(nc, PEER_CHUNK, PEER_HEADS, K),
                            gates.reshape(nc, PEER_CHUNK, PEER_HEADS, K)))
    return y.reshape(B, S, D)

def setup_inputs(seed: int = 0) -> dict:
    key = jax.random.key(seed)
    ks = jax.random.split(key, 20)
    f32 = jnp.float32
    D = D_MODEL

    def nrm(k, shape, scale):
        return jax.random.normal(k, shape, f32) * scale

    def gain(k, shape):
        return 1.0 + 0.02 * jax.random.normal(k, shape, f32)

    return {
        "x": jax.random.normal(ks[0], (BATCH, SEQ, D), f32),
        "p": jax.random.normal(ks[1], (DEPTH, BATCH, SEQ, PLE_DIM), f32),
        "norm_mix_g": gain(ks[2], (DEPTH, D)),
        "w_in": nrm(ks[3], (DEPTH, D, IN_PROJ_W), D ** -0.5),
        "b_forget": jax.random.uniform(ks[4], (DEPTH, FOX_HEADS), f32, 1.0, 4.0),
        "sinks": nrm(ks[5], (DEPTH, SWA_Q_HEADS), 0.5),
        "g_out_a": gain(ks[6], (DEPTH, SWA_Q_W)),
        "g_out_b": gain(ks[7], (DEPTH, FOX_W)),
        "w_out": nrm(ks[8], (DEPTH, MIX_WIDTH, D), MIX_WIDTH ** -0.5),
        "norm_ffn_g": gain(ks[9], (DEPTH, D)),
        "w_query": nrm(ks[10], (DEPTH, D, PEER_HEADS * PEER_QUERY_DIM), D ** -0.5),
        "sub_keys": nrm(ks[11], (DEPTH, 2, PEER_N_KEYS, PEER_HALF), PEER_HALF ** -0.5),
        "expert_u": nrm(ks[12], (DEPTH, PEER_N_EXPERTS, D), D ** -0.5),
        "expert_v": nrm(ks[13], (DEPTH, PEER_N_EXPERTS, D), PEER_HEADS ** -0.5),
        "norm_ple_g": gain(ks[14], (DEPTH, D)),
        "w_ple_gate": nrm(ks[15], (DEPTH, D, D), D ** -0.5),
        "w_ple_proj": nrm(ks[16], (DEPTH, PLE_DIM, D), PLE_DIM ** -0.5),
        "norm_final_g": gain(ks[17], (D,)),
    }

def reference(x, p, norm_mix_g, w_in, b_forget, sinks, g_out_a, g_out_b, w_out,
              norm_ffn_g, w_query, sub_keys, expert_u, expert_v,
              norm_ple_g, w_ple_gate, w_ple_proj, norm_final_g):
    B, S, D = x.shape
    cos, sin = rope_tables(S)
    o1 = SWA_Q_W
    o2 = o1 + SWA_KV_W
    o3 = o2 + SWA_KV_W
    o4 = o3 + FOX_W
    o5 = o4 + FOX_W
    o6 = o5 + FOX_W
    h = x
    for i in range(DEPTH):
        a = rmsnorm(h, norm_mix_g[i])
        proj = a @ w_in[i]
        qa = proj[..., :o1].reshape(B, S, SWA_Q_HEADS, HEAD_DIM)
        ka = proj[..., o1:o2].reshape(B, S, SWA_KV_HEADS, HEAD_DIM)
        va = proj[..., o2:o3].reshape(B, S, SWA_KV_HEADS, HEAD_DIM)
        qf = proj[..., o3:o4].reshape(B, S, FOX_HEADS, HEAD_DIM)
        kf = proj[..., o4:o5].reshape(B, S, FOX_HEADS, HEAD_DIM)
        vf = proj[..., o5:o6].reshape(B, S, FOX_HEADS, HEAD_DIM)
        log_f = jax.nn.log_sigmoid(proj[..., o6:].astype(jnp.float32)
                                   + b_forget[i].astype(jnp.float32))
        qa = apply_rope(qa, cos, sin)
        ka = apply_rope(ka, cos, sin)
        out_a = swa_sink_attention(qa, ka, va, sinks[i]).reshape(B, S, SWA_Q_W)
        out_b = forgetting_attention(qf, kf, vf, log_f).reshape(B, S, FOX_W)
        mixed = jnp.concatenate([rmsnorm(out_a, g_out_a[i]), rmsnorm(out_b, g_out_b[i])], axis=-1)
        h = h + mixed @ w_out[i]
        h = h + peer(rmsnorm(h, norm_ffn_g[i]), w_query[i], sub_keys[i], expert_u[i], expert_v[i])
        gate = jax.nn.sigmoid((rmsnorm(h, norm_ple_g[i]) @ w_ple_gate[i]).astype(jnp.float32))
        h = h + (gate * (p[i] @ w_ple_proj[i]).astype(jnp.float32)).astype(h.dtype)
    return rmsnorm(h, norm_final_g)


_drawn_inputs = setup_inputs


def setup_inputs(seed=0):
    import zlib

    import numpy as np

    out = dict(_drawn_inputs(seed))
    spreads = {}
    factors = {'sinks': 7.428,
     'g_out_a': 10.719,
     'g_out_b': 11.135,
     'norm_ffn_g': 10.625,
     'norm_ple_g': 64.0,
     'norm_final_g': 8.299}
    for name, (base, spread) in spreads.items():
        noise = np.random.default_rng([zlib.crc32(name.encode()), seed]).standard_normal(out[name].shape)
        drawn = base * np.exp(spread * noise) if base else spread * noise
        out[name] = __import__('jax').numpy.asarray(drawn.astype(out[name].dtype))
    for name, factor in factors.items():
        out[name] = (out[name] * factor).astype(out[name].dtype)
    return out
```

```python
from contextlib import ExitStack

import numpy as np

import concourse.bass as bass
from concourse import mybir

F32 = mybir.dt.float32
F32R = mybir.dt.float32r
BF16 = mybir.dt.bfloat16
U32 = mybir.dt.uint32
ACT = mybir.ActivationFunctionType
ALU = mybir.AluOpType
AX = mybir.AxisListType

P = 128
T = 1024
NT = T // P
D = 1024
DC = D // P
HALF = 512
HEAD = 64
SWA_HEADS, SWA_KV, FOX_HEADS = 8, 2, 8
PAIRS = 4
SWA_Q, SWA_K, FOX_Q, FOX_K = 0, 4, 5, 9
QK_CHUNKS = 13
V_COLS = SWA_KV * HEAD + FOX_HEADS * HEAD + FOX_HEADS
V_FOX = SWA_KV * HEAD
V_FORGET = V_FOX + FOX_HEADS * HEAD
V_PART = V_COLS // 2
PEER_HEADS, KEYS, TOPK = 8, 128, 16
HC = 2 * PEER_HEADS
SEL = PEER_HEADS * TOPK
EPS = 1e-6
NEG = -1e30
LOWEST = -3.4e38
FREE = 1
SCALE = HEAD ** -0.5


def spread(ap, at, n):
    shape = list(ap.shape)
    return ap.unsqueeze(at).broadcast_to(shape[:at] + [n] + shape[at:])


class Tools:

    def __init__(self, nc):
        self.nc, self.held = nc, []

    def sem(self, name):
        self.held.append(self.nc.alloc_semaphore(name=name))
        return self.held[-1]

    def recycle(self):
        self.nc.clear_and_free_semaphores(self.held)
        self.nc.all_engine_barrier()
        self.held = []

    def pair(self, name):
        return [self.sem(f"{name}{s}") for s in range(2)]

    def sb(self, ctx, name, shape, dt=F32, side="left"):
        return ctx.enter_context(self.nc.sbuf_tensor(name, shape, dt, side=side))

    def ps(self, ctx, name, shape, dt=F32):
        return ctx.enter_context(self.nc.psum_tensor(name, shape, dt))


def three_passes(pe, out, lhs_hi, lhs_lo, rhs_hi, rhs_lo, n, first=True, last=True):
    for k in range(n):
        pe.matmul(out, lhs_hi(k), rhs_hi(k), start=first and k == 0, stop=False)
        pe.matmul(out, lhs_hi(k), rhs_lo(k), start=False, stop=False)
        mm = pe.matmul(out, lhs_lo(k), rhs_hi(k), start=False, stop=last and k == n - 1)
    return mm


def token_pass(nc, tl, name, src, src_dram, groups, gain, ident, parts, weights, keep, epilogue):
    with ExitStack() as ctx:
        width = parts[1] if parts else 0
        n_parts = parts[0] if parts else 0
        square = tl.sb(ctx, f"{name}_square", [P, D])
        ssq = tl.sb(ctx, f"{name}_ssq", [P, NT, groups])
        root = tl.sb(ctx, f"{name}_root", [P, NT, groups])
        rstd = tl.sb(ctx, f"{name}_rstd", [P, NT, groups])
        scaled = tl.sb(ctx, f"{name}_scaled", [P, 2, D])
        act_hi = tl.sb(ctx, f"{name}_act_hi", [P, 2, DC, P], F32R)
        act_lo = tl.sb(ctx, f"{name}_act_lo", [P, 2, DC, P], F32R)
        turned = [tl.ps(ctx, f"{name}_turned{s}", [P, DC, P]) for s in range(2)]
        if weights is not None:
            w_raw = tl.sb(ctx, f"{name}_w_raw", [P, 2, n_parts * width])
            w_hi = tl.sb(ctx, f"{name}_w_hi", [P, DC, n_parts * width], F32R)
            w_lo = tl.sb(ctx, f"{name}_w_lo", [P, DC, n_parts * width], F32R)
            out = [tl.ps(ctx, f"{name}_out{s}", [P, n_parts, HALF]) for s in range(2)]
        src_loaded = tl.sem(f"{name}_src_loaded")
        w_loaded = tl.pair(f"{name}_w_loaded")
        w_hi_ready = tl.sem(f"{name}_w_hi_ready")
        w_ready = tl.sem(f"{name}_w_ready")
        squared = tl.sem(f"{name}_squared")
        rooted = tl.sem(f"{name}_rooted")
        rstd_ready = tl.sem(f"{name}_rstd_ready")
        scaled_ready = tl.pair(f"{name}_scaled_ready")
        turned_ready = tl.pair(f"{name}_turned_ready")
        hi_ready = tl.pair(f"{name}_hi_ready")
        lo_ready = tl.pair(f"{name}_lo_ready")
        kept = tl.pair(f"{name}_kept")
        out_ready = tl.pair(f"{name}_out_ready")
        out_read = tl.pair(f"{name}_out_read")
        block = ctx.enter_context(nc.Block())
        gw = D // groups

        @block.sync
        def _(sp):
            if src_dram is not None:
                sp.dma_start(src[:], src_dram.rearrange("(t p) d -> p t d", p=P)).then_inc(src_loaded, 16)
            if weights is not None:
                for k in range(DC):
                    if k >= 2:
                        sp.wait_ge(w_ready, k - 1)
                    sp.dma_start(w_raw[:, k % 2, :], weights[k, :, :]).then_inc(w_loaded[k % 2], 16)

        @block.scalar
        def _(act):
            if src_dram is not None:
                act.wait_ge(src_loaded, 16)
            for t in range(NT):
                for g in range(groups):
                    q = act.activation(square[:, 0:gw], src[:, t, g * gw:(g + 1) * gw], ACT.Square,
                                       accum_out=ssq[:, t, g:g + 1])
                    q.then_inc(squared, 1)
                    act.wait_ge(squared, t * groups + g + 1)
            act.activation(root[:], ssq[:], ACT.Sqrt, scale=1.0 / gw, bias=gain["eps"][:, 0:1]).then_inc(rooted, 1)
            if weights is not None:
                for k in range(DC):
                    act.wait_ge(w_loaded[k % 2], 16 * (k // 2 + 1))
                    act.copy(w_hi[:, k, :], w_raw[:, k % 2, :]).then_inc(w_hi_ready, 1)
            with act.Fori(0, NT // 2) as i:
                for s in range(2):
                    act.wait_ge(turned_ready[s], i + 1 + FREE)
                    if weights is not None:
                        act.wait_ge(out_ready[s], i + FREE)
                    if keep is not None:
                        act.wait_ge(kept[s], i + FREE)
                    for k in range(DC):
                        q = act.mul(act_hi[:, s, k, :], turned[s][:, k, :], gain["t"][:, k:k + 1])
                    q.then_inc(hi_ready[s], 1)

        @block.vector
        def _(dve):
            dve.wait_ge(rooted, 1)
            dve.reciprocal(rstd[:], root[:]).then_inc(rstd_ready, 1)
            if weights is not None:
                for k in range(DC):
                    dve.wait_ge(w_hi_ready, k + 1)
                    dve.tensor_tensor(w_lo[:, k, :], w_raw[:, k % 2, :], w_hi[:, k, :].bitcast(F32),
                                      ALU.subtract).then_inc(w_ready, 1)
            dve.wait_ge(rstd_ready, 1)
            for s in range(2):
                dve.sem_inc(lo_ready[s], FREE)
                dve.sem_inc(out_read[s], FREE)
            with dve.Fori(0, NT // 2) as i:
                for s in range(2):
                    t = i * 2 + s
                    dve.wait_ge(turned_ready[s], i + FREE)
                    for g in range(groups):
                        q = dve.tensor_scalar(scaled[:, s, g * gw:(g + 1) * gw], src[:, t, g * gw:(g + 1) * gw],
                                              rstd[:, t, g:g + 1], None, ALU.mult)
                    q.then_inc(scaled_ready[s], 1)
                for s in range(2):
                    dve.wait_ge(hi_ready[s], i + 1)
                    for k in range(DC):
                        q = dve.scalar_tensor_tensor(out=act_lo[:, s, k, :], in0=turned[s][:, k, :],
                                                     scalar=gain["t"][:, k:k + 1],
                                                     in1=act_hi[:, s, k, :].bitcast(F32),
                                                     op0=ALU.mult, op1=ALU.subtract)
                    q.then_inc(lo_ready[s], 1)
                if weights is not None:
                    for s in range(2):
                        dve.wait_ge(out_ready[s], i + 1 + FREE)
                        epilogue(dve, s, i * 2 + s, out[s]).then_inc(out_read[s], 1)

        @block.tensor
        def _(pe):
            for s in range(2):
                pe.sem_inc(turned_ready[s], FREE)
                pe.sem_inc(out_ready[s], FREE)
            if weights is not None:
                pe.wait_ge(w_ready, DC)
            with pe.Fori(0, NT // 2) as i:
                for s in range(2):
                    pe.wait_ge(scaled_ready[s], i + 1)
                    pe.wait_ge(lo_ready[s], i + FREE)
                    for k in range(DC):
                        q = pe.transpose(turned[s][:, k, :], scaled[:, s, k * P:(k + 1) * P], ident[:])
                    q.then_inc(turned_ready[s], 1)
                if weights is not None:
                    for s in range(2):
                        pe.wait_ge(lo_ready[s], i + 1 + FREE)
                        pe.wait_ge(out_read[s], i + FREE)
                        for n in range(n_parts):
                            q = three_passes(pe, out[s][:, n, 0:width],
                                             lambda k: act_hi[:, s, k, :], lambda k: act_lo[:, s, k, :],
                                             lambda k: w_hi[:, k, n * width:(n + 1) * width],
                                             lambda k: w_lo[:, k, n * width:(n + 1) * width], DC)
                        q.then_inc(out_ready[s], 1)

        if keep is not None:
            @block.gpsimd
            def _(pool):
                for s in range(2):
                    pool.sem_inc(kept[s], FREE)
                with pool.Fori(0, NT // 2) as i:
                    for s in range(2):
                        t = i * 2 + s
                        pool.wait_ge(lo_ready[s], i + 1 + FREE)
                        pool.tensor_copy(keep[0][:, :, bass.ts(t, P)], act_hi[:, s, :, :].bitcast(F32))
                        pool.tensor_copy(keep[1][:, :, bass.ts(t, P)], act_lo[:, s, :, :].bitcast(F32)) \
                            .then_inc(kept[s], 1)


def feature_proj(nc, tl, w_dram, xt_hi, xt_lo, qk):
    with ExitStack() as ctx:
        w_raw = tl.sb(ctx, "fp_w_raw", [P, 2, DC, P])
        w_hi = tl.sb(ctx, "fp_w_hi", [P, 2, DC, P], F32R)
        w_lo = tl.sb(ctx, "fp_w_lo", [P, 2, DC, P], F32R)
        out = [tl.ps(ctx, f"fp_out{s}", [P, 2, HALF]) for s in range(2)]
        w_loaded = tl.pair("fp_w_loaded")
        hi_ready = tl.pair("fp_hi_ready")
        lo_ready = tl.pair("fp_lo_ready")
        out_ready = tl.pair("fp_out_ready")
        act_read = tl.pair("fp_act_read")
        dve_read = tl.pair("fp_dve_read")
        block = ctx.enter_context(nc.Block())

        def chunks(engine, step):
            with engine.Fori(0, QK_CHUNKS // 2) as i:
                for s in range(2):
                    step(s, i, i * 2 + s)
            step(0, QK_CHUNKS // 2, QK_CHUNKS - 1)

        @block.sync
        def _(sp):
            def load(s, i, c):
                sp.wait_ge(lo_ready[s], i + FREE)
                sp.dma_start(w_raw[:, s, :, :], w_dram[c, :, :, :]).then_inc(w_loaded[s], 16)
            chunks(sp, load)

        @block.scalar
        def _(act):
            def step(s, i, c):
                act.wait_ge(w_loaded[s], (i + 1) * 16)
                act.wait_ge(out_ready[s], i + FREE)
                act.copy(w_hi[:, s, :, :], w_raw[:, s, :, :]).then_inc(hi_ready[s], 1)
                act.wait_ge(out_ready[s], i + 1 + FREE)
                act.copy(qk[:, c, 0:HALF], out[s][:, 0, :]).then_inc(act_read[s], 1)
            for s in range(2):
                act.sem_inc(act_read[s], FREE)
            chunks(act, step)

        @block.vector
        def _(dve):
            def step(s, i, c):
                dve.wait_ge(hi_ready[s], i + 1)
                dve.tensor_tensor(w_lo[:, s, :, :], w_raw[:, s, :, :], w_hi[:, s, :, :].bitcast(F32),
                                  ALU.subtract).then_inc(lo_ready[s], 1)
                dve.wait_ge(out_ready[s], i + 1 + FREE)
                dve.tensor_copy(qk[:, c, HALF:T], out[s][:, 1, :]).then_inc(dve_read[s], 1)
            for s in range(2):
                dve.sem_inc(lo_ready[s], FREE)
                dve.sem_inc(dve_read[s], FREE)
            chunks(dve, step)

        @block.tensor
        def _(pe):
            def step(s, i, c):
                pe.wait_ge(lo_ready[s], i + 1 + FREE)
                pe.wait_ge(act_read[s], i + FREE)
                pe.wait_ge(dve_read[s], i + FREE)
                for n in range(2):
                    q = three_passes(pe, out[s][:, n, :], lambda k: w_hi[:, s, k, :], lambda k: w_lo[:, s, k, :],
                                     lambda k: xt_hi[:, k, n * HALF:(n + 1) * HALF],
                                     lambda k: xt_lo[:, k, n * HALF:(n + 1) * HALF], DC)
                q.then_inc(out_ready[s], 1)
            for s in range(2):
                pe.sem_inc(out_ready[s], FREE)
            chunks(pe, step)


def rotate(nc, tl, qk, perm, cos_dram, sin_dram):
    with ExitStack() as ctx:
        cos = tl.sb(ctx, "rot_cos", [P, T])
        sin = tl.sb(ctx, "rot_sin", [P, T])
        partner = tl.sb(ctx, "rot_partner", [P, T])
        swapped = [tl.ps(ctx, f"rot_swapped{s}", [P, 2, HALF]) for s in range(2)]
        loaded = tl.sem("rot_loaded")
        swapped_ready = tl.sem("rot_swapped_ready")
        partner_ready = tl.sem("rot_partner_ready")
        straight_ready = tl.sem("rot_straight_ready")
        rotated = tl.sem("rot_rotated")
        block = ctx.enter_context(nc.Block())
        n_chunks = SWA_K + 1

        @block.sync
        def _(sp):
            sp.dma_start(cos[:], cos_dram[:, :]).then_inc(loaded, 16)
            sp.dma_start(sin[:], sin_dram[:, :]).then_inc(loaded, 16)

        @block.tensor
        def _(pe):
            for c in range(n_chunks):
                if c >= 2:
                    pe.wait_ge(partner_ready, c - 1)
                for n in range(2):
                    q = pe.matmul(swapped[c % 2][:, n, :], perm[:], qk[:, c, n * HALF:(n + 1) * HALF],
                                  start=True, stop=True)
                q.then_inc(swapped_ready, 1)

        @block.gpsimd
        def _(pool):
            pool.wait_ge(loaded, 32)
            for c in range(n_chunks):
                pool.wait_ge(swapped_ready, c + 1)
                pool.tensor_tensor(qk[:, c, :], qk[:, c, :], cos[:], ALU.mult).then_inc(straight_ready, 1)

        @block.vector
        def _(dve):
            dve.wait_ge(loaded, 32)
            for c in range(n_chunks):
                dve.wait_ge(swapped_ready, c + 1)
                dve.wait_ge(rotated, c)
                dve.tensor_tensor(partner[:], swapped[c % 2][:].rearrange("p a b -> p (a b)"), sin[:],
                                  ALU.mult).then_inc(partner_ready, 1)
                dve.wait_ge(partner_ready, c + 1)
                dve.wait_ge(straight_ready, c + 1)
                dve.tensor_tensor(qk[:, c, :], qk[:, c, :], partner[:], ALU.add).then_inc(rotated, 1)


def decay(nc, tl, v, b_forget, tri_dram, key_rows, query_rows):
    with ExitStack() as ctx:
        tri = tl.sb(ctx, "dec_tri", [P, 2 * T - P])
        bias = tl.sb(ctx, "dec_bias", [P, FOX_HEADS])
        steps = [tl.sb(ctx, f"dec_step{n}", [P, NT, FOX_HEADS]) for n in range(7)]
        z, neg_abs, e, soft, low, log_f, z_neg = steps
        c = tl.sb(ctx, "dec_c", [FOX_HEADS, T])
        parts = [tl.sb(ctx, f"dec_part{n}", [FOX_HEADS, T], F32R) for n in range(4)]
        c_hi, c_lo, n_hi, n_lo = parts
        total = tl.ps(ctx, "dec_total", [P, 2, HALF])
        loaded = tl.sem("dec_loaded")
        step = tl.sem("dec_step")
        exp_ready = tl.sem("dec_exp_ready")
        ln_ready = tl.sem("dec_ln_ready")
        logs_ready = tl.sem("dec_logs_ready")
        summed = tl.sem("dec_summed")
        parts_ready = tl.sem("dec_parts_ready")
        ones_ready = tl.sem("dec_ones_ready")
        placed = tl.sem("dec_placed")
        block = ctx.enter_context(nc.Block())

        @block.sync
        def _(sp):
            sp.dma_start(tri[:], tri_dram[:, :]).then_inc(loaded, 16)
            sp.dma_start(bias[:], b_forget.partition_broadcast(P)).then_inc(loaded, 16)
            sp.wait_ge(ones_ready, 2)
            sp.wait_ge(parts_ready, 1)
            for rows, n, part in ((key_rows, 0, n_hi), (key_rows, 1, n_lo), (query_rows, 2, c_hi), (query_rows, 3, c_lo)):
                sp.dma_start(rows[n * FOX_HEADS:(n + 1) * FOX_HEADS, :].bitcast(F32), part[:].bitcast(F32)).then_inc(placed, 16)
            sp.wait_ge(placed, 64)

        @block.gpsimd
        def _(pool):
            pool.memset(key_rows[:].bitcast(F32), 1.0).then_inc(ones_ready, 1)
            pool.memset(query_rows[:].bitcast(F32), 1.0).then_inc(ones_ready, 1)

        @block.vector
        def _(dve):
            n = [0]

            def done(q):
                n[0] += 1
                q.then_inc(step, 1)
                dve.wait_ge(step, n[0])

            dve.wait_ge(loaded, 32)
            done(dve.tensor_tensor(z[:], v[:, :, V_FORGET:V_COLS], spread(bias[:], 1, NT), ALU.add))
            done(dve.tensor_scalar(z_neg[:], z[:], -1.0, None, ALU.mult))
            done(dve.tensor_tensor(neg_abs[:], z[:], z_neg[:], ALU.min))
            done(dve.tensor_scalar(low[:], z[:], 0.0, None, ALU.min))
            dve.wait_ge(ln_ready, 1)
            dve.tensor_tensor(log_f[:], low[:], soft[:], ALU.subtract).then_inc(logs_ready, 1)
            dve.wait_ge(summed, 1)
            done(dve.tensor_scalar(c[:], total[0:FOX_HEADS, :, :].rearrange("p a b -> p (a b)"), 1.0 / SCALE, None,
                                   ALU.mult))
            done(dve.tensor_copy(c_hi[:], c[:]))
            done(dve.tensor_tensor(c_lo[:], c[:], c_hi[:].bitcast(F32), ALU.subtract))
            done(dve.tensor_scalar(n_hi[:], c_hi[:].bitcast(F32), -1.0, None, ALU.mult))
            done(dve.tensor_scalar(n_lo[:], c_lo[:].bitcast(F32), -1.0, None, ALU.mult))
            dve.tensor_copy(c[:, 0:1], c[:, 0:1]).then_inc(parts_ready, 1)

        @block.scalar
        def _(act):
            act.wait_ge(step, 3)
            act.activation(e[:], neg_abs[:], ACT.Exp).then_inc(exp_ready, 1)
            act.wait_ge(exp_ready, 1)
            act.activation(soft[:], e[:], ACT.Ln, bias=1.0).then_inc(ln_ready, 1)

        @block.tensor
        def _(pe):
            pe.wait_ge(logs_ready, 1)
            for n in range(2):
                for t in range(NT):
                    at = T - P - t * P + n * HALF
                    q = pe.matmul(total[0:FOX_HEADS, n, :], log_f[:, t, :], tri[:, at:at + HALF],
                                  start=(t == 0), stop=(t == NT - 1))
            q.then_inc(summed, 1)


def attention(nc, tl, qk, v, key_rows, query_rows, sinks, masks, head_pick, ident, ident16, mixed):
    with ExitStack() as ctx:
        fox_q = tl.sb(ctx, "at_fox_q", [P, 2, P])
        swa_q = tl.sb(ctx, "at_swa_q", [P, 2, P])
        fox_rows = tl.sb(ctx, "at_fox_rows", [4 * FOX_HEADS, 2, P], F32R)
        fox_p = tl.sb(ctx, "at_fox_p", [P, 2, T])
        swa_p = tl.sb(ctx, "at_swa_p", [P, 2, 2 * P])
        turned = tl.sb(ctx, "at_turned_sb", [P, 2, NT, P])
        swa_turned = tl.sb(ctx, "at_swa_turned", [P, 2, 2, P])
        neg_max = tl.sb(ctx, "at_neg_max", [P, 4])
        neg_cap = tl.sb(ctx, "at_neg_cap", [P, 2])
        row_sum = tl.sb(ctx, "at_row_sum", [P, 4])
        sink_e = tl.sb(ctx, "at_sink_e", [P, 2])
        total = tl.sb(ctx, "at_total", [P, 4])
        inv = tl.sb(ctx, "at_inv", [P, 4])
        fox_s = tl.ps(ctx, "at_fox_s", [P, 2, 2, HALF])
        swa_s = tl.ps(ctx, "at_swa_s", [P, 2, 2 * P])
        turn = tl.ps(ctx, "at_turn", [P, NT, P])
        o = tl.ps(ctx, "at_o", [P, 4, HEAD])

        names = ("q_ready rows_ready fox_scored swa_scored fox_max swa_max swa_cap fox_prob swa_prob sink_ready "
                 "zeroed turned_ready taken summed inv_ready fox_o swa_o o_read")
        s = {n: tl.sem("at_" + n) for n in names.split()}
        block = ctx.enter_context(nc.Block())

        @block.vector
        def _(dve):
            dve.sem_inc(s["inv_ready"], FREE)
            dve.sem_inc(s["taken"], FREE)
            dve.sem_inc(s["o_read"], FREE)
            dve.memset(fox_q[:], 0.0).then_inc(s["zeroed"], 1)
            dve.memset(swa_q[:], 0.0).then_inc(s["zeroed"], 1)
            dve.wait_ge(s["zeroed"], 2)
            for j in range(NT):
                n_keys = (j + 1) * P
                lo = 0 if j else P
                with dve.Fori(0, PAIRS) as c:
                    step = c + j * PAIRS
                    dve.wait_ge(s["fox_scored"], step + FREE)
                    dve.wait_ge(s["swa_scored"], step + FREE)
                    for q, chunk in ((fox_q, FOX_Q), (swa_q, SWA_Q)):
                        for u in range(2):
                            at = slice(u * HEAD, (u + 1) * HEAD)
                            dve.tensor_copy(q[at, u, :], qk[at, chunk + c, j * P:(j + 1) * P]) \
                                .then_inc(s["q_ready"], 1)
                    for u in range(2):
                        dve.tensor_scalar(fox_rows[:, u, :], query_rows[:, j * P:(j + 1) * P].bitcast(F32),
                                          head_pick[:, bass.ds(2 * c + u, 1)], None,
                                          ALU.mult).then_inc(s["rows_ready"], 1)
                    dve.wait_ge(s["fox_scored"], step + 1 + FREE)
                    dve.tensor_reduce(neg_max[:, 0:2],
                                      fox_s[:].rearrange("p h a b -> p h (a b)")[:, :, 0:n_keys], AX.X, ALU.max,
                                      negate=True).then_inc(s["fox_max"], 1)
                    dve.wait_ge(s["swa_scored"], step + 1 + FREE)
                    dve.tensor_reduce(neg_cap[:], swa_s[:, :, lo:2 * P], AX.X, ALU.max,
                                      negate=True).then_inc(s["swa_cap"], 1)
                    dve.wait_ge(s["swa_cap"], step + 1)
                    dve.tensor_tensor(neg_max[:, 2:4], neg_cap[:], sinks["neg_unscaled"][:, c, :],
                                      ALU.min).then_inc(s["swa_max"], 1)
                    for h in range(2):
                        dve.wait_ge(s["turned_ready"], step * 3 + h + 1 + FREE)
                        dve.tensor_copy(turned[:, h, 0:j + 1, :], turn[:, 0:j + 1, :]).then_inc(s["taken"], 1)
                    dve.wait_ge(s["turned_ready"], step * 3 + 3 + FREE)
                    dve.tensor_copy(swa_turned[:, :, lo // P:2, :],
                                    turn[:].rearrange("p (h b) q -> p h b q", b=4)[:, :, lo // P:2, :]) \
                        .then_inc(s["taken"], 1)
                    dve.wait_ge(s["sink_ready"], step + 1)
                    dve.tensor_copy(total[:, 0:2], row_sum[:, 0:2]).then_inc(s["summed"], 1)
                    dve.tensor_tensor(total[:, 2:4], row_sum[:, 2:4], sink_e[:], ALU.add).then_inc(s["summed"], 1)
                    dve.wait_ge(s["summed"], step * 2 + 2)
                    dve.reciprocal(inv[:], total[:]).then_inc(s["inv_ready"], 1)
                    dve.wait_ge(s["inv_ready"], step + 1 + FREE)
                    dve.wait_ge(s["swa_o"], step + 1)
                    fox_at = FOX_HEADS * HEAD
                    dve.tensor_tensor(mixed[:, j, bass.ds(c * 2 * HEAD + fox_at, 2 * HEAD)].rearrange(
                        "p (h d) -> p h d", d=HEAD), o[:, 0:2, :], spread(inv[:, 0:2], 2, HEAD), ALU.mult)
                    swa = mixed[:, j, 0:fox_at].rearrange("p (u c d) -> p u c d", u=2, d=HEAD)
                    dve.tensor_tensor(swa[:, :, c, :], o[:, 2:4, :], spread(inv[:, 2:4], 2, HEAD),
                                      ALU.mult).then_inc(s["o_read"], 1)

        @block.scalar
        def _(act):
            act.sem_inc(s["fox_prob"], FREE)
            act.sem_inc(s["swa_prob"], FREE)
            for j in range(NT):
                n_keys = (j + 1) * P
                lo = 0 if j else P
                with act.Fori(0, PAIRS) as c:
                    step = c + j * PAIRS
                    act.wait_ge(s["fox_max"], step + 1)
                    for h in range(2):
                        act.mul(sinks["bias"][:, h:h + 1], neg_max[:, h:h + 1], SCALE).then_inc(sinks["bias_ready"], 1)
                    act.wait_ge(sinks["bias_ready"], step * 4 + 2)
                    act.wait_ge(s["turned_ready"], step * 3 + FREE)
                    act.wait_ge(s["inv_ready"], step + FREE)
                    for h in range(2):
                        act.activation(fox_p[:, h, 0:n_keys], fox_s[:, h, :, :].rearrange("p a b -> p (a b)")[:, 0:n_keys],
                                       ACT.Exp, bias=sinks["bias"][:, h:h + 1], scale=SCALE,
                                       accum_out=row_sum[:, h:h + 1]).then_inc(s["fox_prob"], 1)
                    act.wait_ge(s["swa_max"], step + 1)
                    for h in range(2, 4):
                        act.mul(sinks["bias"][:, h:h + 1], neg_max[:, h:h + 1], SCALE).then_inc(sinks["bias_ready"], 1)
                    act.wait_ge(sinks["bias_ready"], step * 4 + 4)
                    for h in range(2):
                        act.activation(swa_p[:, h, lo:2 * P], swa_s[:, h, lo:2 * P], ACT.Exp,
                                       bias=sinks["bias"][:, 2 + h:3 + h], scale=SCALE,
                                       accum_out=row_sum[:, 2 + h:3 + h]).then_inc(s["swa_prob"], 1)
                    for h in range(2):
                        q = act.activation(sink_e[:, h:h + 1], sinks["value"][:, c, h:h + 1], ACT.Exp,
                                           bias=sinks["bias"][:, 2 + h:3 + h])
                    q.then_inc(s["sink_ready"], 1)

        @block.tensor
        def _(pe):
            pe.sem_inc(s["fox_scored"], FREE)
            pe.sem_inc(s["swa_scored"], FREE)
            pe.sem_inc(s["turned_ready"], FREE)
            for j in range(NT):
                n_keys = (j + 1) * P
                lo = 0 if j else P
                with pe.Fori(0, PAIRS) as c:
                    step = c + j * PAIRS
                    pe.wait_ge(s["q_ready"], (step + 1) * 4)
                    pe.wait_ge(s["rows_ready"], (step + 1) * 2)
                    pe.wait_ge(s["fox_prob"], step * 2 + FREE)
                    for h in range(2):
                        for n in range((n_keys + HALF - 1) // HALF):
                            end = min(HALF, n_keys - n * HALF)
                            own = n * HALF + end == n_keys
                            out = fox_s[:, h, n, 0:end]
                            pe.matmul(out, fox_q[:, h, :], qk[:, FOX_K + c, n * HALF:n * HALF + end],
                                      start=True, stop=False)
                            if own:
                                pe.matmul(fox_s[:, h, n, end - P:end], ident16[:], masks[:, P:2 * P],
                                          start=False, stop=False, skip_group_check=True)
                            q = pe.matmul(out, fox_rows[:, h, :], key_rows[:, n * HALF:n * HALF + end],
                                          start=False, stop=True)
                    q.then_inc(s["fox_scored"], 1)
                    pe.wait_ge(s["swa_prob"], step * 2 + FREE)
                    for h in range(2):
                        keys = qk[:, SWA_K, (j - 1) * P + lo:(j + 1) * P]
                        pe.matmul(swa_s[:, h, lo:2 * P], swa_q[:, h, :], keys, start=True, stop=False)
                        q = pe.matmul(swa_s[:, h, lo:2 * P], ident16[:], masks[:, lo:2 * P], start=False, stop=True)
                    q.then_inc(s["swa_scored"], 1)
                    for h in range(2):
                        pe.wait_ge(s["fox_prob"], step * 2 + h + 1 + FREE)
                        pe.wait_ge(s["taken"], step * 3 + h + FREE)
                        for b in range(j + 1):
                            q = pe.transpose(turn[:, b, :], fox_p[:, h, b * P:(b + 1) * P], ident[:])
                        q.then_inc(s["turned_ready"], 1)
                    pe.wait_ge(s["swa_prob"], step * 2 + 2 + FREE)
                    pe.wait_ge(s["taken"], step * 3 + 2 + FREE)
                    for h in range(2):
                        for b in range(lo // P, 2):
                            q = pe.transpose(turn[:, 4 * h + b, :], swa_p[:, h, b * P:(b + 1) * P], ident[:])
                    q.then_inc(s["turned_ready"], 1)
                    pe.wait_ge(s["o_read"], step + FREE)
                    pe.wait_ge(s["taken"], step * 3 + 2 + FREE)
                    for h in range(2):
                        for b in range(j + 1):
                            pe.matmul(o[:, h, :], turned[:, h, b, :],
                                      v[:, b, bass.ds(c * 2 * HEAD + (V_FOX + h * HEAD), HEAD)],
                                      start=(b == 0), stop=(b == j))
                    pe.wait_ge(s["taken"], step * 3 + 3 + FREE)
                    for h in range(2):
                        for b in range(lo // P, 2):
                            q = pe.matmul(o[:, 2 + h, :], swa_turned[:, h, b, :],
                                          v[:, j - 1 + b, h * HEAD:(h + 1) * HEAD],
                                          start=(b == lo // P), stop=(b == 1))
                    q.then_inc(s["swa_o"], 1)


def wait_apart(engine, sem, value, passed):
    engine.wait_ge(sem, value)
    engine.sem_inc(passed, 1)


def peer_scores(nc, tl, w_dram, keys_dram, xn_hi, xn_lo, top_v, top_i):
    with ExitStack() as ctx:
        w_raw = tl.sb(ctx, "ps_w_raw", [P, 2, DC, P])
        w_hi = tl.sb(ctx, "ps_w_hi", [P, 2, DC, P], F32R)
        w_lo = tl.sb(ctx, "ps_w_lo", [P, 2, DC, P], F32R)
        keys = tl.sb(ctx, "ps_keys", [P, 2, KEYS])
        query = tl.sb(ctx, "ps_query", [P, 2, T])
        best = tl.sb(ctx, "ps_best", [P, 2, NT, TOPK])
        where = tl.sb(ctx, "ps_where", [P, 2, NT, TOPK], U32)
        rest = tl.sb(ctx, "ps_rest", [P, NT, KEYS])
        q_out = [tl.ps(ctx, f"ps_q_out{s}", [P, 2, HALF]) for s in range(2)]
        score = [tl.ps(ctx, f"ps_score{s}", [P, NT, KEYS]) for s in range(2)]
        keys_loaded = tl.sem("ps_keys_loaded")
        w_loaded = tl.pair("ps_w_loaded")
        hi_ready = tl.pair("ps_hi_ready")
        lo_ready = tl.pair("ps_lo_ready")
        q_out_ready = tl.pair("ps_q_out_ready")
        query_ready = tl.pair("ps_query_ready")
        score_ready = tl.pair("ps_score_ready")
        score_read = tl.pair("ps_score_read")
        sweep = tl.sem("ps_sweep")
        passed = tl.sem("ps_passed")
        stored = tl.pair("ps_stored")
        block = ctx.enter_context(nc.Block())

        @block.sync
        def _(sp):
            sp.dma_start(keys[:], keys_dram.rearrange("c p k -> p c k")).then_inc(keys_loaded, 16)
            with sp.Fori(0, PEER_HEADS) as i:
                for s in range(2):
                    sp.wait_ge(lo_ready[s], i + FREE)
                    sp.dma_start(w_raw[:, s, :, :], w_dram[i * 2 + s, :, :, :]).then_inc(w_loaded[s], 16)

        @block.scalar
        def _(act):
            for s in range(2):
                act.sem_inc(query_ready[s], FREE)
            with act.Fori(0, PEER_HEADS) as i:
                for s in range(2):
                    act.wait_ge(w_loaded[s], (i + 1) * 16)
                    act.wait_ge(q_out_ready[s], i + FREE)
                    act.copy(w_hi[:, s, :, :], w_raw[:, s, :, :]).then_inc(hi_ready[s], 1)
                for s in range(2):
                    act.wait_ge(q_out_ready[s], i + 1 + FREE)
                    act.wait_ge(score_ready[s], i + FREE)
                    act.copy(query[:, s, :], q_out[s][:].rearrange("p a b -> p (a b)")) \
                        .then_inc(query_ready[s], 1)

        @block.tensor
        def _(pe):
            for s in range(2):
                pe.sem_inc(q_out_ready[s], FREE)
                pe.sem_inc(score_ready[s], FREE)
            pe.wait_ge(keys_loaded, 16)
            with pe.Fori(0, PEER_HEADS) as i:
                for s in range(2):
                    pe.wait_ge(lo_ready[s], i + 1 + FREE)
                    pe.wait_ge(query_ready[s], i + FREE)
                    for n in range(2):
                        q = three_passes(pe, q_out[s][:, n, :], lambda k: w_hi[:, s, k, :],
                                         lambda k: w_lo[:, s, k, :],
                                         lambda k: xn_hi[:, k, n * HALF:(n + 1) * HALF],
                                         lambda k: xn_lo[:, k, n * HALF:(n + 1) * HALF], DC)
                    q.then_inc(q_out_ready[s], 1)
                for s in range(2):
                    pe.wait_ge(query_ready[s], i + 1 + FREE)
                    pe.wait_ge(score_read[s], i + FREE)
                    for t in range(NT):
                        q = pe.matmul(score[s][:, t, :], query[:, s, t * P:(t + 1) * P], keys[:, s, :],
                                      start=True, stop=True)
                    q.then_inc(score_ready[s], 1)

        @block.vector
        def _(dve):
            for s in range(2):
                dve.sem_inc(score_read[s], FREE)
            with dve.Fori(0, PEER_HEADS) as i:
                for s in range(2):
                    done = (i * 2 + s) * 5
                    dve.wait_ge(score_ready[s], i + 1 + FREE)
                    wait_apart(dve, stored[s], i + FREE, passed)
                    for t in range(NT):
                        q = dve.max(best[:, s, t, 0:8], score[s][:, t, :])
                    q.then_inc(sweep, 1)
                    wait_apart(dve, sweep, done + 1, passed)
                    for t in range(NT):
                        q = dve.max_index(where[:, s, t, 0:8], best[:, s, t, 0:8], score[s][:, t, :])
                    q.then_inc(sweep, 1)
                    wait_apart(dve, sweep, done + 2, passed)
                    for t in range(NT):
                        q = dve.match_replace(rest[:, t, :], best[:, s, t, 0:8], score[s][:, t, :], LOWEST)
                    q.then_inc(sweep, 1)
                    wait_apart(dve, sweep, done + 3, passed)
                    for t in range(NT):
                        q = dve.max(best[:, s, t, 8:16], rest[:, t, :])
                        if t == 0:
                            q.then_inc(score_read[s], 1)
                    q.then_inc(sweep, 1)
                    wait_apart(dve, sweep, done + 4, passed)
                    for t in range(NT):
                        q = dve.max_index(where[:, s, t, 8:16], best[:, s, t, 8:16], rest[:, t, :])
                    q.then_inc(sweep, 1)

        @block.gpsimd
        def _(pool):
            for s in range(2):
                pool.sem_inc(lo_ready[s], FREE)
                pool.sem_inc(stored[s], FREE)
            with pool.Fori(0, PEER_HEADS) as i:
                for s in range(2):
                    pool.wait_ge(hi_ready[s], i + 1)
                    pool.tensor_tensor(w_lo[:, s, :, :], w_raw[:, s, :, :], w_hi[:, s, :, :].bitcast(F32),
                                       ALU.subtract).then_inc(lo_ready[s], 1)
                for s in range(2):
                    pool.wait_ge(sweep, (i * 2 + s + 1) * 5)
                    pool.tensor_copy(top_v[:, :, i * 2 + s, :], best[:, s, :, :])
                    pool.tensor_copy(top_i[:, :, i * 2 + s, :], where[:, s, :, :]).then_inc(stored[s], 1)


def peer_best(nc, tl, top_v, top_i, ident, gate_hi, gate_lo, first, second):
    with ExitStack() as ctx:
        HEADS = NT * PEER_HEADS
        LOT = 4
        v = top_v[:].rearrange("p t (h c) k -> p (t h) c k", c=2)
        ti = top_i[:].rearrange("p t (h c) k -> p (t h) c k", c=2)
        sums = tl.sb(ctx, "pb_sums", [P, LOT, TOPK, TOPK])
        rest = tl.sb(ctx, "pb_rest", [P, LOT, TOPK * TOPK])
        lot_v = tl.sb(ctx, "pb_lot_v", [P, LOT, TOPK])
        lot_p = tl.sb(ctx, "pb_lot_p", [P, LOT, TOPK], U32)
        best = tl.sb(ctx, "pb_best", [P, HEADS, TOPK])
        place = tl.sb(ctx, "pb_place", [P, HEADS, TOPK], U32)
        digit_u = tl.sb(ctx, "pb_digit_u", [P, 2, HEADS, TOPK], U32)
        digit = tl.sb(ctx, "pb_digit", [P, 2, HEADS, TOPK])
        gap = tl.sb(ctx, "pb_gap", [P, HEADS, TOPK])
        e = tl.sb(ctx, "pb_e", [P, HEADS, TOPK])
        total = tl.sb(ctx, "pb_total", [P, HEADS])
        inv = tl.sb(ctx, "pb_inv", [P, HEADS])
        gate = tl.sb(ctx, "pb_gate", [P, HEADS, TOPK])
        key = tl.sb(ctx, "pb_key", [P, 2, HEADS, TOPK])
        term = tl.sb(ctx, "pb_term", [P, 2, HEADS, TOPK])
        turned = [tl.ps(ctx, f"pb_turned{n}", [P, NT, P]) for n in range(3)]
        step = tl.sem("pb_step")
        lots = tl.sem("pb_lots")
        passed = tl.sem("pb_passed")
        gap_ready = tl.sem("pb_gap_ready")
        e_ready = tl.sem("pb_e_ready")
        gate_ready = tl.sem("pb_gate_ready")
        key_ready = tl.sem("pb_key_ready")
        turned_ready = tl.sem("pb_turned_ready")
        hi_ready = tl.sem("pb_hi_ready")
        block = ctx.enter_context(nc.Block())

        @block.vector
        def _(dve):
            per = 7
            with dve.Fori(0, HEADS // LOT) as i:
                done = i * per
                for u in range(LOT):
                    row = i * LOT + u
                    q = dve.tensor_tensor(sums[:, u, :, :], spread(v[:, row, 0, :], 2, TOPK),
                                          spread(v[:, row, 1, :], 1, TOPK), ALU.add)
                q.then_inc(lots, 1)
                wait_apart(dve, lots, done + 1, passed)
                flat = sums[:].rearrange("p u a b -> p u (a b)")
                for u in range(LOT):
                    q = dve.max(lot_v[:, u, 0:8], flat[:, u, :])
                q.then_inc(lots, 1)
                wait_apart(dve, lots, done + 2, passed)
                for u in range(LOT):
                    q = dve.max_index(lot_p[:, u, 0:8], lot_v[:, u, 0:8], flat[:, u, :])
                q.then_inc(lots, 1)
                wait_apart(dve, lots, done + 3, passed)
                for u in range(LOT):
                    q = dve.match_replace(rest[:, u, :], lot_v[:, u, 0:8], flat[:, u, :], LOWEST)
                q.then_inc(lots, 1)
                wait_apart(dve, lots, done + 4, passed)
                for u in range(LOT):
                    q = dve.max(lot_v[:, u, 8:16], rest[:, u, :])
                q.then_inc(lots, 1)
                wait_apart(dve, lots, done + 5, passed)
                for u in range(LOT):
                    q = dve.max_index(lot_p[:, u, 8:16], lot_v[:, u, 8:16], rest[:, u, :])
                q.then_inc(lots, 1)
                dve.wait_ge(lots, done + 6)
                dve.tensor_copy(best[:, bass.ds(i * LOT, LOT), :], lot_v[:])
                dve.tensor_copy(place[:, bass.ds(i * LOT, LOT), :], lot_p[:]).then_inc(lots, 1)
            dve.wait_ge(lots, HEADS // LOT * per)
            n = [0]

            def done(q):
                n[0] += 1
                q.then_inc(step, 1)
                dve.wait_ge(step, n[0])

            dve.tensor_tensor(gap[:], best[:], best[:, :, 0:1].broadcast_to([P, HEADS, TOPK]),
                              ALU.subtract).then_inc(gap_ready, 1)
            done(dve.tensor_scalar(digit_u[:, 0, :, :], place[:], 4, None, ALU.logical_shift_right))
            done(dve.tensor_scalar(digit_u[:, 1, :, :], place[:], TOPK - 1, None, ALU.bitwise_and))
            done(dve.tensor_copy(digit[:], digit_u[:]))
            for a in range(TOPK):
                for c in range(2):
                    q = dve.scalar_tensor_tensor(out=(term if a else key)[:, c, :, :], in0=digit[:, c, :, :], scalar=float(a),
                                                 in1=spread(ti[:, :, c, a], 2, TOPK), op0=ALU.is_equal, op1=ALU.mult)
                done(q)
                if a:
                    done(dve.tensor_tensor(key[:], key[:], term[:], ALU.add))
            dve.tensor_copy(digit[:, 0, 0, 0:1], key[:, 0, 0, 0:1]).then_inc(key_ready, 1)
            dve.wait_ge(e_ready, 1)
            done(dve.tensor_reduce(total[:], e[:], AX.X, ALU.add))
            done(dve.reciprocal(inv[:], total[:]))
            dve.tensor_tensor(gate[:], e[:], spread(inv[:], 2, TOPK), ALU.mult).then_inc(gate_ready, 1)
            dve.wait_ge(turned_ready, 3)
            flat = [x[:].rearrange("p t q -> p (t q)") for x in turned]
            dve.tensor_copy(gate_hi[:], flat[2]).then_inc(hi_ready, 1)
            dve.wait_ge(hi_ready, 1)
            dve.tensor_tensor(gate_lo[:], flat[2], gate_hi[:], ALU.subtract)

        @block.scalar
        def _(act):
            act.wait_ge(gap_ready, 1)
            act.activation(e[:], gap[:], ACT.Exp).then_inc(e_ready, 1)
            act.wait_ge(turned_ready, 3)
            for to, of in ((first, 0), (second, 1)):
                act.copy(to[:], turned[of][:].rearrange("p t q -> p (t q)"))

        @block.tensor
        def _(pe):
            for n, ready in ((0, key_ready), (1, key_ready), (2, gate_ready)):
                pe.wait_ge(ready, 1)
                for t in range(NT):
                    rows = (gate[:] if n == 2 else key[:, n, :, :])[:, t * PEER_HEADS:(t + 1) * PEER_HEADS, :]
                    q = pe.transpose(turned[n][:, t, :], rows.rearrange("p h k -> p (h k)"), ident[:])
                q.then_inc(turned_ready, 1)


def gate_matrix(nc, tl, iota_dram, gate_hi, gate_lo, first, second, gates_dram):
    with ExitStack() as ctx:
        LOT = 8
        LOTS = P // LOT
        iota = tl.sb(ctx, "gm_iota", [P, KEYS])
        hot_first = tl.sb(ctx, "gm_hot_first", [P, 2, LOT, KEYS], F32R)
        hot_hi = tl.sb(ctx, "gm_hot_hi", [P, 2, LOT, KEYS], F32R)
        hot_lo = tl.sb(ctx, "gm_hot_lo", [P, 2, LOT, KEYS], F32R)
        tile = tl.sb(ctx, "gm_tile", [P, KEYS, P])
        out = [tl.ps(ctx, f"gm_out{s}", [P, LOT, KEYS]) for s in range(2)]
        iota_loaded = tl.sem("gm_iota_loaded")
        hot_ready = tl.pair("gm_hot_ready")
        out_ready = tl.pair("gm_out_ready")
        out_read = tl.pair("gm_out_read")
        stored = tl.sem("gm_stored")
        tile_free = tl.sem("gm_tile_free")
        block = ctx.enter_context(nc.Block())

        @block.sync
        def _(sp):
            sp.dma_start(iota[:], iota_dram[:, :]).then_inc(iota_loaded, 16)
            sp.sem_inc(tile_free, FREE)
            with sp.Fori(0, NT) as t:
                for s in range(2):
                    sp.wait_ge(out_read[s], (t + 1) * (LOTS // 2) + FREE)
                sp.dma_start(gates_dram[:, :, bass.ts(t, P)].rearrange("b a t -> a b t"), tile[:]) \
                    .then_inc(stored, 16)
                sp.wait_ge(stored, (t + 1) * 16)
                sp.sem_inc(tile_free, 1)

        @block.vector
        def _(dve):
            dve.wait_ge(iota_loaded, 16)
            with dve.Fori(0, NT * LOTS // 2) as i:
                for s in range(2):
                    at = i * 2 * LOT + s * LOT
                    dve.wait_ge(out_ready[s], i + FREE)
                    dve.tensor_tensor(hot_first[:, s, :, :], spread(iota[:], 1, LOT),
                                      spread(first[:, bass.ds(at, LOT)], 2, KEYS), ALU.is_equal)
                    for u in range(LOT):
                        one = bass.ds(at + u, 1)
                        dve.tensor_scalar(hot_hi[:, s, u, :], iota[:], second[:, one], gate_hi[:, one],
                                          ALU.is_equal, ALU.mult)
                        q = dve.tensor_scalar(hot_lo[:, s, u, :], iota[:], second[:, one], gate_lo[:, one],
                                              ALU.is_equal, ALU.mult)
                    q.then_inc(hot_ready[s], 1)

        @block.tensor
        def _(pe):
            for s in range(2):
                pe.sem_inc(out_ready[s], FREE)
            with pe.Fori(0, NT * LOTS // 2) as i:
                for s in range(2):
                    pe.wait_ge(hot_ready[s], i + 1)
                    pe.wait_ge(out_read[s], i + FREE)
                    for u in range(LOT):
                        pe.matmul(out[s][:, u, :], hot_first[:, s, u, :], hot_hi[:, s, u, :], start=True, stop=False)
                        q = pe.matmul(out[s][:, u, :], hot_first[:, s, u, :], hot_lo[:, s, u, :], start=False,
                                      stop=True)
                    q.then_inc(out_ready[s], 1)

        @block.scalar
        def _(act):
            for s in range(2):
                act.sem_inc(out_read[s], FREE)
            with act.Fori(0, NT) as t:
                act.wait_ge(tile_free, t + FREE)
                with act.Fori(0, LOTS // 2) as g:
                    for s in range(2):
                        act.wait_ge(out_ready[s], t * (LOTS // 2) + g + 1 + FREE)
                        act.copy(tile[:, :, bass.ds(g * 2 * LOT + s * LOT, LOT)],
                                 out[s][:].rearrange("p u b -> p b u")).then_inc(out_read[s], 1)


def expert_up(nc, tl, u_dram, xn_hi, xn_lo, act_dram):
    with ExitStack() as ctx:
        u_raw = tl.sb(ctx, "eu_u_raw", [P, 2, DC, KEYS])
        u_hi = tl.sb(ctx, "eu_u_hi", [P, 2, DC, KEYS], F32R)
        u_lo = tl.sb(ctx, "eu_u_lo", [P, 2, DC, KEYS], F32R)
        gelu = tl.sb(ctx, "eu_gelu", [P, 2, T])
        out = [tl.ps(ctx, f"eu_out{s}", [P, 2, HALF]) for s in range(2)]
        loaded = tl.pair("eu_loaded")
        hi_ready = tl.pair("eu_hi_ready")
        lo_ready = tl.pair("eu_lo_ready")
        out_ready = tl.pair("eu_out_ready")
        gelu_ready = tl.pair("eu_gelu_ready")
        stored = tl.pair("eu_stored")
        gelu_free = tl.pair("eu_gelu_free")
        block = ctx.enter_context(nc.Block())

        @block.sync
        def _(sp):
            with sp.Fori(0, KEYS // 2) as i:
                for s in range(2):
                    sp.wait_ge(lo_ready[s], i + FREE)
                    sp.dma_start(u_raw[:, s, :, :], u_dram[i * 2 + s, :, :, :]).then_inc(loaded[s], 16)

        @block.gpsimd
        def _(pool):
            for s in range(2):
                pool.sem_inc(gelu_free[s], FREE)
            with pool.Fori(0, KEYS // 2) as i:
                for s in range(2):
                    pool.wait_ge(gelu_ready[s], i + 1 + FREE)
                    pool.dma_start(act_dram[i * 2 + s, :, :], gelu[:, s, :]).then_inc(stored[s], 16)
                for s in range(2):
                    pool.wait_ge(stored[s], (i + 1) * 16)
                    pool.sem_inc(gelu_free[s], 1)

        @block.scalar
        def _(act):
            for s in range(2):
                act.sem_inc(gelu_ready[s], FREE)
            with act.Fori(0, KEYS // 2) as i:
                for s in range(2):
                    act.wait_ge(loaded[s], (i + 1) * 16)
                    act.wait_ge(out_ready[s], i + FREE)
                    act.copy(u_hi[:, s, :, :], u_raw[:, s, :, :]).then_inc(hi_ready[s], 1)
                for s in range(2):
                    act.wait_ge(out_ready[s], i + 1 + FREE)
                    act.wait_ge(gelu_free[s], i + FREE)
                    act.activation(gelu[:, s, :], out[s][:].rearrange("p a b -> p (a b)"), ACT.Gelu) \
                        .then_inc(gelu_ready[s], 1)

        @block.vector
        def _(dve):
            for s in range(2):
                dve.sem_inc(lo_ready[s], FREE)
            with dve.Fori(0, KEYS // 2) as i:
                for s in range(2):
                    dve.wait_ge(hi_ready[s], i + 1)
                    dve.tensor_tensor(u_lo[:, s, :, :], u_raw[:, s, :, :], u_hi[:, s, :, :].bitcast(F32),
                                      ALU.subtract).then_inc(lo_ready[s], 1)

        @block.tensor
        def _(pe):
            for s in range(2):
                pe.sem_inc(out_ready[s], FREE)
            with pe.Fori(0, KEYS // 2) as i:
                for s in range(2):
                    pe.wait_ge(lo_ready[s], i + 1 + FREE)
                    pe.wait_ge(gelu_ready[s], i + FREE)
                    for n in range(2):
                        q = three_passes(pe, out[s][:, n, :], lambda k: u_hi[:, s, k, :], lambda k: u_lo[:, s, k, :],
                                         lambda k: xn_hi[:, k, n * HALF:(n + 1) * HALF],
                                         lambda k: xn_lo[:, k, n * HALF:(n + 1) * HALF], DC)
                    q.then_inc(out_ready[s], 1)


def expert_down(nc, tl, v_dram, act_dram, gates_dram, h):
    with ExitStack() as ctx:
        SLOTS = 4
        TILES = HALF // P
        v_raw = tl.sb(ctx, "ed_v_raw", [P, SLOTS, D])
        act_in = tl.sb(ctx, "ed_act_in", [P, SLOTS, HALF])
        gate_in = tl.sb(ctx, "ed_gate_in", [P, SLOTS, HALF])
        v_hi = tl.sb(ctx, "ed_v_hi", [P, SLOTS, D], F32R)
        v_lo = tl.sb(ctx, "ed_v_lo", [P, SLOTS, D], F32R)
        coef = tl.sb(ctx, "ed_coef", [P, SLOTS, HALF])
        c_hi = tl.sb(ctx, "ed_c_hi", [P, SLOTS, HALF], F32R)
        c_lo = tl.sb(ctx, "ed_c_lo", [P, SLOTS, HALF], F32R)
        zero = tl.sb(ctx, "ed_zero", [P, HALF], BF16)
        y = tl.ps(ctx, "ed_y", [P, TILES, 2, HALF])
        slots = range(SLOTS)
        v_loaded = [tl.sem(f"ed_v_loaded{s}") for s in slots]
        a_loaded = [tl.sem(f"ed_a_loaded{s}") for s in slots]
        coef_ready = [tl.sem(f"ed_coef_ready{s}") for s in slots]
        hi_ready = [tl.sem(f"ed_hi_ready{s}") for s in slots]
        split = [tl.sem(f"ed_split{s}") for s in slots]
        used = [tl.sem(f"ed_used{s}") for s in slots]
        zeroed = tl.sem("ed_zeroed")
        summed = tl.sem("ed_summed")
        added = tl.sem("ed_added")
        block = ctx.enter_context(nc.Block())
        ROUNDS = KEYS // SLOTS
        v_chunks = v_dram.rearrange("(a b) d -> b a d", b=KEYS)

        @block.sync
        def _(sp):
            for half in range(2):
                tokens = slice(half * HALF, (half + 1) * HALF)
                with sp.Fori(0, ROUNDS) as i:
                    for s in slots:
                        b = i * SLOTS + s
                        sp.wait_ge(split[s], i + half * ROUNDS + FREE)
                        sp.dma_start(v_raw[:, s, :], v_chunks[b, :, :]).then_inc(v_loaded[s], 16)
                        sp.dma_start(act_in[:, s, :], act_dram[b, :, tokens]).then_inc(a_loaded[s], 16)
                        sp.dma_start(gate_in[:, s, :], gates_dram[b, :, tokens]).then_inc(a_loaded[s], 16)

        @block.vector
        def _(dve):
            for s in slots:
                dve.sem_inc(split[s], FREE)
            dve.sem_inc(added, FREE)
            dve.memset(zero[:], 0.0).then_inc(zeroed, 1)
            for half in range(2):
                with dve.Fori(0, ROUNDS) as i:
                    r = i + half * ROUNDS
                    for s in slots:
                        dve.wait_ge(a_loaded[s], (r + 1) * 32)
                        dve.tensor_tensor(coef[:, s, :], act_in[:, s, :], gate_in[:, s, :], ALU.mult) \
                            .then_inc(coef_ready[s], 1)
                        dve.wait_ge(hi_ready[s], (r + 1) * 2)
                        dve.tensor_tensor(v_lo[:, s, :], v_raw[:, s, :], v_hi[:, s, :].bitcast(F32), ALU.subtract)
                        dve.tensor_tensor(c_lo[:, s, :], coef[:, s, :], c_hi[:, s, :].bitcast(F32),
                                          ALU.subtract).then_inc(split[s], 1)
                dve.wait_ge(summed, half + 1)
                for t in range(TILES):
                    rows = h[:, half * TILES + t, :]
                    q = dve.tensor_tensor(rows, rows, y[:, t, :, :].rearrange("p a b -> p (a b)"), ALU.add)
                q.then_inc(added, 1)

        @block.scalar
        def _(act):
            for half in range(2):
                with act.Fori(0, ROUNDS) as i:
                    r = i + half * ROUNDS
                    for s in slots:
                        act.wait_ge(used[s], r + FREE)
                        act.wait_ge(v_loaded[s], (r + 1) * 16)
                        act.copy(v_hi[:, s, :], v_raw[:, s, :]).then_inc(hi_ready[s], 1)
                        act.wait_ge(coef_ready[s], r + 1)
                        act.copy(c_hi[:, s, :], coef[:, s, :]).then_inc(hi_ready[s], 1)

        @block.tensor
        def _(pe):
            for s in slots:
                pe.sem_inc(used[s], FREE)
            pe.wait_ge(zeroed, 1)

            def zeros(start):
                for t in range(TILES):
                    for n in range(2):
                        q = pe.matmul(y[:, t, n, :], zero[:, 0:P], zero[:], start=start, stop=not start)
                return q

            for half in range(2):
                pe.wait_ge(added, half + FREE)
                zeros(True)
                with pe.Fori(0, ROUNDS) as i:
                    r = i + half * ROUNDS
                    for s in slots:
                        pe.wait_ge(split[s], r + 1 + FREE)
                        for t in range(TILES):
                            rows = slice(t * P, (t + 1) * P)
                            for lhs, rhs in ((c_hi, v_hi), (c_hi, v_lo), (c_lo, v_hi)):
                                for n in range(2):
                                    q = pe.matmul(y[:, t, n, :], lhs[:, s, rows],
                                                  rhs[:, s, n * HALF:(n + 1) * HALF], start=False, stop=False)
                        q.then_inc(used[s], 1)
                zeros(False).then_inc(summed, 1)


def layer_input(nc, tl, w_dram, pt_dram, pt, pw):
    loaded = tl.sem("li_loaded")
    with nc.Block() as block:
        @block.sync
        def _(sp):
            sp.dma_start(pt[:], pt_dram.rearrange("(k p) t -> p k t", p=P)).then_inc(loaded, 16)
            sp.dma_start(pw[:], w_dram.rearrange("(k p) d -> p k d", p=P)).then_inc(loaded, 16)
            sp.wait_ge(loaded, 32)


def ple_projection(nc, tl, pt, pw, proj):
    KP = 2
    with ExitStack() as ctx:
        out = [tl.ps(ctx, f"pp_out{s}", [P, 2, HALF]) for s in range(2)]
        ready = tl.sem("pp_ready")
        read = tl.sem("pp_read")
        block = ctx.enter_context(nc.Block())

        @block.tensor
        def _(pe):
            for t in range(NT):
                if t >= 2:
                    pe.wait_ge(read, t - 1)
                for n in range(2):
                    for k in range(KP):
                        q = pe.matmul(out[t % 2][:, n, :], pt[:, k, t * P:(t + 1) * P],
                                      pw[:, k, n * HALF:(n + 1) * HALF], start=(k == 0), stop=(k == KP - 1))
                q.then_inc(ready, 1)

        @block.scalar
        def _(act):
            for t in range(NT):
                act.wait_ge(ready, t + 1)
                act.copy(proj[:, t, :], out[t % 2][:].rearrange("p a b -> p (a b)")).then_inc(read, 1)


def final_norm(nc, tl, h, gate_logit, proj, eps, gain_dram, out_dram):
    with ExitStack() as ctx:
        gain = tl.sb(ctx, "fn_gain", [P, D])
        square = tl.sb(ctx, "fn_square", [P, D])
        ssq = tl.sb(ctx, "fn_ssq", [P, NT])
        root = tl.sb(ctx, "fn_root", [P, NT])
        rstd = tl.sb(ctx, "fn_rstd", [P, NT])
        gain_loaded = tl.sem("fn_gain_loaded")
        gate_ready = tl.sem("fn_gate_ready")
        part_ready = tl.sem("fn_part_ready")
        h_ready = tl.sem("fn_h_ready")
        squared = tl.sem("fn_squared")
        root_ready = tl.sem("fn_root_ready")
        rstd_ready = tl.sem("fn_rstd_ready")
        row_ready = tl.sem("fn_row_ready")
        stored = tl.sem("fn_stored")
        block = ctx.enter_context(nc.Block())

        @block.scalar
        def _(act):
            for t in range(NT):
                act.activation(gate_logit[:, t, :], gate_logit[:, t, :], ACT.Sigmoid).then_inc(gate_ready, 1)
            for t in range(NT):
                act.wait_ge(h_ready, t + 1)
                if t:
                    act.wait_ge(squared, t)
                act.activation(square[:], h[:, t, :], ACT.Square, accum_out=ssq[:, t:t + 1]).then_inc(squared, 1)
            act.wait_ge(squared, NT)
            act.activation(root[:], ssq[:], ACT.Sqrt, scale=1.0 / D, bias=eps[:, 0:1]).then_inc(root_ready, 1)

        @block.vector
        def _(dve):
            for t in range(NT):
                dve.wait_ge(gate_ready, t + 1)
                dve.tensor_tensor(proj[:, t, :], gate_logit[:, t, :], proj[:, t, :], ALU.mult).then_inc(part_ready, 1)
                dve.wait_ge(part_ready, t + 1)
                dve.tensor_tensor(h[:, t, :], h[:, t, :], proj[:, t, :], ALU.add).then_inc(h_ready, 1)
            dve.wait_ge(root_ready, 1)
            dve.reciprocal(rstd[:], root[:]).then_inc(rstd_ready, 1)
            dve.wait_ge(rstd_ready, 1)
            dve.wait_ge(gain_loaded, 16)
            for t in range(NT):
                dve.scalar_tensor_tensor(out=h[:, t, :], in0=h[:, t, :], scalar=rstd[:, t:t + 1], in1=gain[:],
                                         op0=ALU.mult, op1=ALU.mult).then_inc(row_ready, 1)

        @block.sync
        def _(sp):
            sp.dma_start(gain[:], gain_dram.partition_broadcast(P)).then_inc(gain_loaded, 16)
            for t in range(NT):
                sp.wait_ge(row_ready, t + 1)
                sp.dma_start(out_dram[t * P:(t + 1) * P, :], h[:, t, :]).then_inc(stored, 16)
            sp.wait_ge(stored, 16 * NT)


def program(nc, d, out):
    with ExitStack() as top:
        tl = Tools(nc)
        whole = ExitStack()
        top.enter_context(whole)
        h = tl.sb(whole, "h", [P, NT, D])
        ident = tl.sb(whole, "ident", [P, P])
        gains = tl.sb(whole, "gains", [P, 4, DC])
        eps = tl.sb(whole, "eps", [P, 1])
        const_loaded = tl.sem("const_loaded")
        eps_ready = tl.sem("eps_ready")
        with nc.Block() as block:
            @block.sync
            def _(sp):
                sp.dma_start(ident[:], d["ident"][:, :]).then_inc(const_loaded, 16)
                sp.dma_start(gains[:], d["gains"][:, :, :]).then_inc(const_loaded, 16)
                sp.wait_ge(const_loaded, 32)

            @block.gpsimd
            def _(pool):
                pool.memset(eps[:], EPS).then_inc(eps_ready, 1)

        def gain(n):
            return {"t": gains[:, n, :], "eps": eps}

        att = ExitStack()
        v = tl.sb(att, "v", [P, NT, V_COLS])
        masks = tl.sb(att, "masks", [P, 2 * P], BF16)
        ident16 = tl.sb(att, "ident16", [P, P], BF16)
        perm = tl.sb(att, "perm", [P, P])
        key_rows = tl.sb(att, "key_rows", [4 * FOX_HEADS, T], F32R)
        query_rows = tl.sb(att, "query_rows", [4 * FOX_HEADS, T], F32R)
        head_pick = tl.sb(att, "head_pick", [4 * FOX_HEADS, FOX_HEADS])
        sinks = {"value": tl.sb(att, "sink_value", [P, PAIRS, 2]),
                 "neg_unscaled": tl.sb(att, "sink_neg_unscaled", [P, PAIRS, 2]),
                 "bias": tl.sb(att, "sink_bias", [P, 4]), "bias_ready": tl.sem("sink_bias_ready")}
        att_qk = ExitStack()
        acts = ExitStack()
        xt_hi = tl.sb(acts, "xt_hi", [P, DC, T], F32R, "right")
        xt_lo = tl.sb(acts, "xt_lo", [P, DC, T], F32R, "right")

        def keep_v(dve, s, t, o):
            return dve.tensor_copy(v[:, t, :].rearrange("p (n w) -> p n w", n=2), o[:, :, 0:V_PART])

        token_pass(nc, tl, "mix", h, d["x"], 1, gain(0), ident, (2, V_PART), d["w_v"], (xt_hi, xt_lo), keep_v)
        qk = tl.sb(att_qk, "qk", [P, QK_CHUNKS, T])
        feature_proj(nc, tl, d["w_qk"], xt_hi, xt_lo, qk)
        acts.close()
        with ExitStack() as ctx:
            mask_raw = tl.sb(ctx, "mask_raw", [P, 2 * P])
            loaded = tl.sem("small_loaded")
            block = ctx.enter_context(nc.Block())

            @block.sync
            def _(sp):
                sp.dma_start(mask_raw[:], d["masks"][:, :]).then_inc(loaded, 16)
                sp.dma_start(perm[:], d["perm"][:, :]).then_inc(loaded, 16)
                sp.dma_start(head_pick[:], d["head_pick"][:, :]).then_inc(loaded, 16)
                sp.dma_start(sinks["value"][:], d["sinks"].partition_broadcast(P)).then_inc(loaded, 16)

            @block.vector
            def _(dve):
                dve.wait_ge(loaded, 64)
                dve.tensor_copy(masks[:], mask_raw[:])
                dve.tensor_copy(ident16[:], ident[:])
                dve.tensor_scalar(sinks["neg_unscaled"][:], sinks["value"][:], -1.0 / SCALE, None, ALU.mult)
        rotate(nc, tl, qk, perm, d["cos"], d["sin"])
        decay(nc, tl, v, d["b_forget"], d["tri"], key_rows, query_rows)
        mixing = ExitStack()
        mixed = tl.sb(mixing, "mixed", [P, NT, D], F32, "right")
        attention(nc, tl, qk, v, key_rows, query_rows, sinks, masks, head_pick, ident, ident16, mixed)
        att_qk.close()
        att.close()

        def add_out(dve, s, t, o):
            return dve.tensor_tensor(h[:, t, :], h[:, t, :], o[:].rearrange("p n w -> p (n w)"), ALU.add)

        token_pass(nc, tl, "out", mixed, None, 2, gain(1), ident, (2, HALF), d["w_out"], None, add_out)
        mixing.close()
        tl.recycle()
        experts = ExitStack()
        xn_hi = tl.sb(experts, "xn_hi", [P, DC, T], F32R, "right")
        xn_lo = tl.sb(experts, "xn_lo", [P, DC, T], F32R, "right")
        token_pass(nc, tl, "ffn", h, None, 1, gain(2), ident, None, None, (xn_hi, xn_lo), None)
        gates_dram = nc.dram_tensor("gates", (KEYS, KEYS, T), F32, kind="Internal").ap()
        act_dram = nc.dram_tensor("activations", (KEYS, KEYS, T), F32, kind="Internal").ap()
        chosen = ExitStack()
        gate_hi, gate_lo, first, second = (tl.sb(chosen, n, [P, T]) for n in ("gate_hi", "gate_lo", "first", "second"))
        lists = ExitStack()
        top_v = tl.sb(lists, "top_v", [P, NT, HC, TOPK])
        top_i = tl.sb(lists, "top_i", [P, NT, HC, TOPK])
        peer_scores(nc, tl, d["w_query"], d["sub_keys"], xn_hi, xn_lo, top_v, top_i)
        peer_best(nc, tl, top_v, top_i, ident, gate_hi, gate_lo, first, second)
        lists.close()
        gate_matrix(nc, tl, d["iota"], gate_hi, gate_lo, first, second, gates_dram)
        chosen.close()
        tl.recycle()
        expert_up(nc, tl, d["expert_u"], xn_hi, xn_lo, act_dram)
        experts.close()
        expert_down(nc, tl, d["expert_v"], act_dram, gates_dram, h)
        last = ExitStack()
        logit = tl.sb(last, "logit", [P, NT, D])

        def keep_logit(dve, s, t, o):
            return dve.tensor_copy(logit[:, t, :], o[:].rearrange("p n w -> p (n w)"))

        token_pass(nc, tl, "ple", h, None, 1, gain(3), ident, (2, HALF), d["w_ple_gate"], None, keep_logit)
        proj = tl.sb(last, "proj", [P, NT, D])
        pt = tl.sb(last, "pt", [P, 2, T])
        pw = tl.sb(last, "pw", [P, 2, D])
        layer_input(nc, tl, d["w_ple_proj"], d["p_t"], pt, pw)
        ple_projection(nc, tl, pt, pw, proj)
        final_norm(nc, tl, h, logit, proj, eps, d["norm_final_g"], out)
        last.close()



def layouts(i):
    def contiguous(a):
        return np.ascontiguousarray(a)

    w_in = np.asarray(i["w_in"])[0]
    swa_k0 = SWA_HEADS * HEAD
    swa_v0 = swa_k0 + SWA_KV * HEAD
    fox_q0 = swa_v0 + SWA_KV * HEAD
    fox_k0 = fox_q0 + FOX_HEADS * HEAD
    fox_v0 = fox_k0 + FOX_HEADS * HEAD
    forget0 = fox_v0 + FOX_HEADS * HEAD
    cols = []
    for c in range(PAIRS):
        for head in (c, c + SWA_HEADS // SWA_KV):
            cols += range(head * HEAD, (head + 1) * HEAD)
    cols += range(swa_k0, swa_v0)
    cols += range(fox_q0, fox_v0)
    v_cols = list(range(swa_v0, fox_q0)) + list(range(fox_v0, forget0 + FOX_HEADS))

    def chunked(w):
        return contiguous(w.reshape(DC, P, -1, P).transpose(2, 1, 0, 3))

    gains = [i["norm_mix_g"][0], np.concatenate([i["g_out_a"][0], i["g_out_b"][0]]), i["norm_ffn_g"][0],
             i["norm_ple_g"][0]]
    return {
        "x": contiguous(i["x"][0]),
        "gains": contiguous(np.stack([np.asarray(g).reshape(DC, P).T for g in gains], 1)),
        "w_v": contiguous(w_in[:, v_cols].reshape(DC, P, V_COLS)),
        "w_qk": chunked(w_in[:, cols]),
        "b_forget": contiguous(i["b_forget"][0]),
        "sinks": contiguous(np.asarray(i["sinks"])[0].reshape(2, PAIRS).T),
        "expert_u": contiguous(np.asarray(i["expert_u"])[0].reshape(KEYS, KEYS, DC, P).transpose(1, 3, 2, 0)),
        "expert_v": contiguous(np.asarray(i["expert_v"])[0]),
        "w_query": chunked(np.asarray(i["w_query"])[0]),
        "sub_keys": contiguous(np.asarray(i["sub_keys"])[0].transpose(0, 2, 1)),
        "w_ple_gate": contiguous(np.asarray(i["w_ple_gate"])[0].reshape(DC, P, D)),
        "w_ple_proj": contiguous(np.asarray(i["w_ple_proj"])[0]),
        "p_t": contiguous(np.asarray(i["p"])[0, 0].T),
        "norm_final_g": contiguous(i["norm_final_g"]),
        "w_out": contiguous(np.asarray(i["w_out"])[0].reshape(DC, P, D)),
    }


def constants():
    pos = np.arange(T, dtype=np.float32)
    freq = (np.float32(10000.0) ** (-np.arange(0, HEAD, 2, dtype=np.float32) / np.float32(HEAD))).astype(np.float32)
    ang = (pos[:, None] * freq[None, :]).astype(np.float32)
    feature = np.arange(P)
    cos = np.cos(ang).astype(np.float32).T[feature % (HEAD // 2)]
    sin = np.sin(ang).astype(np.float32).T[feature % (HEAD // 2)]
    first = (feature % HEAD) < HEAD // 2
    sin = np.where(first[:, None], -sin, sin).astype(np.float32)
    partner = np.where(first, feature + HEAD // 2, feature - HEAD // 2)
    perm = np.zeros((P, P), np.float32)
    perm[partner, feature] = 1.0
    q, k = np.arange(P)[:, None], np.arange(P)[None, :]
    masks = np.concatenate([np.where(k > q, 0.0, NEG), np.where(k <= q, 0.0, NEG)], 1).astype(np.float32)
    row = np.arange(4 * FOX_HEADS)
    return {
        "ident": np.eye(P, dtype=np.float32),
        "masks": masks,
        "iota": np.tile(np.arange(KEYS, dtype=np.float32), (P, 1)),
        "perm": perm,
        "head_pick": (row[:, None] % FOX_HEADS == np.arange(FOX_HEADS)[None, :]).astype(np.float32),
        "cos": np.ascontiguousarray(cos),
        "sin": np.ascontiguousarray(sin),
        "tri": (np.arange(P)[:, None] <= np.arange(-(T - P), T)[None, :]).astype(np.float32),
    }


def kernel(**inputs):
    import concourse.bacc as _bacc
    from concourse.bass_utils import run_bass_kernel_spmd as _run

    nc = _bacc.Bacc("TRN2", target_bir_lowering=False, num_devices=1)
    arrays = {**layouts({n: np.asarray(a) for n, a in inputs.items()}), **constants()}
    dram = {n: nc.dram_tensor(f"in_{n}", a.shape, mybir.dt.from_np(a.dtype), kind="ExternalInput").ap()
            for n, a in arrays.items()}
    out = nc.dram_tensor("out", (T, D), F32, kind="ExternalOutput").ap()
    program(nc, dram, out)
    r = _run(nc, [{f"in_{n}": a for n, a in arrays.items()}], core_ids=[0])
    return r.results[0]["out"].reshape(1, T, D)
```

```python
from contextlib import ExitStack

import numpy as np

import concourse.bass as bass
from concourse import mybir

F32 = mybir.dt.float32
F32R = mybir.dt.float32r
BF16 = mybir.dt.bfloat16
U32 = mybir.dt.uint32
ACT = mybir.ActivationFunctionType
ALU = mybir.AluOpType
AX = mybir.AxisListType

P = 128
T = 1024
NT = T // P
D = 1024
DC = D // P
HALF = 512
HEAD = 64
SWA_HEADS, SWA_KV, FOX_HEADS = 8, 2, 8
PAIRS = 4
SWA_Q, SWA_K, FOX_Q, FOX_K = 0, 4, 5, 9
QK_CHUNKS = 13
V_COLS = SWA_KV * HEAD + FOX_HEADS * HEAD + FOX_HEADS
V_FOX = SWA_KV * HEAD
V_FORGET = V_FOX + FOX_HEADS * HEAD
V_PART = V_COLS // 2
PEER_HEADS, KEYS, TOPK = 8, 128, 16
HC = 2 * PEER_HEADS
SEL = PEER_HEADS * TOPK
EPS = 1e-6
NEG = -1e30
LOWEST = -3.4e38
FREE = 1
SCALE = HEAD ** -0.5


def spread(ap, at, n):
    shape = list(ap.shape)
    return ap.unsqueeze(at).broadcast_to(shape[:at] + [n] + shape[at:])


class Tools:

    def __init__(self, nc):
        self.nc, self.held = nc, []

    def sem(self, name):
        self.held.append(self.nc.alloc_semaphore(name=name))
        return self.held[-1]

    def recycle(self):
        self.nc.clear_and_free_semaphores(self.held)
        self.nc.all_engine_barrier()
        self.held = []

    def pair(self, name):
        return [self.sem(f"{name}{s}") for s in range(2)]

    def sb(self, ctx, name, shape, dt=F32, side="left"):
        return ctx.enter_context(self.nc.sbuf_tensor(name, shape, dt, side=side))

    def ps(self, ctx, name, shape, dt=F32):
        return ctx.enter_context(self.nc.psum_tensor(name, shape, dt))


def three_passes(pe, out, lhs_hi, lhs_lo, rhs_hi, rhs_lo, n, first=True, last=True):
    for k in range(n):
        pe.matmul(out, lhs_hi(k), rhs_hi(k), start=first and k == 0, stop=False)
        pe.matmul(out, lhs_hi(k), rhs_lo(k), start=False, stop=False)
        mm = pe.matmul(out, lhs_lo(k), rhs_hi(k), start=False, stop=last and k == n - 1)
    return mm


def token_pass(nc, tl, name, src, src_dram, groups, gain, ident, parts, weights, keep, epilogue,
               save=None):
    with ExitStack() as ctx:
        width = parts[1] if parts else 0
        n_parts = parts[0] if parts else 0
        square = tl.sb(ctx, f"{name}_square", [P, D])
        ssq = tl.sb(ctx, f"{name}_ssq", [P, NT, groups])
        root = tl.sb(ctx, f"{name}_root", [P, NT, groups])
        rstd = tl.sb(ctx, f"{name}_rstd", [P, NT, groups])
        scaled = tl.sb(ctx, f"{name}_scaled", [P, 2, D])
        act_hi = tl.sb(ctx, f"{name}_act_hi", [P, 2, DC, P], F32R)
        act_lo = tl.sb(ctx, f"{name}_act_lo", [P, 2, DC, P], F32R)
        turned = [tl.ps(ctx, f"{name}_turned{s}", [P, DC, P]) for s in range(2)]
        if weights is not None:
            w_raw = tl.sb(ctx, f"{name}_w_raw", [P, 2, n_parts * width])
            w_hi = tl.sb(ctx, f"{name}_w_hi", [P, DC, n_parts * width], F32R)
            w_lo = tl.sb(ctx, f"{name}_w_lo", [P, DC, n_parts * width], F32R)
            out = [tl.ps(ctx, f"{name}_out{s}", [P, n_parts, HALF]) for s in range(2)]
        src_loaded = tl.sem(f"{name}_src_loaded")
        saved = tl.sem(f"{name}_saved")
        w_loaded = tl.pair(f"{name}_w_loaded")
        w_hi_ready = tl.sem(f"{name}_w_hi_ready")
        w_ready = tl.sem(f"{name}_w_ready")
        squared = tl.sem(f"{name}_squared")
        rooted = tl.sem(f"{name}_rooted")
        rstd_ready = tl.sem(f"{name}_rstd_ready")
        scaled_ready = tl.pair(f"{name}_scaled_ready")
        turned_ready = tl.pair(f"{name}_turned_ready")
        hi_ready = tl.pair(f"{name}_hi_ready")
        lo_ready = tl.pair(f"{name}_lo_ready")
        kept = tl.pair(f"{name}_kept")
        out_ready = tl.pair(f"{name}_out_ready")
        out_read = tl.pair(f"{name}_out_read")
        block = ctx.enter_context(nc.Block())
        gw = D // groups

        @block.sync
        def _(sp):
            if src_dram is not None:
                sp.dma_start(src[:], src_dram.rearrange("(t p) d -> p t d", p=P)).then_inc(src_loaded, 16)
            if save is not None:
                sp.dma_start(save.rearrange("(t p) d -> p t d", p=P), src[:]).then_inc(saved, 16)
                sp.wait_ge(saved, 16)
            if weights is not None:
                for k in range(DC):
                    if k >= 2:
                        sp.wait_ge(w_ready, k - 1)
                    sp.dma_start(w_raw[:, k % 2, :], weights[k, :, :]).then_inc(w_loaded[k % 2], 16)

        @block.scalar
        def _(act):
            if src_dram is not None:
                act.wait_ge(src_loaded, 16)
            for t in range(NT):
                for g in range(groups):
                    q = act.activation(square[:, 0:gw], src[:, t, g * gw:(g + 1) * gw], ACT.Square,
                                       accum_out=ssq[:, t, g:g + 1])
                    q.then_inc(squared, 1)
                    act.wait_ge(squared, t * groups + g + 1)
            act.activation(root[:], ssq[:], ACT.Sqrt, scale=1.0 / gw, bias=gain["eps"][:, 0:1]).then_inc(rooted, 1)
            if weights is not None:
                for k in range(DC):
                    act.wait_ge(w_loaded[k % 2], 16 * (k // 2 + 1))
                    act.copy(w_hi[:, k, :], w_raw[:, k % 2, :]).then_inc(w_hi_ready, 1)
            with act.Fori(0, NT // 2) as i:
                for s in range(2):
                    act.wait_ge(turned_ready[s], i + 1 + FREE)
                    if weights is not None:
                        act.wait_ge(out_ready[s], i + FREE)
                    if keep is not None:
                        act.wait_ge(kept[s], i + FREE)
                    for k in range(DC):
                        q = act.mul(act_hi[:, s, k, :], turned[s][:, k, :], gain["t"][:, k:k + 1])
                    q.then_inc(hi_ready[s], 1)

        @block.vector
        def _(dve):
            dve.wait_ge(rooted, 1)
            dve.reciprocal(rstd[:], root[:]).then_inc(rstd_ready, 1)
            if weights is not None:
                for k in range(DC):
                    dve.wait_ge(w_hi_ready, k + 1)
                    dve.tensor_tensor(w_lo[:, k, :], w_raw[:, k % 2, :], w_hi[:, k, :].bitcast(F32),
                                      ALU.subtract).then_inc(w_ready, 1)
            dve.wait_ge(rstd_ready, 1)
            for s in range(2):
                dve.sem_inc(lo_ready[s], FREE)
                dve.sem_inc(out_read[s], FREE)
            with dve.Fori(0, NT // 2) as i:
                for s in range(2):
                    t = i * 2 + s
                    dve.wait_ge(turned_ready[s], i + FREE)
                    for g in range(groups):
                        q = dve.tensor_scalar(scaled[:, s, g * gw:(g + 1) * gw], src[:, t, g * gw:(g + 1) * gw],
                                              rstd[:, t, g:g + 1], None, ALU.mult)
                    q.then_inc(scaled_ready[s], 1)
                for s in range(2):
                    dve.wait_ge(hi_ready[s], i + 1)
                    for k in range(DC):
                        q = dve.scalar_tensor_tensor(out=act_lo[:, s, k, :], in0=turned[s][:, k, :],
                                                     scalar=gain["t"][:, k:k + 1],
                                                     in1=act_hi[:, s, k, :].bitcast(F32),
                                                     op0=ALU.mult, op1=ALU.subtract)
                    q.then_inc(lo_ready[s], 1)
                if weights is not None:
                    for s in range(2):
                        dve.wait_ge(out_ready[s], i + 1 + FREE)
                        epilogue(dve, s, i * 2 + s, out[s]).then_inc(out_read[s], 1)

        @block.tensor
        def _(pe):
            for s in range(2):
                pe.sem_inc(turned_ready[s], FREE)
                pe.sem_inc(out_ready[s], FREE)
            if weights is not None:
                pe.wait_ge(w_ready, DC)
            with pe.Fori(0, NT // 2) as i:
                for s in range(2):
                    pe.wait_ge(scaled_ready[s], i + 1)
                    pe.wait_ge(lo_ready[s], i + FREE)
                    for k in range(DC):
                        q = pe.transpose(turned[s][:, k, :], scaled[:, s, k * P:(k + 1) * P], ident[:])
                    q.then_inc(turned_ready[s], 1)
                if weights is not None:
                    for s in range(2):
                        pe.wait_ge(lo_ready[s], i + 1 + FREE)
                        pe.wait_ge(out_read[s], i + FREE)
                        for n in range(n_parts):
                            q = three_passes(pe, out[s][:, n, 0:width],
                                             lambda k: act_hi[:, s, k, :], lambda k: act_lo[:, s, k, :],
                                             lambda k: w_hi[:, k, n * width:(n + 1) * width],
                                             lambda k: w_lo[:, k, n * width:(n + 1) * width], DC)
                        q.then_inc(out_ready[s], 1)

        if keep is not None:
            @block.gpsimd
            def _(pool):
                for s in range(2):
                    pool.sem_inc(kept[s], FREE)
                with pool.Fori(0, NT // 2) as i:
                    for s in range(2):
                        t = i * 2 + s
                        pool.wait_ge(lo_ready[s], i + 1 + FREE)
                        pool.tensor_copy(keep[0][:, :, bass.ts(t, P)], act_hi[:, s, :, :].bitcast(F32))
                        pool.tensor_copy(keep[1][:, :, bass.ts(t, P)], act_lo[:, s, :, :].bitcast(F32)) \
                            .then_inc(kept[s], 1)


def feature_proj(nc, tl, w_dram, xt_hi, xt_lo, qk):
    with ExitStack() as ctx:
        w_raw = tl.sb(ctx, "fp_w_raw", [P, 2, DC, P])
        w_hi = tl.sb(ctx, "fp_w_hi", [P, 2, DC, P], F32R)
        w_lo = tl.sb(ctx, "fp_w_lo", [P, 2, DC, P], F32R)
        out = [tl.ps(ctx, f"fp_out{s}", [P, 2, HALF]) for s in range(2)]
        w_loaded = tl.pair("fp_w_loaded")
        hi_ready = tl.pair("fp_hi_ready")
        lo_ready = tl.pair("fp_lo_ready")
        out_ready = tl.pair("fp_out_ready")
        act_read = tl.pair("fp_act_read")
        dve_read = tl.pair("fp_dve_read")
        block = ctx.enter_context(nc.Block())

        def chunks(engine, step):
            with engine.Fori(0, QK_CHUNKS // 2) as i:
                for s in range(2):
                    step(s, i, i * 2 + s)
            step(0, QK_CHUNKS // 2, QK_CHUNKS - 1)

        @block.sync
        def _(sp):
            def load(s, i, c):
                sp.wait_ge(lo_ready[s], i + FREE)
                sp.dma_start(w_raw[:, s, :, :], w_dram[c, :, :, :]).then_inc(w_loaded[s], 16)
            chunks(sp, load)

        @block.scalar
        def _(act):
            def step(s, i, c):
                act.wait_ge(w_loaded[s], (i + 1) * 16)
                act.wait_ge(out_ready[s], i + FREE)
                act.copy(w_hi[:, s, :, :], w_raw[:, s, :, :]).then_inc(hi_ready[s], 1)
                act.wait_ge(out_ready[s], i + 1 + FREE)
                act.copy(qk[:, c, 0:HALF], out[s][:, 0, :]).then_inc(act_read[s], 1)
            for s in range(2):
                act.sem_inc(act_read[s], FREE)
            chunks(act, step)

        @block.vector
        def _(dve):
            def step(s, i, c):
                dve.wait_ge(hi_ready[s], i + 1)
                dve.tensor_tensor(w_lo[:, s, :, :], w_raw[:, s, :, :], w_hi[:, s, :, :].bitcast(F32),
                                  ALU.subtract).then_inc(lo_ready[s], 1)
                dve.wait_ge(out_ready[s], i + 1 + FREE)
                dve.tensor_copy(qk[:, c, HALF:T], out[s][:, 1, :]).then_inc(dve_read[s], 1)
            for s in range(2):
                dve.sem_inc(lo_ready[s], FREE)
                dve.sem_inc(dve_read[s], FREE)
            chunks(dve, step)

        @block.tensor
        def _(pe):
            def step(s, i, c):
                pe.wait_ge(lo_ready[s], i + 1 + FREE)
                pe.wait_ge(act_read[s], i + FREE)
                pe.wait_ge(dve_read[s], i + FREE)
                for n in range(2):
                    q = three_passes(pe, out[s][:, n, :], lambda k: w_hi[:, s, k, :], lambda k: w_lo[:, s, k, :],
                                     lambda k: xt_hi[:, k, n * HALF:(n + 1) * HALF],
                                     lambda k: xt_lo[:, k, n * HALF:(n + 1) * HALF], DC)
                q.then_inc(out_ready[s], 1)
            for s in range(2):
                pe.sem_inc(out_ready[s], FREE)
            chunks(pe, step)


def rotate(nc, tl, qk, perm, cos_dram, sin_dram):
    with ExitStack() as ctx:
        cos = tl.sb(ctx, "rot_cos", [P, T])
        sin = tl.sb(ctx, "rot_sin", [P, T])
        partner = tl.sb(ctx, "rot_partner", [P, T])
        swapped = [tl.ps(ctx, f"rot_swapped{s}", [P, 2, HALF]) for s in range(2)]
        loaded = tl.sem("rot_loaded")
        swapped_ready = tl.sem("rot_swapped_ready")
        partner_ready = tl.sem("rot_partner_ready")
        straight_ready = tl.sem("rot_straight_ready")
        rotated = tl.sem("rot_rotated")
        block = ctx.enter_context(nc.Block())
        n_chunks = SWA_K + 1

        @block.sync
        def _(sp):
            sp.dma_start(cos[:], cos_dram[:, :]).then_inc(loaded, 16)
            sp.dma_start(sin[:], sin_dram[:, :]).then_inc(loaded, 16)

        @block.tensor
        def _(pe):
            for c in range(n_chunks):
                if c >= 2:
                    pe.wait_ge(partner_ready, c - 1)
                for n in range(2):
                    q = pe.matmul(swapped[c % 2][:, n, :], perm[:], qk[:, c, n * HALF:(n + 1) * HALF],
                                  start=True, stop=True)
                q.then_inc(swapped_ready, 1)

        @block.gpsimd
        def _(pool):
            pool.wait_ge(loaded, 32)
            for c in range(n_chunks):
                pool.wait_ge(swapped_ready, c + 1)
                pool.tensor_tensor(qk[:, c, :], qk[:, c, :], cos[:], ALU.mult).then_inc(straight_ready, 1)

        @block.vector
        def _(dve):
            dve.wait_ge(loaded, 32)
            for c in range(n_chunks):
                dve.wait_ge(swapped_ready, c + 1)
                dve.wait_ge(rotated, c)
                dve.tensor_tensor(partner[:], swapped[c % 2][:].rearrange("p a b -> p (a b)"), sin[:],
                                  ALU.mult).then_inc(partner_ready, 1)
                dve.wait_ge(partner_ready, c + 1)
                dve.wait_ge(straight_ready, c + 1)
                dve.tensor_tensor(qk[:, c, :], qk[:, c, :], partner[:], ALU.add).then_inc(rotated, 1)


def decay(nc, tl, v, b_forget, tri_dram, key_rows, query_rows):
    with ExitStack() as ctx:
        tri = tl.sb(ctx, "dec_tri", [P, 2 * T - P])
        bias = tl.sb(ctx, "dec_bias", [P, FOX_HEADS])
        steps = [tl.sb(ctx, f"dec_step{n}", [P, NT, FOX_HEADS]) for n in range(7)]
        z, neg_abs, e, soft, low, log_f, z_neg = steps
        c = tl.sb(ctx, "dec_c", [FOX_HEADS, T])
        parts = [tl.sb(ctx, f"dec_part{n}", [FOX_HEADS, T], F32R) for n in range(4)]
        c_hi, c_lo, n_hi, n_lo = parts
        total = tl.ps(ctx, "dec_total", [P, 2, HALF])
        loaded = tl.sem("dec_loaded")
        step = tl.sem("dec_step")
        exp_ready = tl.sem("dec_exp_ready")
        ln_ready = tl.sem("dec_ln_ready")
        logs_ready = tl.sem("dec_logs_ready")
        summed = tl.sem("dec_summed")
        parts_ready = tl.sem("dec_parts_ready")
        ones_ready = tl.sem("dec_ones_ready")
        placed = tl.sem("dec_placed")
        block = ctx.enter_context(nc.Block())

        @block.sync
        def _(sp):
            sp.dma_start(tri[:], tri_dram[:, :]).then_inc(loaded, 16)
            sp.dma_start(bias[:], b_forget.partition_broadcast(P)).then_inc(loaded, 16)
            sp.wait_ge(ones_ready, 2)
            sp.wait_ge(parts_ready, 1)
            for rows, n, part in ((key_rows, 0, n_hi), (key_rows, 1, n_lo), (query_rows, 2, c_hi), (query_rows, 3, c_lo)):
                sp.dma_start(rows[n * FOX_HEADS:(n + 1) * FOX_HEADS, :].bitcast(F32), part[:].bitcast(F32)).then_inc(placed, 16)
            sp.wait_ge(placed, 64)

        @block.gpsimd
        def _(pool):
            pool.memset(key_rows[:].bitcast(F32), 1.0).then_inc(ones_ready, 1)
            pool.memset(query_rows[:].bitcast(F32), 1.0).then_inc(ones_ready, 1)

        @block.vector
        def _(dve):
            n = [0]

            def done(q):
                n[0] += 1
                q.then_inc(step, 1)
                dve.wait_ge(step, n[0])

            dve.wait_ge(loaded, 32)
            done(dve.tensor_tensor(z[:], v[:, :, V_FORGET:V_COLS], spread(bias[:], 1, NT), ALU.add))
            done(dve.tensor_scalar(z_neg[:], z[:], -1.0, None, ALU.mult))
            done(dve.tensor_tensor(neg_abs[:], z[:], z_neg[:], ALU.min))
            done(dve.tensor_scalar(low[:], z[:], 0.0, None, ALU.min))
            dve.wait_ge(ln_ready, 1)
            dve.tensor_tensor(log_f[:], low[:], soft[:], ALU.subtract).then_inc(logs_ready, 1)
            dve.wait_ge(summed, 1)
            done(dve.tensor_scalar(c[:], total[0:FOX_HEADS, :, :].rearrange("p a b -> p (a b)"), 1.0 / SCALE, None,
                                   ALU.mult))
            done(dve.tensor_copy(c_hi[:], c[:]))
            done(dve.tensor_tensor(c_lo[:], c[:], c_hi[:].bitcast(F32), ALU.subtract))
            done(dve.tensor_scalar(n_hi[:], c_hi[:].bitcast(F32), -1.0, None, ALU.mult))
            done(dve.tensor_scalar(n_lo[:], c_lo[:].bitcast(F32), -1.0, None, ALU.mult))
            dve.tensor_copy(c[:, 0:1], c[:, 0:1]).then_inc(parts_ready, 1)

        @block.scalar
        def _(act):
            act.wait_ge(step, 3)
            act.activation(e[:], neg_abs[:], ACT.Exp).then_inc(exp_ready, 1)
            act.wait_ge(exp_ready, 1)
            act.activation(soft[:], e[:], ACT.Ln, bias=1.0).then_inc(ln_ready, 1)

        @block.tensor
        def _(pe):
            pe.wait_ge(logs_ready, 1)
            for n in range(2):
                for t in range(NT):
                    at = T - P - t * P + n * HALF
                    q = pe.matmul(total[0:FOX_HEADS, n, :], log_f[:, t, :], tri[:, at:at + HALF],
                                  start=(t == 0), stop=(t == NT - 1))
            q.then_inc(summed, 1)


def attention(nc, tl, qk, v, key_rows, query_rows, sinks, masks, head_pick, ident, ident16, mixed):
    with ExitStack() as ctx:
        fox_q = tl.sb(ctx, "at_fox_q", [P, 2, P])
        swa_q = tl.sb(ctx, "at_swa_q", [P, 2, P])
        fox_rows = tl.sb(ctx, "at_fox_rows", [4 * FOX_HEADS, 2, P], F32R)
        fox_p = tl.sb(ctx, "at_fox_p", [P, 2, T])
        swa_p = tl.sb(ctx, "at_swa_p", [P, 2, 2 * P])
        turned = tl.sb(ctx, "at_turned_sb", [P, 2, NT, P])
        swa_turned = tl.sb(ctx, "at_swa_turned", [P, 2, 2, P])
        neg_max = tl.sb(ctx, "at_neg_max", [P, 4])
        neg_cap = tl.sb(ctx, "at_neg_cap", [P, 2])
        row_sum = tl.sb(ctx, "at_row_sum", [P, 4])
        sink_e = tl.sb(ctx, "at_sink_e", [P, 2])
        total = tl.sb(ctx, "at_total", [P, 4])
        inv = tl.sb(ctx, "at_inv", [P, 4])
        fox_s = tl.ps(ctx, "at_fox_s", [P, 2, 2, HALF])
        swa_s = tl.ps(ctx, "at_swa_s", [P, 2, 2 * P])
        turn = tl.ps(ctx, "at_turn", [P, NT, P])
        o = tl.ps(ctx, "at_o", [P, 4, HEAD])

        names = ("q_ready rows_ready fox_scored swa_scored fox_max swa_max swa_cap fox_prob swa_prob sink_ready "
                 "zeroed turned_ready taken summed inv_ready fox_o swa_o o_read")
        s = {n: tl.sem("at_" + n) for n in names.split()}
        block = ctx.enter_context(nc.Block())

        @block.vector
        def _(dve):
            dve.sem_inc(s["inv_ready"], FREE)
            dve.sem_inc(s["taken"], FREE)
            dve.sem_inc(s["o_read"], FREE)
            dve.memset(fox_q[:], 0.0).then_inc(s["zeroed"], 1)
            dve.memset(swa_q[:], 0.0).then_inc(s["zeroed"], 1)
            dve.wait_ge(s["zeroed"], 2)
            for j in range(NT):
                n_keys = (j + 1) * P
                lo = 0 if j else P
                with dve.Fori(0, PAIRS) as c:
                    step = c + j * PAIRS
                    dve.wait_ge(s["fox_scored"], step + FREE)
                    dve.wait_ge(s["swa_scored"], step + FREE)
                    for q, chunk in ((fox_q, FOX_Q), (swa_q, SWA_Q)):
                        for u in range(2):
                            at = slice(u * HEAD, (u + 1) * HEAD)
                            dve.tensor_copy(q[at, u, :], qk[at, chunk + c, j * P:(j + 1) * P]) \
                                .then_inc(s["q_ready"], 1)
                    for u in range(2):
                        dve.tensor_scalar(fox_rows[:, u, :], query_rows[:, j * P:(j + 1) * P].bitcast(F32),
                                          head_pick[:, bass.ds(2 * c + u, 1)], None,
                                          ALU.mult).then_inc(s["rows_ready"], 1)
                    dve.wait_ge(s["fox_scored"], step + 1 + FREE)
                    dve.tensor_reduce(neg_max[:, 0:2],
                                      fox_s[:].rearrange("p h a b -> p h (a b)")[:, :, 0:n_keys], AX.X, ALU.max,
                                      negate=True).then_inc(s["fox_max"], 1)
                    dve.wait_ge(s["swa_scored"], step + 1 + FREE)
                    dve.tensor_reduce(neg_cap[:], swa_s[:, :, lo:2 * P], AX.X, ALU.max,
                                      negate=True).then_inc(s["swa_cap"], 1)
                    dve.wait_ge(s["swa_cap"], step + 1)
                    dve.tensor_tensor(neg_max[:, 2:4], neg_cap[:], sinks["neg_unscaled"][:, c, :],
                                      ALU.min).then_inc(s["swa_max"], 1)
                    for h in range(2):
                        dve.wait_ge(s["turned_ready"], step * 3 + h + 1 + FREE)
                        dve.tensor_copy(turned[:, h, 0:j + 1, :], turn[:, 0:j + 1, :]).then_inc(s["taken"], 1)
                    dve.wait_ge(s["turned_ready"], step * 3 + 3 + FREE)
                    dve.tensor_copy(swa_turned[:, :, lo // P:2, :],
                                    turn[:].rearrange("p (h b) q -> p h b q", b=4)[:, :, lo // P:2, :]) \
                        .then_inc(s["taken"], 1)
                    dve.wait_ge(s["sink_ready"], step + 1)
                    dve.tensor_copy(total[:, 0:2], row_sum[:, 0:2]).then_inc(s["summed"], 1)
                    dve.tensor_tensor(total[:, 2:4], row_sum[:, 2:4], sink_e[:], ALU.add).then_inc(s["summed"], 1)
                    dve.wait_ge(s["summed"], step * 2 + 2)
                    dve.reciprocal(inv[:], total[:]).then_inc(s["inv_ready"], 1)
                    dve.wait_ge(s["inv_ready"], step + 1 + FREE)
                    dve.wait_ge(s["swa_o"], step + 1)
                    fox_at = FOX_HEADS * HEAD
                    dve.tensor_tensor(mixed[:, j, bass.ds(c * 2 * HEAD + fox_at, 2 * HEAD)].rearrange(
                        "p (h d) -> p h d", d=HEAD), o[:, 0:2, :], spread(inv[:, 0:2], 2, HEAD), ALU.mult)
                    swa = mixed[:, j, 0:fox_at].rearrange("p (u c d) -> p u c d", u=2, d=HEAD)
                    dve.tensor_tensor(swa[:, :, c, :], o[:, 2:4, :], spread(inv[:, 2:4], 2, HEAD),
                                      ALU.mult).then_inc(s["o_read"], 1)

        @block.scalar
        def _(act):
            act.sem_inc(s["fox_prob"], FREE)
            act.sem_inc(s["swa_prob"], FREE)
            for j in range(NT):
                n_keys = (j + 1) * P
                lo = 0 if j else P
                with act.Fori(0, PAIRS) as c:
                    step = c + j * PAIRS
                    act.wait_ge(s["fox_max"], step + 1)
                    for h in range(2):
                        act.mul(sinks["bias"][:, h:h + 1], neg_max[:, h:h + 1], SCALE).then_inc(sinks["bias_ready"], 1)
                    act.wait_ge(sinks["bias_ready"], step * 4 + 2)
                    act.wait_ge(s["turned_ready"], step * 3 + FREE)
                    act.wait_ge(s["inv_ready"], step + FREE)
                    for h in range(2):
                        act.activation(fox_p[:, h, 0:n_keys], fox_s[:, h, :, :].rearrange("p a b -> p (a b)")[:, 0:n_keys],
                                       ACT.Exp, bias=sinks["bias"][:, h:h + 1], scale=SCALE,
                                       accum_out=row_sum[:, h:h + 1]).then_inc(s["fox_prob"], 1)
                    act.wait_ge(s["swa_max"], step + 1)
                    for h in range(2, 4):
                        act.mul(sinks["bias"][:, h:h + 1], neg_max[:, h:h + 1], SCALE).then_inc(sinks["bias_ready"], 1)
                    act.wait_ge(sinks["bias_ready"], step * 4 + 4)
                    for h in range(2):
                        act.activation(swa_p[:, h, lo:2 * P], swa_s[:, h, lo:2 * P], ACT.Exp,
                                       bias=sinks["bias"][:, 2 + h:3 + h], scale=SCALE,
                                       accum_out=row_sum[:, 2 + h:3 + h]).then_inc(s["swa_prob"], 1)
                    for h in range(2):
                        q = act.activation(sink_e[:, h:h + 1], sinks["value"][:, c, h:h + 1], ACT.Exp,
                                           bias=sinks["bias"][:, 2 + h:3 + h])
                    q.then_inc(s["sink_ready"], 1)

        @block.tensor
        def _(pe):
            pe.sem_inc(s["fox_scored"], FREE)
            pe.sem_inc(s["swa_scored"], FREE)
            pe.sem_inc(s["turned_ready"], FREE)
            for j in range(NT):
                n_keys = (j + 1) * P
                lo = 0 if j else P
                with pe.Fori(0, PAIRS) as c:
                    step = c + j * PAIRS
                    pe.wait_ge(s["q_ready"], (step + 1) * 4)
                    pe.wait_ge(s["rows_ready"], (step + 1) * 2)
                    pe.wait_ge(s["fox_prob"], step * 2 + FREE)
                    for h in range(2):
                        for n in range((n_keys + HALF - 1) // HALF):
                            end = min(HALF, n_keys - n * HALF)
                            own = n * HALF + end == n_keys
                            out = fox_s[:, h, n, 0:end]
                            pe.matmul(out, fox_q[:, h, :], qk[:, FOX_K + c, n * HALF:n * HALF + end],
                                      start=True, stop=False)
                            if own:
                                pe.matmul(fox_s[:, h, n, end - P:end], ident16[:], masks[:, P:2 * P],
                                          start=False, stop=False, skip_group_check=True)
                            q = pe.matmul(out, fox_rows[:, h, :], key_rows[:, n * HALF:n * HALF + end],
                                          start=False, stop=True)
                    q.then_inc(s["fox_scored"], 1)
                    pe.wait_ge(s["swa_prob"], step * 2 + FREE)
                    for h in range(2):
                        keys = qk[:, SWA_K, (j - 1) * P + lo:(j + 1) * P]
                        pe.matmul(swa_s[:, h, lo:2 * P], swa_q[:, h, :], keys, start=True, stop=False)
                        q = pe.matmul(swa_s[:, h, lo:2 * P], ident16[:], masks[:, lo:2 * P], start=False, stop=True)
                    q.then_inc(s["swa_scored"], 1)
                    for h in range(2):
                        pe.wait_ge(s["fox_prob"], step * 2 + h + 1 + FREE)
                        pe.wait_ge(s["taken"], step * 3 + h + FREE)
                        for b in range(j + 1):
                            q = pe.transpose(turn[:, b, :], fox_p[:, h, b * P:(b + 1) * P], ident[:])
                        q.then_inc(s["turned_ready"], 1)
                    pe.wait_ge(s["swa_prob"], step * 2 + 2 + FREE)
                    pe.wait_ge(s["taken"], step * 3 + 2 + FREE)
                    for h in range(2):
                        for b in range(lo // P, 2):
                            q = pe.transpose(turn[:, 4 * h + b, :], swa_p[:, h, b * P:(b + 1) * P], ident[:])
                    q.then_inc(s["turned_ready"], 1)
                    pe.wait_ge(s["o_read"], step + FREE)
                    pe.wait_ge(s["taken"], step * 3 + 2 + FREE)
                    for h in range(2):
                        for b in range(j + 1):
                            pe.matmul(o[:, h, :], turned[:, h, b, :],
                                      v[:, b, bass.ds(c * 2 * HEAD + (V_FOX + h * HEAD), HEAD)],
                                      start=(b == 0), stop=(b == j))
                    pe.wait_ge(s["taken"], step * 3 + 3 + FREE)
                    for h in range(2):
                        for b in range(lo // P, 2):
                            q = pe.matmul(o[:, 2 + h, :], swa_turned[:, h, b, :],
                                          v[:, j - 1 + b, h * HEAD:(h + 1) * HEAD],
                                          start=(b == lo // P), stop=(b == 1))
                    q.then_inc(s["swa_o"], 1)


def wait_for(engine, sem, value):
    if not (isinstance(value, int) and value == 0):
        engine.wait_ge(sem, value)


def wait_apart(engine, sem, value, passed):
    engine.wait_ge(sem, value)
    engine.sem_inc(passed, 1)


def peer_scores(nc, tl, w_dram, keys_dram, xn_hi, xn_lo, top_v, top_i):
    with ExitStack() as ctx:
        w_raw = tl.sb(ctx, "ps_w_raw", [P, 2, DC, P])
        w_hi = tl.sb(ctx, "ps_w_hi", [P, 2, DC, P], F32R)
        w_lo = tl.sb(ctx, "ps_w_lo", [P, 2, DC, P], F32R)
        keys = tl.sb(ctx, "ps_keys", [P, 2, KEYS])
        query = tl.sb(ctx, "ps_query", [P, 2, T])
        best = tl.sb(ctx, "ps_best", [P, 2, NT, TOPK])
        where = tl.sb(ctx, "ps_where", [P, 2, NT, TOPK], U32)
        rest = tl.sb(ctx, "ps_rest", [P, NT, KEYS])
        q_out = [tl.ps(ctx, f"ps_q_out{s}", [P, 2, HALF]) for s in range(2)]
        score = [tl.ps(ctx, f"ps_score{s}", [P, NT, KEYS]) for s in range(2)]
        keys_loaded = tl.sem("ps_keys_loaded")
        w_loaded = tl.pair("ps_w_loaded")
        hi_ready = tl.pair("ps_hi_ready")
        lo_ready = tl.pair("ps_lo_ready")
        q_out_ready = tl.pair("ps_q_out_ready")
        query_ready = tl.pair("ps_query_ready")
        score_ready = tl.pair("ps_score_ready")
        score_read = tl.pair("ps_score_read")
        sweep = tl.sem("ps_sweep")
        passed = tl.sem("ps_passed")
        stored = tl.pair("ps_stored")
        block = ctx.enter_context(nc.Block())

        @block.sync
        def _(sp):
            sp.dma_start(keys[:], keys_dram.rearrange("c p k -> p c k")).then_inc(keys_loaded, 16)
            with sp.Fori(0, PEER_HEADS) as i:
                for s in range(2):
                    sp.wait_ge(lo_ready[s], i + FREE)
                    sp.dma_start(w_raw[:, s, :, :], w_dram[i * 2 + s, :, :, :]).then_inc(w_loaded[s], 16)

        @block.scalar
        def _(act):
            for s in range(2):
                act.sem_inc(query_ready[s], FREE)
            with act.Fori(0, PEER_HEADS) as i:
                for s in range(2):
                    act.wait_ge(w_loaded[s], (i + 1) * 16)
                    act.wait_ge(q_out_ready[s], i + FREE)
                    act.copy(w_hi[:, s, :, :], w_raw[:, s, :, :]).then_inc(hi_ready[s], 1)
                for s in range(2):
                    act.wait_ge(q_out_ready[s], i + 1 + FREE)
                    act.wait_ge(score_ready[s], i + FREE)
                    act.copy(query[:, s, :], q_out[s][:].rearrange("p a b -> p (a b)")) \
                        .then_inc(query_ready[s], 1)

        @block.tensor
        def _(pe):
            for s in range(2):
                pe.sem_inc(q_out_ready[s], FREE)
                pe.sem_inc(score_ready[s], FREE)
            pe.wait_ge(keys_loaded, 16)
            with pe.Fori(0, PEER_HEADS) as i:
                for s in range(2):
                    pe.wait_ge(lo_ready[s], i + 1 + FREE)
                    pe.wait_ge(query_ready[s], i + FREE)
                    for n in range(2):
                        q = three_passes(pe, q_out[s][:, n, :], lambda k: w_hi[:, s, k, :],
                                         lambda k: w_lo[:, s, k, :],
                                         lambda k: xn_hi[:, k, n * HALF:(n + 1) * HALF],
                                         lambda k: xn_lo[:, k, n * HALF:(n + 1) * HALF], DC)
                    q.then_inc(q_out_ready[s], 1)
                for s in range(2):
                    pe.wait_ge(query_ready[s], i + 1 + FREE)
                    pe.wait_ge(score_read[s], i + FREE)
                    for t in range(NT):
                        q = pe.matmul(score[s][:, t, :], query[:, s, t * P:(t + 1) * P], keys[:, s, :],
                                      start=True, stop=True)
                    q.then_inc(score_ready[s], 1)

        @block.vector
        def _(dve):
            for s in range(2):
                dve.sem_inc(score_read[s], FREE)
            with dve.Fori(0, PEER_HEADS) as i:
                for s in range(2):
                    done = (i * 2 + s) * 5
                    dve.wait_ge(score_ready[s], i + 1 + FREE)
                    wait_apart(dve, stored[s], i + FREE, passed)
                    for t in range(NT):
                        q = dve.max(best[:, s, t, 0:8], score[s][:, t, :])
                    q.then_inc(sweep, 1)
                    wait_apart(dve, sweep, done + 1, passed)
                    for t in range(NT):
                        q = dve.max_index(where[:, s, t, 0:8], best[:, s, t, 0:8], score[s][:, t, :])
                    q.then_inc(sweep, 1)
                    wait_apart(dve, sweep, done + 2, passed)
                    for t in range(NT):
                        q = dve.match_replace(rest[:, t, :], best[:, s, t, 0:8], score[s][:, t, :], LOWEST)
                    q.then_inc(sweep, 1)
                    wait_apart(dve, sweep, done + 3, passed)
                    for t in range(NT):
                        q = dve.max(best[:, s, t, 8:16], rest[:, t, :])
                        if t == 0:
                            q.then_inc(score_read[s], 1)
                    q.then_inc(sweep, 1)
                    wait_apart(dve, sweep, done + 4, passed)
                    for t in range(NT):
                        q = dve.max_index(where[:, s, t, 8:16], best[:, s, t, 8:16], rest[:, t, :])
                    q.then_inc(sweep, 1)

        @block.gpsimd
        def _(pool):
            for s in range(2):
                pool.sem_inc(lo_ready[s], FREE)
                pool.sem_inc(stored[s], FREE)
            with pool.Fori(0, PEER_HEADS) as i:
                for s in range(2):
                    pool.wait_ge(hi_ready[s], i + 1)
                    pool.tensor_tensor(w_lo[:, s, :, :], w_raw[:, s, :, :], w_hi[:, s, :, :].bitcast(F32),
                                       ALU.subtract).then_inc(lo_ready[s], 1)
                for s in range(2):
                    pool.wait_ge(sweep, (i * 2 + s + 1) * 5)
                    pool.tensor_copy(top_v[:, :, i * 2 + s, :], best[:, s, :, :])
                    pool.tensor_copy(top_i[:, :, i * 2 + s, :], where[:, s, :, :]).then_inc(stored[s], 1)


def experts_up(nc, tl, u_dram, iota_dram, xn_hi, xn_lo, top_v, top_i, ident, act_dram, gates_dram):
    with ExitStack() as ctx:
        GROUPS, LOTS, LOT = 8, 4, 4
        SIDE = P // 2
        u_raw = tl.sb(ctx, "eu_u_raw", [P, 2, DC, KEYS])
        u_hi = tl.sb(ctx, "eu_u_hi", [P, 2, DC, KEYS], F32R)
        u_lo = tl.sb(ctx, "eu_u_lo", [P, 2, DC, KEYS], F32R)
        gelu = tl.sb(ctx, "eu_gelu", [P, 2, T])
        iota = tl.sb(ctx, "eu_iota", [P, KEYS])
        hot = tl.sb(ctx, "eu_hot", [P, 2, 2, LOT, KEYS], F32R)
        hot_gate = tl.sb(ctx, "eu_hot_gate", [P, 2, 2, LOT, KEYS], F32R)
        dense = tl.sb(ctx, "eu_dense", [P, 2, KEYS, SIDE])
        sums = tl.sb(ctx, "eu_sums", [P, TOPK, TOPK])
        rest = tl.sb(ctx, "eu_rest", [P, TOPK * TOPK])
        head_v = tl.sb(ctx, "eu_head_v", [P, TOPK])
        head_p = tl.sb(ctx, "eu_head_p", [P, TOPK], U32)
        small = [P, PEER_HEADS, TOPK]
        best = tl.sb(ctx, "eu_best", small)
        place = tl.sb(ctx, "eu_place", small, U32)
        digit_u = tl.sb(ctx, "eu_digit_u", [P, 2, PEER_HEADS, TOPK], U32)
        digit = tl.sb(ctx, "eu_digit", [P, 2, PEER_HEADS, TOPK])
        gap = tl.sb(ctx, "eu_gap", small)
        e = tl.sb(ctx, "eu_e", small)
        total = tl.sb(ctx, "eu_total", [P, PEER_HEADS])
        inv = tl.sb(ctx, "eu_inv", [P, PEER_HEADS])
        gate = tl.sb(ctx, "eu_gate", small)
        key = tl.sb(ctx, "eu_key", [P, 2, PEER_HEADS, TOPK])
        term = tl.sb(ctx, "eu_term", [P, 2, PEER_HEADS, TOPK])
        key_t = tl.sb(ctx, "eu_key_t", [P, 2, P])
        gate_t = tl.sb(ctx, "eu_gate_t", [P, 2, P], F32R)
        u_out = [tl.ps(ctx, f"eu_u_out{s}", [P, 2, HALF]) for s in range(2)]
        lot_out = [tl.ps(ctx, f"eu_lot_out{s}", [P, LOT, KEYS]) for s in range(2)]
        turned = tl.ps(ctx, "eu_turned", [P, 3, P])

        iota_loaded = tl.sem("eu_iota_loaded")
        u_loaded = tl.pair("eu_u_loaded")
        hi_ready = tl.pair("eu_hi_ready")
        lo_ready = tl.pair("eu_lo_ready")
        u_done = tl.pair("eu_u_done")
        gelu_ready = tl.pair("eu_gelu_ready")
        gelu_stored = tl.pair("eu_gelu_stored")
        one_ready = tl.pair("eu_one_ready")
        hot_ready = tl.pair("eu_hot_ready")
        lot_done = tl.pair("eu_lot_done")
        lot_read = tl.pair("eu_lot_read")
        dense_stored = tl.pair("eu_dense_stored")
        passed = tl.sem("eu_passed")
        sweep = tl.sem("eu_sweep")
        gap_ready = tl.sem("eu_gap_ready")
        e_ready = tl.sem("eu_e_ready")
        step = tl.sem("eu_step")
        choice_ready = tl.sem("eu_choice_ready")
        turned_ready = tl.sem("eu_turned_ready")
        turned_read = tl.sem("eu_turned_read")
        chosen = tl.sem("eu_chosen")
        block = ctx.enter_context(nc.Block())

        def tiles(engine, tile):
            tile(0, False)
            with engine.Fori(1, NT - 1) as t:
                tile(t, False)
            tile(NT - 1, True)

        def groups(engine, t, last, side, group):
            low, high = 0, GROUPS // 2
            base = t * GROUPS + side * high
            if side == 0:
                group(side, 0, base, True, False)
                low = 1
            if side == 1 and last:
                high -= 1
            with engine.Fori(low, high) as g:
                group(side, g, base + g, False, False)
            if side == 1 and last:
                group(side, high, base + high, False, True)

        @block.sync
        def _(sp):
            def load(s, n):
                sp.dma_start(u_raw[:, s, :, :], u_dram[n * 2 + s, :, :, :]).then_inc(u_loaded[s], 16)

            sp.dma_start(iota[:], iota_dram[:, :]).then_inc(iota_loaded, 16)
            for s in range(2):
                load(s, 0)

            def group(side, g, n, first, final):
                for s in range(2):
                    if not final:
                        sp.wait_ge(lo_ready[s], n + 1)
                        load(s, n + 1)

            def tile(t, last):
                for side in range(2):
                    groups(sp, t, last, side, group)
            tiles(sp, tile)

        @block.gpsimd
        def _(pool):
            def group(side, g, n, first, final):
                for s in range(2):
                    pool.wait_ge(hi_ready[s], n + 1)
                    pool.tensor_tensor(u_lo[:, s, :, :], u_raw[:, s, :, :], u_hi[:, s, :, :].bitcast(F32),
                                       ALU.subtract).then_inc(lo_ready[s], 1)

            def tile(t, last):
                for side in range(2):
                    groups(pool, t, last, side, group)
            tiles(pool, tile)

        @block.scalar
        def _(act):
            def split(s, n):
                act.wait_ge(u_loaded[s], (n + 1) * 16)
                act.copy(u_hi[:, s, :, :], u_raw[:, s, :, :]).then_inc(hi_ready[s], 1)

            def activate(s, n, final):
                act.wait_ge(u_done[s], n + 1)
                wait_for(act, gelu_stored[s], n * 16)
                act.activation(gelu[:, s, :], u_out[s][:].rearrange("p a b -> p (a b)"), ACT.Gelu) \
                    .then_inc(gelu_ready[s], 1)
                if not final:
                    split(s, n + 1)
                act.wait_ge(gelu_ready[s], n + 1)
                act.dma_start(act_dram[n * 2 + s, :, :], gelu[:, s, :]).then_inc(gelu_stored[s], 16)

            def take(side, g, n, lot):
                s = lot % 2
                act.wait_ge(lot_done[s], n * 2 + (lot // 2 + 1))
                at = g * (LOTS * LOT) + lot * LOT
                act.copy(dense[:, side, :, bass.ds(at, LOT)], lot_out[s][:].rearrange("p u b -> p b u")) \
                    .then_inc(lot_read[s], 1)

            def group(side, g, n, first, final):
                for s in range(2):
                    activate(s, n, final)
                    for lot in (2 * s, 2 * s + 1):
                        take(side, g, n, lot)

            def soften(t):
                act.wait_ge(gap_ready, t + 1)
                act.activation(e[:], gap[:], ACT.Exp).then_inc(e_ready, 1)

            def tile(t, last):
                for side in range(2):
                    wait_for(act, dense_stored[side], t * 16)
                    groups(act, t, last, side, group)
                    act.wait_ge(lot_read[1], (t * 2 + (side + 1)) * GROUPS)
                    act.wait_ge(lot_read[0], (t * 2 + (side + 1)) * GROUPS)
                    act.dma_start(gates_dram[:, :, bass.ds(t * P + side * SIDE, SIDE)].rearrange("b a t -> a b t"),
                                  dense[:, side, :, :]).then_inc(dense_stored[side], 16)
                if not last:
                    soften(t + 1)

            for s in range(2):
                split(s, 0)
            soften(0)
            tiles(act, tile)
            for s in range(2):
                act.wait_ge(dense_stored[s], NT * 16)
                act.wait_ge(gelu_stored[s], NT * GROUPS * 16)

        @block.vector
        def _(dve):
            lists = top_v[:].rearrange("p t (h c) k -> p (t h) c k", c=2)
            numbers = top_i[:].rearrange("p t (h c) k -> p t h c k", c=2)

            def choose(row, head):
                flat = sums[:].rearrange("p a b -> p (a b)")
                n = row * 6
                dve.tensor_tensor(sums[:], spread(lists[:, row, 0, :], 2, TOPK), spread(lists[:, row, 1, :], 1, TOPK),
                                  ALU.add).then_inc(sweep, 1)
                wait_apart(dve, sweep, n + 1, passed)
                dve.max(head_v[:, 0:8], flat).then_inc(sweep, 1)
                wait_apart(dve, sweep, n + 2, passed)
                dve.max_index(head_p[:, 0:8], head_v[:, 0:8], flat).then_inc(sweep, 1)
                dve.match_replace(rest[:], head_v[:, 0:8], flat, LOWEST).then_inc(sweep, 1)
                wait_apart(dve, sweep, n + 4, passed)
                dve.max(head_v[:, 8:16], rest[:]).then_inc(sweep, 1)
                wait_apart(dve, sweep, n + 5, passed)
                dve.max_index(head_p[:, 8:16], head_v[:, 8:16], rest[:]).then_inc(sweep, 1)
                dve.wait_ge(sweep, n + 6)
                dve.tensor_copy(best[:, head, :], head_v[:])
                dve.tensor_copy(place[:, head, :], head_p[:]).then_inc(chosen, 1)

            STEPS = 5 + 2 * TOPK - 1

            def settle(t):
                n = [0]

                def done(q):
                    n[0] += 1
                    q.then_inc(step, 1)
                    dve.wait_ge(step, t * STEPS + n[0])

                dve.wait_ge(chosen, (t + 1) * PEER_HEADS)
                dve.tensor_tensor(gap[:], best[:], best[:, :, 0:1].broadcast_to(small), ALU.subtract) \
                    .then_inc(gap_ready, 1)
                dve.tensor_scalar(digit_u[:, 0, :, :], place[:], 4, None, ALU.logical_shift_right)
                done(dve.tensor_scalar(digit_u[:, 1, :, :], place[:], TOPK - 1, None, ALU.bitwise_and))
                done(dve.tensor_copy(digit[:], digit_u[:]))
                for a in range(TOPK):
                    for c in range(2):
                        q = dve.scalar_tensor_tensor(out=(term if a else key)[:, c, :, :], in0=digit[:, c, :, :],
                                                     scalar=float(a), in1=spread(numbers[:, t, :, c, a], 2, TOPK),
                                                     op0=ALU.is_equal, op1=ALU.mult)
                    done(q)
                    if a:
                        done(dve.tensor_tensor(key[:], key[:], term[:], ALU.add))
                dve.wait_ge(e_ready, t + 1)
                done(dve.tensor_reduce(total[:], e[:], AX.X, ALU.add))
                done(dve.reciprocal(inv[:], total[:]))
                done(dve.tensor_tensor(gate[:], e[:], spread(inv[:], 2, TOPK), ALU.mult))
                dve.tensor_copy(total[:, 0:1], inv[:, 0:1]).then_inc(choice_ready, 1)
                assert n[0] == STEPS

            def untangle(t):
                dve.wait_ge(turned_ready, t + 1)
                dve.tensor_copy(key_t[:], turned[:, 0:2, :])
                dve.tensor_copy(gate_t[:, 0, :], turned[:, 2, :]).then_inc(turned_read, 1)
                dve.wait_ge(turned_read, t * 2 + 1)
                dve.tensor_tensor(gate_t[:, 1, :], turned[:, 2, :], gate_t[:, 0, :].bitcast(F32), ALU.subtract) \
                    .then_inc(turned_read, 1)
                dve.wait_ge(turned_read, t * 2 + 2)

            def build(side, g, n, lot):
                s = lot % 2
                at = g * (LOTS * LOT) + (side * SIDE + lot * LOT)
                wait_for(dve, lot_done[s], n * 2 + lot // 2)
                dve.tensor_tensor(hot[:, s, :, :, :], spread(spread(iota[:], 1, LOT), 1, 2),
                                  spread(key_t[:, :, bass.ds(at, LOT)], 3, KEYS), ALU.is_equal) \
                    .then_inc(one_ready[s], 1)
                dve.wait_ge(one_ready[s], n * 2 + (lot // 2 + 1))
                dve.tensor_tensor(hot_gate[:, s, :, :, :], spread(hot[:, s, 1, :, :].bitcast(F32), 1, 2),
                                  spread(gate_t[:, :, bass.ds(at, LOT)].bitcast(F32), 3, KEYS), ALU.mult) \
                    .then_inc(hot_ready[s], 1)

            def tile(t, last):
                def group(side, g, n, first, final):
                    if first:
                        untangle(t)
                    build(side, g, n, 0)
                    build(side, g, n, 1)
                    if not last:
                        choose(n + PEER_HEADS, side * 4 + g)
                    build(side, g, n, 2)
                    build(side, g, n, 3)

                for side in range(2):
                    groups(dve, t, last, side, group)
                if not last:
                    settle(t + 1)

            with dve.Fori(0, PEER_HEADS) as head:
                choose(head, head)
            settle(0)
            dve.wait_ge(iota_loaded, 16)
            tiles(dve, tile)

        @block.tensor
        def _(pe):
            def chunk(s, n):
                pe.wait_ge(lo_ready[s], n + 1)
                wait_for(pe, gelu_ready[s], n)
                for half in range(2):
                    tokens = slice(half * HALF, (half + 1) * HALF)
                    q = three_passes(pe, u_out[s][:, half, :], lambda k: u_hi[:, s, k, :], lambda k: u_lo[:, s, k, :],
                                     lambda k: xn_hi[:, k, tokens], lambda k: xn_lo[:, k, tokens], DC)
                q.then_inc(u_done[s], 1)

            def turn(t):
                pe.wait_ge(choice_ready, t + 1)
                wait_for(pe, turned_read, t * 2)
                for j in range(3):
                    rows = gate[:] if j == 2 else key[:, j, :, :]
                    q = pe.transpose(turned[:, j, :], rows.rearrange("p h k -> p (h k)"), ident[:])
                q.then_inc(turned_ready, 1)

            def scatter(n, lot):
                s = lot % 2
                pe.wait_ge(hot_ready[s], n * 2 + (lot // 2 + 1))
                wait_for(pe, lot_read[s], n * 2 + lot // 2)
                for u in range(LOT):
                    pe.matmul(lot_out[s][:, u, :], hot[:, s, 0, u, :], hot_gate[:, s, 0, u, :], start=True, stop=False)
                    q = pe.matmul(lot_out[s][:, u, :], hot[:, s, 0, u, :], hot_gate[:, s, 1, u, :], start=False,
                                  stop=True)
                q.then_inc(lot_done[s], 1)

            def tile(t, last):
                def group(side, g, n, first, final):
                    for s in range(2):
                        chunk(s, n)
                        if first and s == 0:
                            turn(t)
                        scatter(n, 2 * s)
                        scatter(n, 2 * s + 1)

                for side in range(2):
                    groups(pe, t, last, side, group)
            tiles(pe, tile)


def expert_down(nc, tl, v_dram, act_dram, gates_dram, h, h_dram):
    with ExitStack() as ctx:
        SLOTS = 4
        TILES = HALF // P
        v_raw = tl.sb(ctx, "ed_v_raw", [P, SLOTS, D])
        act_in = tl.sb(ctx, "ed_act_in", [P, SLOTS, HALF])
        gate_in = tl.sb(ctx, "ed_gate_in", [P, SLOTS, HALF])
        v_hi = tl.sb(ctx, "ed_v_hi", [P, SLOTS, D], F32R)
        v_lo = tl.sb(ctx, "ed_v_lo", [P, SLOTS, D], F32R)
        coef = tl.sb(ctx, "ed_coef", [P, SLOTS, HALF])
        c_hi = tl.sb(ctx, "ed_c_hi", [P, SLOTS, HALF], F32R)
        c_lo = tl.sb(ctx, "ed_c_lo", [P, SLOTS, HALF], F32R)
        zero = tl.sb(ctx, "ed_zero", [P, HALF], BF16)
        y = tl.ps(ctx, "ed_y", [P, TILES, 2, HALF])
        slots = range(SLOTS)
        v_loaded = [tl.sem(f"ed_v_loaded{s}") for s in slots]
        a_loaded = [tl.sem(f"ed_a_loaded{s}") for s in slots]
        coef_ready = [tl.sem(f"ed_coef_ready{s}") for s in slots]
        hi_ready = [tl.sem(f"ed_hi_ready{s}") for s in slots]
        split = [tl.sem(f"ed_split{s}") for s in slots]
        used = [tl.sem(f"ed_used{s}") for s in slots]
        zeroed = tl.sem("ed_zeroed")
        h_loaded = tl.sem("ed_h_loaded")
        summed = tl.sem("ed_summed")
        added = tl.sem("ed_added")
        block = ctx.enter_context(nc.Block())
        ROUNDS = KEYS // SLOTS
        v_chunks = v_dram.rearrange("(a b) d -> b a d", b=KEYS)

        @block.sync
        def _(sp):
            sp.dma_start(h[:], h_dram.rearrange("(t p) d -> p t d", p=P)).then_inc(h_loaded, 16)
            for half in range(2):
                tokens = slice(half * HALF, (half + 1) * HALF)
                with sp.Fori(0, ROUNDS) as i:
                    for s in slots:
                        b = i * SLOTS + s
                        sp.wait_ge(split[s], i + half * ROUNDS + FREE)
                        sp.dma_start(v_raw[:, s, :], v_chunks[b, :, :]).then_inc(v_loaded[s], 16)
                        sp.dma_start(act_in[:, s, :], act_dram[b, :, tokens]).then_inc(a_loaded[s], 16)
                        sp.dma_start(gate_in[:, s, :], gates_dram[b, :, tokens]).then_inc(a_loaded[s], 16)

        @block.vector
        def _(dve):
            for s in slots:
                dve.sem_inc(split[s], FREE)
            dve.sem_inc(added, FREE)
            dve.memset(zero[:], 0.0).then_inc(zeroed, 1)
            for half in range(2):
                with dve.Fori(0, ROUNDS) as i:
                    r = i + half * ROUNDS
                    for s in slots:
                        dve.wait_ge(a_loaded[s], (r + 1) * 32)
                        dve.tensor_tensor(coef[:, s, :], act_in[:, s, :], gate_in[:, s, :], ALU.mult) \
                            .then_inc(coef_ready[s], 1)
                        dve.wait_ge(hi_ready[s], (r + 1) * 2)
                        dve.tensor_tensor(v_lo[:, s, :], v_raw[:, s, :], v_hi[:, s, :].bitcast(F32), ALU.subtract)
                        dve.tensor_tensor(c_lo[:, s, :], coef[:, s, :], c_hi[:, s, :].bitcast(F32),
                                          ALU.subtract).then_inc(split[s], 1)
                dve.wait_ge(summed, half + 1)
                dve.wait_ge(h_loaded, 16)
                for t in range(TILES):
                    rows = h[:, half * TILES + t, :]
                    q = dve.tensor_tensor(rows, rows, y[:, t, :, :].rearrange("p a b -> p (a b)"), ALU.add)
                q.then_inc(added, 1)

        @block.scalar
        def _(act):
            for half in range(2):
                with act.Fori(0, ROUNDS) as i:
                    r = i + half * ROUNDS
                    for s in slots:
                        act.wait_ge(used[s], r + FREE)
                        act.wait_ge(v_loaded[s], (r + 1) * 16)
                        act.copy(v_hi[:, s, :], v_raw[:, s, :]).then_inc(hi_ready[s], 1)
                        act.wait_ge(coef_ready[s], r + 1)
                        act.copy(c_hi[:, s, :], coef[:, s, :]).then_inc(hi_ready[s], 1)

        @block.tensor
        def _(pe):
            for s in slots:
                pe.sem_inc(used[s], FREE)
            pe.wait_ge(zeroed, 1)

            def zeros(start):
                for t in range(TILES):
                    for n in range(2):
                        q = pe.matmul(y[:, t, n, :], zero[:, 0:P], zero[:], start=start, stop=not start)
                return q

            for half in range(2):
                pe.wait_ge(added, half + FREE)
                zeros(True)
                with pe.Fori(0, ROUNDS) as i:
                    r = i + half * ROUNDS
                    for s in slots:
                        pe.wait_ge(split[s], r + 1 + FREE)
                        for t in range(TILES):
                            rows = slice(t * P, (t + 1) * P)
                            for lhs, rhs in ((c_hi, v_hi), (c_hi, v_lo), (c_lo, v_hi)):
                                for n in range(2):
                                    q = pe.matmul(y[:, t, n, :], lhs[:, s, rows],
                                                  rhs[:, s, n * HALF:(n + 1) * HALF], start=False, stop=False)
                        q.then_inc(used[s], 1)
                zeros(False).then_inc(summed, 1)


def layer_input(nc, tl, w_dram, pt_dram, pt, pw):
    loaded = tl.sem("li_loaded")
    with nc.Block() as block:
        @block.sync
        def _(sp):
            sp.dma_start(pt[:], pt_dram.rearrange("(k p) t -> p k t", p=P)).then_inc(loaded, 16)
            sp.dma_start(pw[:], w_dram.rearrange("(k p) d -> p k d", p=P)).then_inc(loaded, 16)
            sp.wait_ge(loaded, 32)


def ple_projection(nc, tl, pt, pw, proj):
    KP = 2
    with ExitStack() as ctx:
        out = [tl.ps(ctx, f"pp_out{s}", [P, 2, HALF]) for s in range(2)]
        ready = tl.sem("pp_ready")
        read = tl.sem("pp_read")
        block = ctx.enter_context(nc.Block())

        @block.tensor
        def _(pe):
            for t in range(NT):
                if t >= 2:
                    pe.wait_ge(read, t - 1)
                for n in range(2):
                    for k in range(KP):
                        q = pe.matmul(out[t % 2][:, n, :], pt[:, k, t * P:(t + 1) * P],
                                      pw[:, k, n * HALF:(n + 1) * HALF], start=(k == 0), stop=(k == KP - 1))
                q.then_inc(ready, 1)

        @block.scalar
        def _(act):
            for t in range(NT):
                act.wait_ge(ready, t + 1)
                act.copy(proj[:, t, :], out[t % 2][:].rearrange("p a b -> p (a b)")).then_inc(read, 1)


def final_norm(nc, tl, h, gate_logit, proj, eps, gain_dram, out_dram):
    with ExitStack() as ctx:
        gain = tl.sb(ctx, "fn_gain", [P, D])
        square = tl.sb(ctx, "fn_square", [P, D])
        ssq = tl.sb(ctx, "fn_ssq", [P, NT])
        root = tl.sb(ctx, "fn_root", [P, NT])
        rstd = tl.sb(ctx, "fn_rstd", [P, NT])
        gain_loaded = tl.sem("fn_gain_loaded")
        gate_ready = tl.sem("fn_gate_ready")
        part_ready = tl.sem("fn_part_ready")
        h_ready = tl.sem("fn_h_ready")
        squared = tl.sem("fn_squared")
        root_ready = tl.sem("fn_root_ready")
        rstd_ready = tl.sem("fn_rstd_ready")
        row_ready = tl.sem("fn_row_ready")
        stored = tl.sem("fn_stored")
        block = ctx.enter_context(nc.Block())

        @block.scalar
        def _(act):
            for t in range(NT):
                act.activation(gate_logit[:, t, :], gate_logit[:, t, :], ACT.Sigmoid).then_inc(gate_ready, 1)
            for t in range(NT):
                act.wait_ge(h_ready, t + 1)
                if t:
                    act.wait_ge(squared, t)
                act.activation(square[:], h[:, t, :], ACT.Square, accum_out=ssq[:, t:t + 1]).then_inc(squared, 1)
            act.wait_ge(squared, NT)
            act.activation(root[:], ssq[:], ACT.Sqrt, scale=1.0 / D, bias=eps[:, 0:1]).then_inc(root_ready, 1)

        @block.vector
        def _(dve):
            for t in range(NT):
                dve.wait_ge(gate_ready, t + 1)
                dve.tensor_tensor(proj[:, t, :], gate_logit[:, t, :], proj[:, t, :], ALU.mult).then_inc(part_ready, 1)
                dve.wait_ge(part_ready, t + 1)
                dve.tensor_tensor(h[:, t, :], h[:, t, :], proj[:, t, :], ALU.add).then_inc(h_ready, 1)
            dve.wait_ge(root_ready, 1)
            dve.reciprocal(rstd[:], root[:]).then_inc(rstd_ready, 1)
            dve.wait_ge(rstd_ready, 1)
            dve.wait_ge(gain_loaded, 16)
            for t in range(NT):
                dve.scalar_tensor_tensor(out=h[:, t, :], in0=h[:, t, :], scalar=rstd[:, t:t + 1], in1=gain[:],
                                         op0=ALU.mult, op1=ALU.mult).then_inc(row_ready, 1)

        @block.sync
        def _(sp):
            sp.dma_start(gain[:], gain_dram.partition_broadcast(P)).then_inc(gain_loaded, 16)
            for t in range(NT):
                sp.wait_ge(row_ready, t + 1)
                sp.dma_start(out_dram[t * P:(t + 1) * P, :], h[:, t, :]).then_inc(stored, 16)
            sp.wait_ge(stored, 16 * NT)


def program(nc, d, out):
    with ExitStack() as top:
        tl = Tools(nc)
        whole = ExitStack()
        top.enter_context(whole)
        ident = tl.sb(whole, "ident", [P, P])
        gains = tl.sb(whole, "gains", [P, 4, DC])
        eps = tl.sb(whole, "eps", [P, 1])
        const_loaded = tl.sem("const_loaded")
        eps_ready = tl.sem("eps_ready")
        with nc.Block() as block:
            @block.sync
            def _(sp):
                sp.dma_start(ident[:], d["ident"][:, :]).then_inc(const_loaded, 16)
                sp.dma_start(gains[:], d["gains"][:, :, :]).then_inc(const_loaded, 16)
                sp.wait_ge(const_loaded, 32)

            @block.gpsimd
            def _(pool):
                pool.memset(eps[:], EPS).then_inc(eps_ready, 1)

        residual = top.enter_context(ExitStack())
        h = tl.sb(residual, "h", [P, NT, D])

        def gain(n):
            return {"t": gains[:, n, :], "eps": eps}

        att = ExitStack()
        v = tl.sb(att, "v", [P, NT, V_COLS])
        masks = tl.sb(att, "masks", [P, 2 * P], BF16)
        ident16 = tl.sb(att, "ident16", [P, P], BF16)
        perm = tl.sb(att, "perm", [P, P])
        key_rows = tl.sb(att, "key_rows", [4 * FOX_HEADS, T], F32R)
        query_rows = tl.sb(att, "query_rows", [4 * FOX_HEADS, T], F32R)
        head_pick = tl.sb(att, "head_pick", [4 * FOX_HEADS, FOX_HEADS])
        sinks = {"value": tl.sb(att, "sink_value", [P, PAIRS, 2]),
                 "neg_unscaled": tl.sb(att, "sink_neg_unscaled", [P, PAIRS, 2]),
                 "bias": tl.sb(att, "sink_bias", [P, 4]), "bias_ready": tl.sem("sink_bias_ready")}
        att_qk = ExitStack()
        acts = ExitStack()
        xt_hi = tl.sb(acts, "xt_hi", [P, DC, T], F32R, "right")
        xt_lo = tl.sb(acts, "xt_lo", [P, DC, T], F32R, "right")

        def keep_v(dve, s, t, o):
            return dve.tensor_copy(v[:, t, :].rearrange("p (n w) -> p n w", n=2), o[:, :, 0:V_PART])

        token_pass(nc, tl, "mix", h, d["x"], 1, gain(0), ident, (2, V_PART), d["w_v"], (xt_hi, xt_lo), keep_v)
        qk = tl.sb(att_qk, "qk", [P, QK_CHUNKS, T])
        feature_proj(nc, tl, d["w_qk"], xt_hi, xt_lo, qk)
        acts.close()
        with ExitStack() as ctx:
            mask_raw = tl.sb(ctx, "mask_raw", [P, 2 * P])
            loaded = tl.sem("small_loaded")
            block = ctx.enter_context(nc.Block())

            @block.sync
            def _(sp):
                sp.dma_start(mask_raw[:], d["masks"][:, :]).then_inc(loaded, 16)
                sp.dma_start(perm[:], d["perm"][:, :]).then_inc(loaded, 16)
                sp.dma_start(head_pick[:], d["head_pick"][:, :]).then_inc(loaded, 16)
                sp.dma_start(sinks["value"][:], d["sinks"].partition_broadcast(P)).then_inc(loaded, 16)

            @block.vector
            def _(dve):
                dve.wait_ge(loaded, 64)
                dve.tensor_copy(masks[:], mask_raw[:])
                dve.tensor_copy(ident16[:], ident[:])
                dve.tensor_scalar(sinks["neg_unscaled"][:], sinks["value"][:], -1.0 / SCALE, None, ALU.mult)
        rotate(nc, tl, qk, perm, d["cos"], d["sin"])
        decay(nc, tl, v, d["b_forget"], d["tri"], key_rows, query_rows)
        mixing = ExitStack()
        mixed = tl.sb(mixing, "mixed", [P, NT, D], F32, "right")
        attention(nc, tl, qk, v, key_rows, query_rows, sinks, masks, head_pick, ident, ident16, mixed)
        att_qk.close()
        att.close()

        def add_out(dve, s, t, o):
            return dve.tensor_tensor(h[:, t, :], h[:, t, :], o[:].rearrange("p n w -> p (n w)"), ALU.add)

        token_pass(nc, tl, "out", mixed, None, 2, gain(1), ident, (2, HALF), d["w_out"], None, add_out)
        mixing.close()
        tl.recycle()
        experts = ExitStack()
        xn_hi = tl.sb(experts, "xn_hi", [P, DC, T], F32R, "right")
        xn_lo = tl.sb(experts, "xn_lo", [P, DC, T], F32R, "right")
        h_dram = nc.dram_tensor("residual", (T, D), F32, kind="Internal").ap()
        gates_dram = nc.dram_tensor("gates", (KEYS, KEYS, T), F32, kind="Internal").ap()
        act_dram = nc.dram_tensor("activations", (KEYS, KEYS, T), F32, kind="Internal").ap()
        token_pass(nc, tl, "ffn", h, None, 1, gain(2), ident, None, None, (xn_hi, xn_lo), None, h_dram)
        residual.close()
        lists = ExitStack()
        top_v = tl.sb(lists, "top_v", [P, NT, HC, TOPK])
        top_i = tl.sb(lists, "top_i", [P, NT, HC, TOPK], BF16)
        peer_scores(nc, tl, d["w_query"], d["sub_keys"], xn_hi, xn_lo, top_v, top_i)
        tl.recycle()
        experts_up(nc, tl, d["expert_u"], d["iota"], xn_hi, xn_lo, top_v, top_i, ident, act_dram, gates_dram)
        lists.close()
        experts.close()
        h = tl.sb(residual, "h_again", [P, NT, D])
        expert_down(nc, tl, d["expert_v"], act_dram, gates_dram, h, h_dram)
        last = ExitStack()
        logit = tl.sb(last, "logit", [P, NT, D])

        def keep_logit(dve, s, t, o):
            return dve.tensor_copy(logit[:, t, :], o[:].rearrange("p n w -> p (n w)"))

        token_pass(nc, tl, "ple", h, None, 1, gain(3), ident, (2, HALF), d["w_ple_gate"], None, keep_logit)
        proj = tl.sb(last, "proj", [P, NT, D])
        pt = tl.sb(last, "pt", [P, 2, T])
        pw = tl.sb(last, "pw", [P, 2, D])
        layer_input(nc, tl, d["w_ple_proj"], d["p_t"], pt, pw)
        ple_projection(nc, tl, pt, pw, proj)
        final_norm(nc, tl, h, logit, proj, eps, d["norm_final_g"], out)
        last.close()
        residual.close()



def layouts(i):
    def contiguous(a):
        return np.ascontiguousarray(a)

    w_in = np.asarray(i["w_in"])[0]
    swa_k0 = SWA_HEADS * HEAD
    swa_v0 = swa_k0 + SWA_KV * HEAD
    fox_q0 = swa_v0 + SWA_KV * HEAD
    fox_k0 = fox_q0 + FOX_HEADS * HEAD
    fox_v0 = fox_k0 + FOX_HEADS * HEAD
    forget0 = fox_v0 + FOX_HEADS * HEAD
    cols = []
    for c in range(PAIRS):
        for head in (c, c + SWA_HEADS // SWA_KV):
            cols += range(head * HEAD, (head + 1) * HEAD)
    cols += range(swa_k0, swa_v0)
    cols += range(fox_q0, fox_v0)
    v_cols = list(range(swa_v0, fox_q0)) + list(range(fox_v0, forget0 + FOX_HEADS))

    def chunked(w):
        return contiguous(w.reshape(DC, P, -1, P).transpose(2, 1, 0, 3))

    gains = [i["norm_mix_g"][0], np.concatenate([i["g_out_a"][0], i["g_out_b"][0]]), i["norm_ffn_g"][0],
             i["norm_ple_g"][0]]
    return {
        "x": contiguous(i["x"][0]),
        "gains": contiguous(np.stack([np.asarray(g).reshape(DC, P).T for g in gains], 1)),
        "w_v": contiguous(w_in[:, v_cols].reshape(DC, P, V_COLS)),
        "w_qk": chunked(w_in[:, cols]),
        "b_forget": contiguous(i["b_forget"][0]),
        "sinks": contiguous(np.asarray(i["sinks"])[0].reshape(2, PAIRS).T),
        "expert_u": contiguous(np.asarray(i["expert_u"])[0].reshape(KEYS, KEYS, DC, P).transpose(1, 3, 2, 0)),
        "expert_v": contiguous(np.asarray(i["expert_v"])[0]),
        "w_query": chunked(np.asarray(i["w_query"])[0]),
        "sub_keys": contiguous(np.asarray(i["sub_keys"])[0].transpose(0, 2, 1)),
        "w_ple_gate": contiguous(np.asarray(i["w_ple_gate"])[0].reshape(DC, P, D)),
        "w_ple_proj": contiguous(np.asarray(i["w_ple_proj"])[0]),
        "p_t": contiguous(np.asarray(i["p"])[0, 0].T),
        "norm_final_g": contiguous(i["norm_final_g"]),
        "w_out": contiguous(np.asarray(i["w_out"])[0].reshape(DC, P, D)),
    }


def constants():
    pos = np.arange(T, dtype=np.float32)
    freq = (np.float32(10000.0) ** (-np.arange(0, HEAD, 2, dtype=np.float32) / np.float32(HEAD))).astype(np.float32)
    ang = (pos[:, None] * freq[None, :]).astype(np.float32)
    feature = np.arange(P)
    cos = np.cos(ang).astype(np.float32).T[feature % (HEAD // 2)]
    sin = np.sin(ang).astype(np.float32).T[feature % (HEAD // 2)]
    first = (feature % HEAD) < HEAD // 2
    sin = np.where(first[:, None], -sin, sin).astype(np.float32)
    partner = np.where(first, feature + HEAD // 2, feature - HEAD // 2)
    perm = np.zeros((P, P), np.float32)
    perm[partner, feature] = 1.0
    q, k = np.arange(P)[:, None], np.arange(P)[None, :]
    masks = np.concatenate([np.where(k > q, 0.0, NEG), np.where(k <= q, 0.0, NEG)], 1).astype(np.float32)
    row = np.arange(4 * FOX_HEADS)
    return {
        "ident": np.eye(P, dtype=np.float32),
        "masks": masks,
        "iota": np.tile(np.arange(KEYS, dtype=np.float32), (P, 1)),
        "perm": perm,
        "head_pick": (row[:, None] % FOX_HEADS == np.arange(FOX_HEADS)[None, :]).astype(np.float32),
        "cos": np.ascontiguousarray(cos),
        "sin": np.ascontiguousarray(sin),
        "tri": (np.arange(P)[:, None] <= np.arange(-(T - P), T)[None, :]).astype(np.float32),
    }


def kernel(**inputs):
    import concourse.bacc as _bacc
    from concourse.bass_utils import run_bass_kernel_spmd as _run

    nc = _bacc.Bacc("TRN2", target_bir_lowering=False, num_devices=1)
    arrays = {**layouts({n: np.asarray(a) for n, a in inputs.items()}), **constants()}
    dram = {n: nc.dram_tensor(f"in_{n}", a.shape, mybir.dt.from_np(a.dtype), kind="ExternalInput").ap()
            for n, a in arrays.items()}
    out = nc.dram_tensor("out", (T, D), F32, kind="ExternalOutput").ap()
    program(nc, dram, out)
    r = _run(nc, [{f"in_{n}": a for n, a in arrays.items()}], core_ids=[0])
    return r.results[0]["out"].reshape(1, T, D)
```

```python
from contextlib import ExitStack

import numpy as np

import concourse.bass as bass
from concourse import mybir

F32 = mybir.dt.float32
F32R = mybir.dt.float32r
BF16 = mybir.dt.bfloat16
U32 = mybir.dt.uint32
ACT = mybir.ActivationFunctionType
ALU = mybir.AluOpType
AX = mybir.AxisListType

P = 128
T = 1024
NT = T // P
D = 1024
DC = D // P
HALF = 512
HEAD = 64
SWA_HEADS, SWA_KV, FOX_HEADS = 8, 2, 8
PAIRS = 4
SWA_Q, SWA_K, FOX_Q, FOX_K = 0, 4, 5, 9
QK_CHUNKS = 13
V_COLS = SWA_KV * HEAD + FOX_HEADS * HEAD + FOX_HEADS
V_FOX = SWA_KV * HEAD
V_FORGET = V_FOX + FOX_HEADS * HEAD
V_PART = V_COLS // 2
PEER_HEADS, KEYS, TOPK = 8, 128, 16
HC = 2 * PEER_HEADS
SEL = PEER_HEADS * TOPK
EPS = 1e-6
NEG = -1e30
LOWEST = -3.4e38
FREE = 1
SCALE = HEAD ** -0.5


def spread(ap, at, n):
    shape = list(ap.shape)
    return ap.unsqueeze(at).broadcast_to(shape[:at] + [n] + shape[at:])


class Tools:

    def __init__(self, nc):
        self.nc, self.held = nc, []

    def sem(self, name):
        self.held.append(self.nc.alloc_semaphore(name=name))
        return self.held[-1]

    def recycle(self):
        self.nc.clear_and_free_semaphores(self.held)
        self.nc.all_engine_barrier()
        self.held = []

    def pair(self, name):
        return [self.sem(f"{name}{s}") for s in range(2)]

    def sb(self, ctx, name, shape, dt=F32, side="left"):
        return ctx.enter_context(self.nc.sbuf_tensor(name, shape, dt, side=side))

    def ps(self, ctx, name, shape, dt=F32):
        return ctx.enter_context(self.nc.psum_tensor(name, shape, dt))


def three_passes(pe, out, lhs_hi, lhs_lo, rhs_hi, rhs_lo, n, chunk_ready=None):
    for k in range(n):
        if chunk_ready is not None:
            pe.wait_ge(chunk_ready, k + 1)
        pe.matmul(out, lhs_hi(k), rhs_hi(k), start=(k == 0), stop=False)
        pe.matmul(out, lhs_hi(k), rhs_lo(k), start=False, stop=False)
        mm = pe.matmul(out, lhs_lo(k), rhs_hi(k), start=False, stop=(k == n - 1))
    return mm


def token_pass(nc, tl, name, src, src_dram, groups, gain, ident, parts, weights, keep, epilogue,
               save=None):
    with ExitStack() as ctx:
        width = parts[1] if parts else 0
        n_parts = parts[0] if parts else 0
        square = tl.sb(ctx, f"{name}_square", [P, D])
        ssq = tl.sb(ctx, f"{name}_ssq", [P, NT, groups])
        root = tl.sb(ctx, f"{name}_root", [P, NT, groups])
        rstd = tl.sb(ctx, f"{name}_rstd", [P, NT, groups])
        scaled = tl.sb(ctx, f"{name}_scaled", [P, 2, D])
        act_hi = tl.sb(ctx, f"{name}_act_hi", [P, 2, DC, P], F32R)
        act_lo = tl.sb(ctx, f"{name}_act_lo", [P, 2, DC, P], F32R)
        turned = [tl.ps(ctx, f"{name}_turned{s}", [P, DC, P]) for s in range(2)]
        if weights is not None:
            w_raw = tl.sb(ctx, f"{name}_w_raw", [P, 2, n_parts * width])
            w_hi = tl.sb(ctx, f"{name}_w_hi", [P, DC, n_parts * width], F32R)
            w_lo = tl.sb(ctx, f"{name}_w_lo", [P, DC, n_parts * width], F32R)
            out = [tl.ps(ctx, f"{name}_out{s}", [P, n_parts, HALF]) for s in range(2)]
        src_loaded = [tl.sem(f"{name}_src_loaded{t}") for t in range(NT)] if src_dram is not None else None
        saved = tl.sem(f"{name}_saved")
        w_loaded = tl.pair(f"{name}_w_loaded")
        w_hi_ready = tl.sem(f"{name}_w_hi_ready")
        w_ready = tl.sem(f"{name}_w_ready")
        squared = tl.sem(f"{name}_squared")
        rooted = tl.sem(f"{name}_rooted")
        rstd_ready = tl.sem(f"{name}_rstd_ready")
        scaled_ready = tl.pair(f"{name}_scaled_ready")
        turned_ready = tl.pair(f"{name}_turned_ready")
        hi_ready = tl.pair(f"{name}_hi_ready")
        lo_ready = tl.pair(f"{name}_lo_ready")
        kept = tl.pair(f"{name}_kept")
        out_ready = tl.pair(f"{name}_out_ready")
        out_read = tl.pair(f"{name}_out_read")
        block = ctx.enter_context(nc.Block())
        gw = D // groups
        LOOPS = NT // 2
        direct = weights is None

        def hi_at(s, t, k):
            return keep[0][:, k, bass.ts(t, P)] if direct else act_hi[:, s, k, :]

        def lo_at(s, t, k):
            return keep[1][:, k, bass.ts(t, P)] if direct else act_lo[:, s, k, :]

        @block.sync
        def _(sp):
            if save is not None:
                sp.dma_start(save.rearrange("(t p) d -> p t d", p=P), src[:]).then_inc(saved, 16)
            if src_dram is not None:
                for t in range(NT):
                    sp.dma_start(src[:, t, :], src_dram[t * P:(t + 1) * P, :]).then_inc(src_loaded[t], 16)
                    if t < 2:
                        sp.dma_start(w_raw[:, t, :], weights[t, :, :]).then_inc(w_loaded[t], 16)
            if weights is not None:
                for k in range(0 if src_dram is None else 2, DC):
                    if k >= 2:
                        sp.wait_ge(w_ready, k - 1)
                    sp.dma_start(w_raw[:, k % 2, :], weights[k, :, :]).then_inc(w_loaded[k % 2], 16)
            if save is not None:
                sp.wait_ge(saved, 16)

        @block.scalar
        def _(act):
            def squares(tiles):
                for t in tiles:
                    if src_dram is not None:
                        act.wait_ge(src_loaded[t], 16)
                    for g in range(groups):
                        q = act.activation(square[:, 0:gw], src[:, t, g * gw:(g + 1) * gw], ACT.Square,
                                           accum_out=ssq[:, t, g:g + 1])
                        q.then_inc(squared, 1)
                        act.wait_ge(squared, t * groups + g + 1)
                now = slice(tiles[0], tiles[-1] + 1)
                act.activation(root[:, now, :], ssq[:, now, :], ACT.Sqrt, scale=1.0 / gw,
                               bias=gain["eps"][:, 0:1]).then_inc(rooted, 1)

            def hi(s, i):
                act.wait_ge(turned_ready[s], i + 1)
                if keep is not None and not direct:
                    act.wait_ge(kept[s], i + FREE)
                for k in range(DC):
                    q = act.mul(hi_at(s, i * 2 + s, k), turned[s][:, k, :], gain["t"][:, k:k + 1])
                q.then_inc(hi_ready[s], 1)

            squares(range(2))
            for s in range(2):
                hi(s, 0)
            squares(range(2, NT))
            with act.Fori(1, LOOPS) as i:
                for s in range(2):
                    hi(s, i)

        @block.vector
        def _(dve):
            def scale(s, i):
                t = i * 2 + s
                for g in range(groups):
                    q = dve.tensor_scalar(scaled[:, s, g * gw:(g + 1) * gw], src[:, t, g * gw:(g + 1) * gw],
                                          rstd[:, t, g:g + 1], None, ALU.mult)
                q.then_inc(scaled_ready[s], 1)

            def split(s, i):
                dve.wait_ge(hi_ready[s], i + 1)
                for k in range(DC):
                    q = dve.scalar_tensor_tensor(out=lo_at(s, i * 2 + s, k), in0=turned[s][:, k, :],
                                                 scalar=gain["t"][:, k:k + 1],
                                                 in1=hi_at(s, i * 2 + s, k).bitcast(F32),
                                                 op0=ALU.mult, op1=ALU.subtract)
                q.then_inc(lo_ready[s], 1)

            def split_weights(chunks):
                for k in chunks:
                    dve.wait_ge(w_loaded[k % 2], 16 * (k // 2 + 1))
                    dve.tensor_copy(w_hi[:, k, :], w_raw[:, k % 2, :]).then_inc(w_hi_ready, 1)
                    dve.wait_ge(w_hi_ready, k + 1)
                    dve.tensor_tensor(w_lo[:, k, :], w_raw[:, k % 2, :], w_hi[:, k, :].bitcast(F32),
                                      ALU.subtract).then_inc(w_ready, 1)

            def empty(s, i):
                dve.wait_ge(out_ready[s], i + 1)
                epilogue(dve, s, i * 2 + s, out[s]).then_inc(out_read[s], 1)

            for s in range(2):
                dve.sem_inc(lo_ready[s], FREE)
                dve.sem_inc(out_read[s], FREE)
            def invert(tiles, n):
                dve.wait_ge(rooted, n)
                now = slice(tiles[0], tiles[-1] + 1)
                dve.reciprocal(rstd[:, now, :], root[:, now, :]).then_inc(rstd_ready, 1)
                dve.wait_ge(rstd_ready, n)

            if weights is not None:
                split_weights(range(2))
            invert(range(2), 1)
            for s in range(2):
                scale(s, 0)
            if weights is not None:
                split_weights(range(2, 4))
            for s in range(2):
                split(s, 0)
            if weights is not None:
                split_weights(range(4, DC))
            invert(range(2, NT), 2)
            with dve.Fori(0, LOOPS - 1) as i:
                if direct:
                    for s in range(2):
                        dve.wait_ge(turned_ready[s], i + 1)
                        scale(s, i + 1)
                    for s in range(2):
                        split(s, i + 1)
                else:
                    for s in range(2):
                        dve.wait_ge(turned_ready[s], i + 1)
                        scale(s, i + 1)
                        empty(s, i)
                        split(s, i + 1)
            if weights is not None:
                for s in range(2):
                    empty(s, LOOPS - 1)

        @block.tensor
        def _(pe):
            def turn(s, i):
                pe.wait_ge(scaled_ready[s], i + 1)
                pe.wait_ge(lo_ready[s], i + FREE)
                for k in range(DC):
                    q = pe.transpose(turned[s][:, k, :], scaled[:, s, k * P:(k + 1) * P], ident[:])
                q.then_inc(turned_ready[s], 1)

            def multiply(s, i, chunk_ready=None):
                if weights is None:
                    return
                pe.wait_ge(lo_ready[s], i + 1 + FREE)
                pe.wait_ge(out_read[s], i + FREE)
                for n in range(n_parts):
                    q = three_passes(pe, out[s][:, n, 0:width],
                                     lambda k: act_hi[:, s, k, :], lambda k: act_lo[:, s, k, :],
                                     lambda k: w_hi[:, k, n * width:(n + 1) * width],
                                     lambda k: w_lo[:, k, n * width:(n + 1) * width], DC,
                                     chunk_ready if n == 0 else None)
                q.then_inc(out_ready[s], 1)

            for s in range(2):
                turn(s, 0)
            multiply(0, 0, w_ready)
            turn(0, 1)
            multiply(1, 0)
            turn(1, 1)
            with pe.Fori(1, LOOPS - 1) as i:
                for s in range(2):
                    multiply(s, i)
                    turn(s, i + 1)
            for s in range(2):
                multiply(s, LOOPS - 1)

        if keep is not None and not direct:
            @block.gpsimd
            def _(pool):
                for s in range(2):
                    pool.sem_inc(kept[s], FREE)
                with pool.Fori(0, LOOPS) as i:
                    for s in range(2):
                        t = i * 2 + s
                        pool.wait_ge(lo_ready[s], i + 1 + FREE)
                        pool.tensor_copy(keep[0][:, :, bass.ts(t, P)], act_hi[:, s, :, :].bitcast(F32))
                        pool.tensor_copy(keep[1][:, :, bass.ts(t, P)], act_lo[:, s, :, :].bitcast(F32)) \
                            .then_inc(kept[s], 1)


def feature_proj(nc, tl, w_dram, xt_hi, xt_lo, qk):
    with ExitStack() as ctx:
        w_raw = tl.sb(ctx, "fp_w_raw", [P, 2, DC, P])
        w_hi = tl.sb(ctx, "fp_w_hi", [P, 2, DC, P], F32R)
        w_lo = tl.sb(ctx, "fp_w_lo", [P, 2, DC, P], F32R)
        out = [tl.ps(ctx, f"fp_out{s}", [P, 2, HALF]) for s in range(2)]
        w_loaded = tl.pair("fp_w_loaded")
        hi_ready = tl.pair("fp_hi_ready")
        lo_ready = tl.pair("fp_lo_ready")
        out_ready = tl.pair("fp_out_ready")
        act_read = tl.pair("fp_act_read")
        dve_read = tl.pair("fp_dve_read")
        block = ctx.enter_context(nc.Block())

        LOOPS = QK_CHUNKS // 2

        def chunks(engine, step):
            with engine.Fori(0, LOOPS) as i:
                for s in range(2):
                    step(s, i, i * 2 + s)
            step(0, LOOPS, QK_CHUNKS - 1)

        @block.sync
        def _(sp):
            def load(s, i, c):
                sp.wait_ge(lo_ready[s], i + FREE)
                sp.dma_start(w_raw[:, s, :, :], w_dram[c, :, :, :]).then_inc(w_loaded[s], 16)
            chunks(sp, load)

        def chunks_ahead(engine, split, empty):
            for s in range(2):
                split(s, 0)
            with engine.Fori(0, LOOPS - 1) as i:
                for s in range(2):
                    empty(s, i, i * 2 + s)
                    split(s, i + 1)
            empty(0, LOOPS - 1, QK_CHUNKS - 3)
            split(0, LOOPS)
            empty(1, LOOPS - 1, QK_CHUNKS - 2)
            empty(0, LOOPS, QK_CHUNKS - 1)

        @block.scalar
        def _(act):
            def split(s, i):
                act.wait_ge(w_loaded[s], (i + 1) * 16)
                act.copy(w_hi[:, s, :, :], w_raw[:, s, :, :]).then_inc(hi_ready[s], 1)

            def empty(s, i, c):
                act.wait_ge(out_ready[s], i + 1)
                act.copy(qk[:, c, 0:HALF], out[s][:, 0, :]).then_inc(act_read[s], 1)
            for s in range(2):
                act.sem_inc(act_read[s], FREE)
            chunks_ahead(act, split, empty)

        @block.vector
        def _(dve):
            def split(s, i):
                dve.wait_ge(hi_ready[s], i + 1)
                dve.tensor_tensor(w_lo[:, s, :, :], w_raw[:, s, :, :], w_hi[:, s, :, :].bitcast(F32),
                                  ALU.subtract).then_inc(lo_ready[s], 1)

            def empty(s, i, c):
                dve.wait_ge(out_ready[s], i + 1)
                dve.tensor_copy(qk[:, c, HALF:T], out[s][:, 1, :]).then_inc(dve_read[s], 1)
            for s in range(2):
                dve.sem_inc(lo_ready[s], FREE)
                dve.sem_inc(dve_read[s], FREE)
            chunks_ahead(dve, split, empty)

        @block.tensor
        def _(pe):
            def step(s, i, c):
                pe.wait_ge(lo_ready[s], i + 1 + FREE)
                pe.wait_ge(act_read[s], i + FREE)
                pe.wait_ge(dve_read[s], i + FREE)
                for n in range(2):
                    q = three_passes(pe, out[s][:, n, :], lambda k: w_hi[:, s, k, :], lambda k: w_lo[:, s, k, :],
                                     lambda k: xt_hi[:, k, n * HALF:(n + 1) * HALF],
                                     lambda k: xt_lo[:, k, n * HALF:(n + 1) * HALF], DC)
                q.then_inc(out_ready[s], 1)
            chunks(pe, step)


def rotate(nc, tl, qk, perm, cos_dram, sin_dram):
    with ExitStack() as ctx:
        cos = tl.sb(ctx, "rot_cos", [P, T])
        sin = tl.sb(ctx, "rot_sin", [P, T])
        partner = tl.sb(ctx, "rot_partner", [P, T])
        swapped = [tl.ps(ctx, f"rot_swapped{s}", [P, 2, HALF]) for s in range(2)]
        loaded = tl.sem("rot_loaded")
        swapped_ready = tl.sem("rot_swapped_ready")
        partner_ready = tl.sem("rot_partner_ready")
        straight_ready = tl.sem("rot_straight_ready")
        rotated = tl.sem("rot_rotated")
        block = ctx.enter_context(nc.Block())
        n_chunks = SWA_K + 1

        @block.sync
        def _(sp):
            sp.dma_start(cos[:], cos_dram[:, :]).then_inc(loaded, 16)
            sp.dma_start(sin[:], sin_dram[:, :]).then_inc(loaded, 16)

        @block.tensor
        def _(pe):
            for c in range(n_chunks):
                if c >= 2:
                    pe.wait_ge(partner_ready, c - 1)
                for n in range(2):
                    q = pe.matmul(swapped[c % 2][:, n, :], perm[:], qk[:, c, n * HALF:(n + 1) * HALF],
                                  start=True, stop=True)
                q.then_inc(swapped_ready, 1)

        @block.gpsimd
        def _(pool):
            pool.wait_ge(loaded, 32)
            for c in range(n_chunks):
                pool.wait_ge(swapped_ready, c + 1)
                pool.tensor_tensor(qk[:, c, :], qk[:, c, :], cos[:], ALU.mult).then_inc(straight_ready, 1)

        @block.vector
        def _(dve):
            dve.wait_ge(loaded, 32)
            for c in range(n_chunks):
                dve.wait_ge(swapped_ready, c + 1)
                dve.wait_ge(rotated, c)
                dve.tensor_tensor(partner[:], swapped[c % 2][:].rearrange("p a b -> p (a b)"), sin[:],
                                  ALU.mult).then_inc(partner_ready, 1)
                dve.wait_ge(partner_ready, c + 1)
                dve.wait_ge(straight_ready, c + 1)
                dve.tensor_tensor(qk[:, c, :], qk[:, c, :], partner[:], ALU.add).then_inc(rotated, 1)


def decay(nc, tl, v, b_forget, tri_dram, key_rows, query_rows):
    with ExitStack() as ctx:
        tri = tl.sb(ctx, "dec_tri", [P, 2 * T - P])
        bias = tl.sb(ctx, "dec_bias", [P, FOX_HEADS])
        steps = [tl.sb(ctx, f"dec_step{n}", [P, NT, FOX_HEADS]) for n in range(7)]
        z, neg_abs, e, soft, low, log_f, z_neg = steps
        c = tl.sb(ctx, "dec_c", [FOX_HEADS, T])
        parts = [tl.sb(ctx, f"dec_part{n}", [FOX_HEADS, T], F32R) for n in range(4)]
        c_hi, c_lo, n_hi, n_lo = parts
        total = tl.ps(ctx, "dec_total", [P, 2, HALF])
        loaded = tl.sem("dec_loaded")
        step = tl.sem("dec_step")
        exp_ready = tl.sem("dec_exp_ready")
        ln_ready = tl.sem("dec_ln_ready")
        logs_ready = tl.sem("dec_logs_ready")
        summed = tl.sem("dec_summed")
        parts_ready = tl.sem("dec_parts_ready")
        ones_ready = tl.sem("dec_ones_ready")
        placed = tl.sem("dec_placed")
        block = ctx.enter_context(nc.Block())

        @block.sync
        def _(sp):
            sp.dma_start(tri[:], tri_dram[:, :]).then_inc(loaded, 16)
            sp.dma_start(bias[:], b_forget.partition_broadcast(P)).then_inc(loaded, 16)
            sp.wait_ge(ones_ready, 2)
            sp.wait_ge(parts_ready, 1)
            for rows, n, part in ((key_rows, 0, n_hi), (key_rows, 1, n_lo), (query_rows, 2, c_hi), (query_rows, 3, c_lo)):
                sp.dma_start(rows[n * FOX_HEADS:(n + 1) * FOX_HEADS, :].bitcast(F32), part[:].bitcast(F32)).then_inc(placed, 16)
            sp.wait_ge(placed, 64)

        @block.gpsimd
        def _(pool):
            pool.memset(key_rows[:].bitcast(F32), 1.0).then_inc(ones_ready, 1)
            pool.memset(query_rows[:].bitcast(F32), 1.0).then_inc(ones_ready, 1)

        @block.vector
        def _(dve):
            n = [0]

            def done(q):
                n[0] += 1
                q.then_inc(step, 1)
                dve.wait_ge(step, n[0])

            dve.wait_ge(loaded, 32)
            done(dve.tensor_tensor(z[:], v[:, :, V_FORGET:V_COLS], spread(bias[:], 1, NT), ALU.add))
            done(dve.tensor_scalar(z_neg[:], z[:], -1.0, None, ALU.mult))
            done(dve.tensor_tensor(neg_abs[:], z[:], z_neg[:], ALU.min))
            done(dve.tensor_scalar(low[:], z[:], 0.0, None, ALU.min))
            dve.wait_ge(ln_ready, 1)
            dve.tensor_tensor(log_f[:], low[:], soft[:], ALU.subtract).then_inc(logs_ready, 1)
            dve.wait_ge(summed, 1)
            done(dve.tensor_copy(c[:], total[0:FOX_HEADS, :, :].rearrange("p a b -> p (a b)")))
            done(dve.tensor_copy(c_hi[:], c[:]))
            done(dve.tensor_tensor(c_lo[:], c[:], c_hi[:].bitcast(F32), ALU.subtract))
            done(dve.tensor_scalar(n_hi[:], c_hi[:].bitcast(F32), -1.0, None, ALU.mult))
            done(dve.tensor_scalar(n_lo[:], c_lo[:].bitcast(F32), -1.0, None, ALU.mult))
            dve.tensor_copy(c[:, 0:1], c[:, 0:1]).then_inc(parts_ready, 1)

        @block.scalar
        def _(act):
            act.wait_ge(step, 3)
            act.activation(e[:], neg_abs[:], ACT.Exp).then_inc(exp_ready, 1)
            act.wait_ge(exp_ready, 1)
            act.activation(soft[:], e[:], ACT.Ln, bias=1.0).then_inc(ln_ready, 1)

        @block.tensor
        def _(pe):
            pe.wait_ge(logs_ready, 1)
            for n in range(2):
                for t in range(NT):
                    at = T - P - t * P + n * HALF
                    q = pe.matmul(total[0:FOX_HEADS, n, :], log_f[:, t, :], tri[:, at:at + HALF],
                                  start=(t == 0), stop=(t == NT - 1))
            q.then_inc(summed, 1)


def attention(nc, tl, qk, v, key_rows, query_rows, sinks, masks, head_pick, ident, ident16, mixed):
    with ExitStack() as ctx:
        fox_q = tl.sb(ctx, "at_fox_q", [P, 2, P])
        swa_q = tl.sb(ctx, "at_swa_q", [P, 2, P])
        scale = tl.sb(ctx, "at_scale", [P, 1])
        fox_rows = tl.sb(ctx, "at_fox_rows", [4 * FOX_HEADS, 2, P], F32R)
        fox_p = tl.sb(ctx, "at_fox_p", [P, 2, T])
        swa_p = tl.sb(ctx, "at_swa_p", [P, 2, 2 * P])
        fox_turned = tl.sb(ctx, "at_fox_turned", [P, 2, NT, P])
        swa_turned = tl.sb(ctx, "at_swa_turned", [P, 2, 2, P])
        neg_max = tl.sb(ctx, "at_neg_max", [P, 4])
        neg_cap = tl.sb(ctx, "at_neg_cap", [P, 2])
        row_sum = tl.sb(ctx, "at_row_sum", [P, 4])
        sink_e = tl.sb(ctx, "at_sink_e", [P, 2])
        total = tl.sb(ctx, "at_total", [P, 2])
        inv = tl.sb(ctx, "at_inv", [P, 4])
        fox_s = tl.ps(ctx, "at_fox_s", [P, 2, 2, HALF])
        swa_s = tl.ps(ctx, "at_swa_s", [P, 2, 2 * P])
        turn = tl.ps(ctx, "at_turn", [P, NT, P])
        o = tl.ps(ctx, "at_o", [P, 4, HEAD])

        FOX, SWA, UNITS = (0, 1), 2, ("fox0", "fox1", "swa")

        def per_unit(name):
            return [tl.sem(f"at_{name}_{u}") for u in UNITS]

        q_ready, scored, max_ready, prob, turned, taken = (
            per_unit(n) for n in ("q_ready", "scored", "max_ready", "prob", "turned", "taken"))
        zeroed = tl.sem("at_zeroed")
        capped = tl.sem("at_capped")
        totalled = tl.sem("at_totalled")
        inverted = tl.sem("at_inverted")
        o_ready = tl.sem("at_o_ready")
        o_read = tl.sem("at_o_read")
        block = ctx.enter_context(nc.Block())

        def steps(engine, body):
            for j in range(NT):
                with engine.Fori(0, PAIRS - 1) as c:
                    body(j, c, c + j * PAIRS, j, c + 1)
                body(j, PAIRS - 1, (j + 1) * PAIRS - 1, j + 1, 0)

        def first_key(j):
            return 0 if j else P

        @block.gpsimd
        def _(pool):
            pool.memset(fox_q[:], 0.0).then_inc(zeroed, 1)
            pool.memset(swa_q[:], 0.0).then_inc(zeroed, 1)
            pool.memset(scale[:], SCALE).then_inc(zeroed, 1)
            pool.wait_ge(zeroed, 3)
            for j in range(NT):
                now = slice(j * P, (j + 1) * P)
                with pool.Fori(0, PAIRS) as c:
                    step = c + j * PAIRS
                    for u in FOX:
                        at = slice(u * HEAD, (u + 1) * HEAD)
                        pool.wait_ge(scored[u], step + FREE)
                        pool.tensor_tensor(fox_q[at, u, :], qk[at, FOX_Q + c, now], scale[at, 0:1].broadcast_to([HEAD, P]), ALU.mult)
                        pool.tensor_tensor(fox_rows[:, u, :], query_rows[:, now].bitcast(F32),
                                           head_pick[:, bass.ds(2 * c + u, 1)].broadcast_to([4 * FOX_HEADS, P]),
                                           ALU.mult).then_inc(q_ready[u], 1)
                    pool.wait_ge(scored[SWA], step + FREE)
                    for u in range(2):
                        at = slice(u * HEAD, (u + 1) * HEAD)
                        q = pool.tensor_tensor(swa_q[at, u, :], qk[at, SWA_Q + c, now], scale[at, 0:1].broadcast_to([HEAD, P]), ALU.mult)
                    q.then_inc(q_ready[SWA], 1)

        @block.vector
        def _(dve):
            def maximum(u, j, c, step):
                dve.wait_ge(scored[u], step + 1 + FREE)
                if u in FOX:
                    dve.tensor_reduce(neg_max[:, u:u + 1],
                                      fox_s[:, u, :, :].rearrange("p a b -> p (a b)")[:, 0:(j + 1) * P],
                                      AX.X, ALU.max, negate=True).then_inc(max_ready[u], 1)
                    return
                dve.tensor_reduce(neg_cap[:], swa_s[:, :, first_key(j):2 * P], AX.X, ALU.max,
                                  negate=True).then_inc(capped, 1)
                dve.wait_ge(capped, step + 1)
                dve.tensor_tensor(neg_max[:, 2:4], neg_cap[:], sinks["negative"][:, c, :],
                                  ALU.min).then_inc(max_ready[u], 1)

            def take(u, j, step):
                if u == 0:
                    dve.wait_ge(o_read, step + FREE)
                dve.wait_ge(prob[u], step + 1 + FREE)
                if u in FOX:
                    dve.reciprocal(inv[:, u:u + 1], row_sum[:, u:u + 1]).then_inc(inverted, 1)
                    dve.wait_ge(turned[u], step + 1)
                    dve.tensor_copy(fox_turned[:, u, 0:j + 1, :], turn[:, 0:j + 1, :]).then_inc(taken[u], 1)
                    return
                dve.tensor_tensor(total[:], row_sum[:, 2:4], sink_e[:], ALU.add).then_inc(totalled, 1)
                dve.wait_ge(totalled, step + 1)
                dve.reciprocal(inv[:, 2:4], total[:]).then_inc(inverted, 1)
                dve.wait_ge(turned[u], step + 1)
                b = first_key(j) // P
                dve.tensor_copy(swa_turned[:, :, b:2, :],
                                turn[:].rearrange("p (h b) q -> p h b q", b=4)[:, :, b:2, :]).then_inc(taken[u], 1)

            def body(j, c, step, next_j, next_c):
                for u in (*FOX, SWA):
                    take(u, j, step)
                    if next_j < NT:
                        maximum(u, next_j, next_c, step + 1)
                dve.wait_ge(inverted, (step + 1) * 3)
                dve.wait_ge(o_ready, step + 1)
                fox_at = FOX_HEADS * HEAD
                dve.tensor_tensor(mixed[:, j, bass.ds(c * 2 * HEAD + fox_at, 2 * HEAD)].rearrange(
                    "p (h d) -> p h d", d=HEAD), o[:, 0:2, :], spread(inv[:, 0:2], 2, HEAD), ALU.mult)
                swa = mixed[:, j, 0:fox_at].rearrange("p (u c d) -> p u c d", u=2, d=HEAD)
                dve.tensor_tensor(swa[:, :, c, :], o[:, 2:4, :], spread(inv[:, 2:4], 2, HEAD),
                                  ALU.mult).then_inc(o_read, 1)

            dve.sem_inc(o_read, FREE)
            for u in (*FOX, SWA):
                maximum(u, 0, 0, 0)
            steps(dve, body)

        @block.scalar
        def _(act):
            for u in (*FOX, SWA):
                act.sem_inc(prob[u], FREE)
            for j in range(NT):
                n_keys, lo = (j + 1) * P, first_key(j)
                with act.Fori(0, PAIRS) as c:
                    step = c + j * PAIRS
                    for u in FOX:
                        act.wait_ge(max_ready[u], step + 1)
                        act.activation(fox_p[:, u, 0:n_keys],
                                       fox_s[:, u, :, :].rearrange("p a b -> p (a b)")[:, 0:n_keys], ACT.Exp,
                                       bias=neg_max[:, u:u + 1],
                                       accum_out=row_sum[:, u:u + 1]).then_inc(prob[u], 1)
                    act.wait_ge(max_ready[SWA], step + 1)
                    for h in range(2):
                        act.activation(sink_e[:, h:h + 1], sinks["value"][:, c, h:h + 1], ACT.Exp,
                                       bias=neg_max[:, 2 + h:3 + h])
                    for h in range(2):
                        q = act.activation(swa_p[:, h, lo:2 * P], swa_s[:, h, lo:2 * P], ACT.Exp,
                                           bias=neg_max[:, 2 + h:3 + h], accum_out=row_sum[:, 2 + h:3 + h])
                    q.then_inc(prob[SWA], 1)

        @block.tensor
        def _(pe):
            def score(u, j, c, step):
                pe.wait_ge(q_ready[u], step + 1)
                pe.wait_ge(prob[u], step + FREE)
                if u == SWA:
                    lo = first_key(j)
                    for h in range(2):
                        pe.matmul(swa_s[:, h, lo:2 * P], swa_q[:, h, :], qk[:, SWA_K, (j - 1) * P + lo:(j + 1) * P],
                                  start=True, stop=False)
                        q = pe.matmul(swa_s[:, h, lo:2 * P], ident16[:], masks[:, lo:2 * P], start=False, stop=True)
                    q.then_inc(scored[u], 1)
                    return
                n_keys = (j + 1) * P
                for n in range((n_keys + HALF - 1) // HALF):
                    end = min(HALF, n_keys - n * HALF)
                    out = fox_s[:, u, n, 0:end]
                    pe.matmul(out, fox_q[:, u, :], qk[:, FOX_K + c, n * HALF:n * HALF + end], start=True, stop=False)
                    if n * HALF + end == n_keys:
                        pe.matmul(fox_s[:, u, n, end - P:end], ident16[:], masks[:, P:2 * P],
                                  start=False, stop=False, skip_group_check=True)
                    q = pe.matmul(out, fox_rows[:, u, :], key_rows[:, n * HALF:n * HALF + end],
                                  start=False, stop=True)
                q.then_inc(scored[u], 1)

            def turn_probs(u, j, step):
                pe.wait_ge(prob[u], step + 1 + FREE)
                if u == 1:
                    pe.wait_ge(taken[0], step + 1)
                if u == SWA:
                    pe.wait_ge(taken[1], step + 1)
                    for h in range(2):
                        for b in range(first_key(j) // P, 2):
                            q = pe.transpose(turn[:, 4 * h + b, :], swa_p[:, h, b * P:(b + 1) * P], ident[:])
                else:
                    for b in range(j + 1):
                        q = pe.transpose(turn[:, b, :], fox_p[:, u, b * P:(b + 1) * P], ident[:])
                q.then_inc(turned[u], 1)

            def mix(u, j, c, step):
                pe.wait_ge(taken[u], step + 1)
                if u == SWA:
                    for h in range(2):
                        b0 = first_key(j) // P
                        for b in range(b0, 2):
                            q = pe.matmul(o[:, 2 + h, :], swa_turned[:, h, b, :],
                                          v[:, j - 1 + b, h * HEAD:(h + 1) * HEAD], start=(b == b0), stop=(b == 1))
                    q.then_inc(o_ready, 1)
                    return
                if u == 0:
                    pe.wait_ge(o_read, step + FREE)
                for b in range(j + 1):
                    pe.matmul(o[:, u, :], fox_turned[:, u, b, :],
                              v[:, b, bass.ds(c * 2 * HEAD + (V_FOX + u * HEAD), HEAD)],
                              start=(b == 0), stop=(b == j))

            def body(j, c, step, next_j, next_c):
                for u in (*FOX, SWA):
                    turn_probs(u, j, step)
                    if u > 0:
                        mix(u - 1, j, c, step)
                    if next_j < NT:
                        score(u, next_j, next_c, step + 1)
                mix(SWA, j, c, step)

            for u in (*FOX, SWA):
                pe.sem_inc(scored[u], FREE)
            for u in (*FOX, SWA):
                score(u, 0, 0, 0)
            steps(pe, body)


def wait_for(engine, sem, value):
    if not (isinstance(value, int) and value == 0):
        engine.wait_ge(sem, value)


def wait_apart(engine, sem, value, passed):
    engine.wait_ge(sem, value)
    engine.sem_inc(passed, 1)


def peer_scores(nc, tl, w_dram, keys_dram, xn_hi, xn_lo, top_v, top_i):
    with ExitStack() as ctx:
        w_raw = tl.sb(ctx, "ps_w_raw", [P, 2, DC, P])
        w_hi = tl.sb(ctx, "ps_w_hi", [P, 2, DC, P], F32R)
        w_lo = tl.sb(ctx, "ps_w_lo", [P, 2, DC, P], F32R)
        keys = tl.sb(ctx, "ps_keys", [P, 2, KEYS])
        query = tl.sb(ctx, "ps_query", [P, 2, T])
        best = tl.sb(ctx, "ps_best", [P, 2, NT, TOPK])
        where = tl.sb(ctx, "ps_where", [P, 2, NT, TOPK], U32)
        rest = tl.sb(ctx, "ps_rest", [P, NT, KEYS])
        q_out = [tl.ps(ctx, f"ps_q_out{s}", [P, 2, HALF]) for s in range(2)]
        score = [tl.ps(ctx, f"ps_score{s}", [P, NT, KEYS]) for s in range(2)]
        keys_loaded = tl.sem("ps_keys_loaded")
        w_loaded = tl.pair("ps_w_loaded")
        hi_ready = tl.pair("ps_hi_ready")
        lo_ready = tl.pair("ps_lo_ready")
        q_out_ready = tl.pair("ps_q_out_ready")
        query_ready = tl.pair("ps_query_ready")
        score_ready = tl.pair("ps_score_ready")
        score_read = tl.pair("ps_score_read")
        sweep = tl.sem("ps_sweep")
        passed = tl.sem("ps_passed")
        stored = tl.pair("ps_stored")
        block = ctx.enter_context(nc.Block())

        @block.sync
        def _(sp):
            sp.dma_start(keys[:], keys_dram.rearrange("c p k -> p c k")).then_inc(keys_loaded, 16)
            with sp.Fori(0, PEER_HEADS) as i:
                for s in range(2):
                    sp.wait_ge(lo_ready[s], i + FREE)
                    sp.dma_start(w_raw[:, s, :, :], w_dram[i * 2 + s, :, :, :]).then_inc(w_loaded[s], 16)

        @block.scalar
        def _(act):
            def split(s, i):
                act.wait_ge(w_loaded[s], (i + 1) * 16)
                act.copy(w_hi[:, s, :, :], w_raw[:, s, :, :]).then_inc(hi_ready[s], 1)

            def empty(s, i):
                act.wait_ge(q_out_ready[s], i + 1)
                act.wait_ge(score_ready[s], i + FREE)
                act.copy(query[:, s, :], q_out[s][:].rearrange("p a b -> p (a b)")) \
                    .then_inc(query_ready[s], 1)

            for s in range(2):
                act.sem_inc(query_ready[s], FREE)
                split(s, 0)
            with act.Fori(0, PEER_HEADS - 1) as i:
                for s in range(2):
                    empty(s, i)
                    split(s, i + 1)
            for s in range(2):
                empty(s, PEER_HEADS - 1)

        @block.tensor
        def _(pe):
            def queries(s, i, between=None):
                pe.wait_ge(lo_ready[s], i + 1 + FREE)
                pe.wait_ge(query_ready[s], i + FREE)
                for n in range(2):
                    if n == 1 and between is not None:
                        scores(*between)
                    q = three_passes(pe, q_out[s][:, n, :], lambda k: w_hi[:, s, k, :],
                                     lambda k: w_lo[:, s, k, :],
                                     lambda k: xn_hi[:, k, n * HALF:(n + 1) * HALF],
                                     lambda k: xn_lo[:, k, n * HALF:(n + 1) * HALF], DC)
                q.then_inc(q_out_ready[s], 1)

            def scores(s, i):
                pe.wait_ge(query_ready[s], i + 1 + FREE)
                pe.wait_ge(score_read[s], i + FREE)
                for t in range(NT):
                    q = pe.matmul(score[s][:, t, :], query[:, s, t * P:(t + 1) * P], keys[:, s, :],
                                  start=True, stop=True)
                q.then_inc(score_ready[s], 1)

            for s in range(2):
                pe.sem_inc(score_ready[s], FREE)
            pe.wait_ge(keys_loaded, 16)
            queries(0, 0)
            with pe.Fori(0, PEER_HEADS - 1) as i:
                for s in range(2):
                    queries(1 - s, i + s, (s, i))
            queries(1, PEER_HEADS - 1, (0, PEER_HEADS - 1))
            scores(1, PEER_HEADS - 1)

        @block.vector
        def _(dve):
            for s in range(2):
                dve.sem_inc(score_read[s], FREE)
            with dve.Fori(0, PEER_HEADS) as i:
                for s in range(2):
                    done = (i * 2 + s) * 5
                    dve.wait_ge(score_ready[s], i + 1 + FREE)
                    wait_apart(dve, stored[s], i + FREE, passed)
                    for t in range(NT):
                        q = dve.max(best[:, s, t, 0:8], score[s][:, t, :])
                    q.then_inc(sweep, 1)
                    wait_apart(dve, sweep, done + 1, passed)
                    for t in range(NT):
                        q = dve.max_index(where[:, s, t, 0:8], best[:, s, t, 0:8], score[s][:, t, :])
                    q.then_inc(sweep, 1)
                    wait_apart(dve, sweep, done + 2, passed)
                    for t in range(NT):
                        q = dve.match_replace(rest[:, t, :], best[:, s, t, 0:8], score[s][:, t, :], LOWEST)
                    q.then_inc(sweep, 1)
                    wait_apart(dve, sweep, done + 3, passed)
                    for t in range(NT):
                        q = dve.max(best[:, s, t, 8:16], rest[:, t, :])
                        if t == 0:
                            q.then_inc(score_read[s], 1)
                    q.then_inc(sweep, 1)
                    wait_apart(dve, sweep, done + 4, passed)
                    for t in range(NT):
                        q = dve.max_index(where[:, s, t, 8:16], best[:, s, t, 8:16], rest[:, t, :])
                    q.then_inc(sweep, 1)

        @block.gpsimd
        def _(pool):
            for s in range(2):
                pool.sem_inc(lo_ready[s], FREE)
                pool.sem_inc(stored[s], FREE)

            def split(s, i):
                pool.wait_ge(hi_ready[s], i + 1)
                pool.tensor_tensor(w_lo[:, s, :, :], w_raw[:, s, :, :], w_hi[:, s, :, :].bitcast(F32),
                                   ALU.subtract).then_inc(lo_ready[s], 1)

            def store(s, i):
                pool.wait_ge(sweep, (i * 2 + s + 1) * 5)
                pool.tensor_copy(top_v[:, :, i * 2 + s, :], best[:, s, :, :])
                pool.tensor_copy(top_i[:, :, i * 2 + s, :], where[:, s, :, :]).then_inc(stored[s], 1)

            for s in range(2):
                split(s, 0)
            with pool.Fori(0, PEER_HEADS - 1) as i:
                for s in range(2):
                    split(s, i + 1)
                    store(s, i)
            for s in range(2):
                store(s, PEER_HEADS - 1)


def experts_up(nc, tl, u_dram, iota_dram, xn_hi, xn_lo, top_v, top_i, ident, act_dram, gates_dram,
               dense_late, dense_stored):
    with ExitStack() as ctx:
        GROUPS, LOTS, LOT = 8, 4, 4
        SIDE = dense_late.shape[2]
        u_raw = tl.sb(ctx, "eu_u_raw", [P, 2, DC, KEYS])
        u_hi = tl.sb(ctx, "eu_u_hi", [P, 2, DC, KEYS], F32R)
        u_lo = tl.sb(ctx, "eu_u_lo", [P, 2, DC, KEYS], F32R)
        gelu = tl.sb(ctx, "eu_gelu", [P, 2, T])
        iota = tl.sb(ctx, "eu_iota", [P, KEYS])
        hot = tl.sb(ctx, "eu_hot", [P, 2, 2, LOT, KEYS], F32R)
        hot_gate = tl.sb(ctx, "eu_hot_gate", [P, 2, LOT, 2, KEYS], F32R)
        dense = [tl.sb(ctx, "eu_dense", [P, KEYS, SIDE]), dense_late]
        sums = tl.sb(ctx, "eu_sums", [P, TOPK, TOPK])
        rest = tl.sb(ctx, "eu_rest", [P, TOPK * TOPK])
        head_v = tl.sb(ctx, "eu_head_v", [P, TOPK])
        head_p = tl.sb(ctx, "eu_head_p", [P, TOPK], U32)
        small = [P, PEER_HEADS, TOPK]
        best = tl.sb(ctx, "eu_best", small)
        place = tl.sb(ctx, "eu_place", small, U32)
        digit_u = tl.sb(ctx, "eu_digit_u", [P, 2, PEER_HEADS, TOPK], U32)
        digit = tl.sb(ctx, "eu_digit", [P, 2, PEER_HEADS, TOPK])
        gap = tl.sb(ctx, "eu_gap", small)
        e = tl.sb(ctx, "eu_e", small)
        total = tl.sb(ctx, "eu_total", [P, PEER_HEADS])
        inv = tl.sb(ctx, "eu_inv", [P, PEER_HEADS])
        gate = tl.sb(ctx, "eu_gate", small)
        key = tl.sb(ctx, "eu_key", [P, 2, PEER_HEADS, TOPK])
        term = tl.sb(ctx, "eu_term", [P, 2, PEER_HEADS, TOPK])
        key_t = tl.sb(ctx, "eu_key_t", [P, 2, P])
        gate_t = tl.sb(ctx, "eu_gate_t", [P, 2, P], F32R)
        u_out = [tl.ps(ctx, f"eu_u_out{s}", [P, 2, HALF]) for s in range(2)]
        lot_out = [tl.ps(ctx, f"eu_lot_out{s}", [P, LOT, 2, KEYS]) for s in range(2)]
        turned = lot_out[0][:].rearrange("p u h b -> p (u h) b")

        iota_loaded = tl.sem("eu_iota_loaded")
        u_loaded = tl.pair("eu_u_loaded")
        hi_ready = tl.pair("eu_hi_ready")
        lo_ready = tl.pair("eu_lo_ready")
        u_done = tl.pair("eu_u_done")
        gelu_ready = tl.pair("eu_gelu_ready")
        gelu_stored = tl.pair("eu_gelu_stored")
        one_ready = tl.pair("eu_one_ready")
        hot_ready = tl.pair("eu_hot_ready")
        lot_done = tl.pair("eu_lot_done")
        lot_hi_read = tl.pair("eu_lot_hi_read")
        lot_read = tl.pair("eu_lot_read")
        passed = tl.sem("eu_passed")
        sweep = tl.sem("eu_sweep")
        gap_ready = tl.sem("eu_gap_ready")
        e_ready = tl.sem("eu_e_ready")
        step = tl.sem("eu_step")
        choice_ready = tl.sem("eu_choice_ready")
        turned_ready = tl.sem("eu_turned_ready")
        turned_read = tl.sem("eu_turned_read")
        chosen = tl.sem("eu_chosen")
        block = ctx.enter_context(nc.Block())

        def tiles(engine, tile):
            tile(0, False)
            with engine.Fori(1, NT - 1) as t:
                tile(t, False)
            tile(NT - 1, True)

        def groups(engine, t, last, side, group):
            PER_SIDE = GROUPS // 2
            base = t * GROUPS + side * PER_SIDE
            for g in range(side + 1):
                group(side, g, base + g, g, 2)
            end = 2 if side == 1 and last else 0
            if PER_SIDE - end > side + 1:
                with engine.Fori(side + 1, PER_SIDE - end) as g:
                    group(side, g, base + g, None, 2)
            for left in reversed(range(end)):
                g = PER_SIDE - 1 - left
                group(side, g, base + g, None, left)

        @block.sync
        def _(sp):
            def load(s, n):
                sp.dma_start(u_raw[:, s, :, :], u_dram[n * 2 + s, :, :, :]).then_inc(u_loaded[s], 16)

            sp.dma_start(iota[:], iota_dram[:, :]).then_inc(iota_loaded, 16)
            for s in range(2):
                load(s, 0)

            def group(side, g, n, spot, left):
                for s in range(2):
                    if left:
                        sp.wait_ge(lo_ready[s], n + 1)
                        load(s, n + 1)

            def tile(t, last):
                for side in range(2):
                    groups(sp, t, last, side, group)
            tiles(sp, tile)

        @block.gpsimd
        def _(pool):
            def group(side, g, n, spot, left):
                for s in range(2):
                    pool.wait_ge(hi_ready[s], n + 1)
                    pool.tensor_tensor(u_lo[:, s, :, :], u_raw[:, s, :, :], u_hi[:, s, :, :].bitcast(F32),
                                       ALU.subtract).then_inc(lo_ready[s], 1)

            def tile(t, last):
                for side in range(2):
                    groups(pool, t, last, side, group)
            tiles(pool, tile)

        @block.scalar
        def _(act):
            def split(s, n):
                act.wait_ge(u_loaded[s], (n + 1) * 16)
                act.copy(u_hi[:, s, :, :], u_raw[:, s, :, :]).then_inc(hi_ready[s], 1)

            def activate(s, n, final):
                act.wait_ge(u_done[s], n + 1)
                wait_for(act, gelu_stored[s], n * 16)
                act.activation(gelu[:, s, :], u_out[s][:].rearrange("p a b -> p (a b)"), ACT.Gelu) \
                    .then_inc(gelu_ready[s], 1)
                if not final:
                    split(s, n + 1)
                act.wait_ge(gelu_ready[s], n + 1)
                act.dma_start(act_dram[n * 2 + s, :, :], gelu[:, s, :]).then_inc(gelu_stored[s], 16)

            def take_hi(side, g, n, lot):
                s = lot % 2
                act.wait_ge(lot_done[s], n * 2 + (lot // 2 + 1))
                at = g * (LOTS * LOT) + lot * LOT
                act.copy(dense[side][:, :, bass.ds(at, LOT)], lot_out[s][:, :, 0, :].rearrange("p u b -> p b u")) \
                    .then_inc(lot_hi_read[s], 1)

            def soften(t):
                act.wait_ge(gap_ready, t + 1)
                act.activation(e[:], gap[:], ACT.Exp).then_inc(e_ready, 1)

            def store(t, side, half):
                b = slice(half * (KEYS // 2), (half + 1) * (KEYS // 2))
                act.dma_start(gates_dram[b, :, bass.ds(t * P + side * SIDE, SIDE)].rearrange("b a t -> a b t"),
                              dense[side][:, b, :]).then_inc(dense_stored[side], 16)

            def tile(t, last):
                def side_group(side, g, n, spot, left):
                    for s in range(2):
                        if left:
                            activate(s, n + 1, left == 1)
                        for lot in (2 * s, 2 * s + 1):
                            take_hi(side, g, n, lot)
                        if s == 0 and spot == 0:
                            if side == 1:
                                store(t, 0, 1)
                            elif not isinstance(t, int) or t > 0:
                                store(t - 1, 1, 1)
                        if s == 0 and (side, spot) == (1, 1) and not last:
                            soften(t + 1)

                for side in range(2):
                    wait_for(act, dense_stored[side], t * 32)
                    groups(act, t, last, side, side_group)
                    act.wait_ge(lot_read[1], (t * 2 + (side + 1)) * GROUPS)
                    act.wait_ge(lot_read[0], (t * 2 + (side + 1)) * GROUPS)
                    if not (last and side == 1):
                        store(t, side, 0)

            for s in range(2):
                split(s, 0)
            for s in range(2):
                activate(s, 0, False)
            soften(0)
            tiles(act, tile)
            act.wait_ge(dense_stored[0], NT * 32)
            for s in range(2):
                act.wait_ge(gelu_stored[s], NT * GROUPS * 16)

        @block.vector
        def _(dve):
            lists = top_v[:].rearrange("p t (h c) k -> p (t h) c k", c=2)
            numbers = top_i[:].rearrange("p t (h c) k -> p t h c k", c=2)

            def choose(row, head):
                flat = sums[:].rearrange("p a b -> p (a b)")
                n = row * 6
                dve.tensor_tensor(sums[:], spread(lists[:, row, 0, :], 2, TOPK), spread(lists[:, row, 1, :], 1, TOPK),
                                  ALU.add).then_inc(sweep, 1)
                wait_apart(dve, sweep, n + 1, passed)
                dve.max(head_v[:, 0:8], flat).then_inc(sweep, 1)
                wait_apart(dve, sweep, n + 2, passed)
                dve.max_index(head_p[:, 0:8], head_v[:, 0:8], flat).then_inc(sweep, 1)
                dve.match_replace(rest[:], head_v[:, 0:8], flat, LOWEST).then_inc(sweep, 1)
                wait_apart(dve, sweep, n + 4, passed)
                dve.max(head_v[:, 8:16], rest[:]).then_inc(sweep, 1)
                wait_apart(dve, sweep, n + 5, passed)
                dve.max_index(head_p[:, 8:16], head_v[:, 8:16], rest[:]).then_inc(sweep, 1)
                dve.wait_ge(sweep, n + 6)
                dve.tensor_copy(best[:, head, :], head_v[:])
                dve.tensor_copy(place[:, head, :], head_p[:]).then_inc(chosen, 1)

            STEPS = 5 + 2 * TOPK - 1
            taken = [0]

            def done(t, w):
                taken[0] = taken[0] % STEPS + 1
                w.then_inc(step, 1)
                dve.wait_ge(step, t * STEPS + taken[0])

            def settle_gaps(t):
                dve.wait_ge(chosen, (t + 1) * PEER_HEADS)
                dve.tensor_tensor(gap[:], best[:], best[:, :, 0:1].broadcast_to(small), ALU.subtract) \
                    .then_inc(gap_ready, 1)
                dve.tensor_scalar(digit_u[:, 0, :, :], place[:], 4, None, ALU.logical_shift_right)
                done(t, dve.tensor_scalar(digit_u[:, 1, :, :], place[:], TOPK - 1, None, ALU.bitwise_and))
                done(t, dve.tensor_copy(digit[:], digit_u[:]))

            def settle_keys(t, places):
                for a in places:
                    for c in range(2):
                        w = dve.scalar_tensor_tensor(out=(term if a else key)[:, c, :, :], in0=digit[:, c, :, :],
                                                     scalar=float(a), in1=spread(numbers[:, t, :, c, a], 2, TOPK),
                                                     op0=ALU.is_equal, op1=ALU.mult)
                    done(t, w)
                    if a:
                        done(t, dve.tensor_tensor(key[:], key[:], term[:], ALU.add))

            def settle_gates(t):
                dve.wait_ge(e_ready, t + 1)
                done(t, dve.tensor_reduce(total[:], e[:], AX.X, ALU.add))
                done(t, dve.reciprocal(inv[:], total[:]))
                done(t, dve.tensor_tensor(gate[:], e[:], spread(inv[:], 2, TOPK), ALU.mult))
                dve.tensor_copy(total[:, 0:1], inv[:, 0:1]).then_inc(choice_ready, 1)

            def untangle(t):
                dve.wait_ge(turned_ready, t + 1)
                dve.tensor_copy(key_t[:], turned[:, 0:2, :])
                dve.tensor_copy(gate_t[:, 0, :], turned[:, 2, :]).then_inc(turned_read, 1)
                dve.wait_ge(turned_read, t * 2 + 1)
                dve.tensor_tensor(gate_t[:, 1, :], turned[:, 2, :], gate_t[:, 0, :].bitcast(F32), ALU.subtract) \
                    .then_inc(turned_read, 1)
                dve.wait_ge(turned_read, t * 2 + 2)

            def build(side, g, n, lot):
                s = lot % 2
                at = g * (LOTS * LOT) + (side * SIDE + lot * LOT)
                dve.tensor_tensor(hot[:, s, :, :, :], spread(spread(iota[:], 1, LOT), 1, 2),
                                  spread(key_t[:, :, bass.ds(at, LOT)], 3, KEYS), ALU.is_equal) \
                    .then_inc(one_ready[s], 1)
                dve.wait_ge(one_ready[s], n * 2 + (lot // 2 + 1))
                dve.tensor_tensor(hot_gate[:, s, :, :, :].rearrange("p u h k -> p h u k"), spread(hot[:, s, 1, :, :].bitcast(F32), 1, 2),
                                  spread(gate_t[:, :, bass.ds(at, LOT)].bitcast(F32), 3, KEYS), ALU.mult) \
                    .then_inc(hot_ready[s], 1)

            def take_lo(side, g, n, lot):
                s = lot % 2
                dve.wait_ge(lot_hi_read[s], n * 2 + (lot // 2 + 1))
                at = g * (LOTS * LOT) + lot * LOT
                gates = dense[side][:, :, bass.ds(at, LOT)]
                dve.tensor_tensor(gates, gates, lot_out[s][:, :, 1, :].rearrange("p u b -> p b u"), ALU.add) \
                    .then_inc(lot_read[s], 1)

            def tile(t, last):
                def group(side, g, n, spot, left):
                    opens = (side, spot) == (0, 0)
                    if opens:
                        untangle(t)
                    build(side, g, n, 0)
                    build(side, g, n, 1)
                    if not last:
                        if side == 0 and not opens:
                            choose((t + 1) * PEER_HEADS + 2 * g, 2 * g)
                        elif side == 1 and spot == 0:
                            settle_gaps(t + 1)
                            settle_keys(t + 1, range(4))
                        elif side == 1 and spot == 1:
                            settle_keys(t + 1, range(10, TOPK))
                    take_lo(side, g, n, 0)
                    build(side, g, n, 2)
                    take_lo(side, g, n, 1)
                    build(side, g, n, 3)
                    if not last:
                        if opens:
                            choose((t + 1) * PEER_HEADS, 0)
                        if side == 0:
                            choose((t + 1) * PEER_HEADS + (2 * g + 1), 2 * g + 1)
                        elif spot == 0:
                            settle_keys(t + 1, range(4, 10))
                        elif spot == 1:
                            settle_gates(t + 1)
                    take_lo(side, g, n, 2)
                    take_lo(side, g, n, 3)

                for side in range(2):
                    groups(dve, t, last, side, group)

            with dve.Fori(0, PEER_HEADS) as head:
                choose(head, head)
            settle_gaps(0)
            settle_keys(0, range(TOPK))
            settle_gates(0)
            dve.wait_ge(iota_loaded, 16)
            tiles(dve, tile)

        @block.tensor
        def _(pe):
            def chunk(s, n, turning=None):
                pe.wait_ge(lo_ready[s], n + 1)
                wait_for(pe, gelu_ready[s], n)
                for half in range(2):
                    if half == 1 and turning is not None:
                        turn(turning)
                    tokens = slice(half * HALF, (half + 1) * HALF)
                    q = three_passes(pe, u_out[s][:, half, :], lambda k: u_hi[:, s, k, :], lambda k: u_lo[:, s, k, :],
                                     lambda k: xn_hi[:, k, tokens], lambda k: xn_lo[:, k, tokens], DC)
                q.then_inc(u_done[s], 1)

            def turn(t):
                pe.wait_ge(choice_ready, t + 1)
                wait_for(pe, lot_read[0], t * (2 * GROUPS))
                for j in range(3):
                    rows = gate[:] if j == 2 else key[:, j, :, :]
                    q = pe.transpose(turned[:, j, :], rows.rearrange("p h k -> p (h k)"), ident[:])
                q.then_inc(turned_ready, 1)

            def scatter(n, lot):
                s = lot % 2
                pe.wait_ge(hot_ready[s], n * 2 + (lot // 2 + 1))
                wait_for(pe, lot_read[s], n * 2 + lot // 2)
                for u in range(LOT):
                    q = pe.matmul(lot_out[s][:, u, :, :], hot[:, s, 0, u, :], hot_gate[:, s, u, :, :],
                                  start=True, stop=True)
                q.then_inc(lot_done[s], 1)

            def tile(t, last):
                def group(side, g, n, spot, left):
                    for s in range(2):
                        if left:
                            chunk(s, n + 1, t if (side, spot, s) == (0, 0, 0) else None)
                        scatter(n, 2 * s)
                        scatter(n, 2 * s + 1)

                for side in range(2):
                    groups(pe, t, last, side, group)

            for s in range(2):
                chunk(s, 0)
            tiles(pe, tile)


def expert_down(nc, tl, v_dram, act_dram, gates_dram, h, h_dram, dense_late, gates_stored):
    with ExitStack() as ctx:
        SLOTS = 4
        PIECES = 8
        SIDE = dense_late.shape[2]
        TILES = HALF // P
        v_raw = tl.sb(ctx, "ed_v_raw", [P, SLOTS, D])
        act_in = tl.sb(ctx, "ed_act_in", [P, SLOTS, HALF])
        gate_in = tl.sb(ctx, "ed_gate_in", [P, SLOTS, HALF])
        v_hi = tl.sb(ctx, "ed_v_hi", [P, SLOTS, D], F32R)
        v_lo = tl.sb(ctx, "ed_v_lo", [P, SLOTS, D], F32R)
        coef = tl.sb(ctx, "ed_coef", [P, SLOTS, HALF])
        c_hi = tl.sb(ctx, "ed_c_hi", [P, SLOTS, HALF], F32R)
        c_lo = tl.sb(ctx, "ed_c_lo", [P, SLOTS, HALF], F32R)
        zero = tl.sb(ctx, "ed_zero", [P, HALF], BF16)
        y = tl.ps(ctx, "ed_y", [P, TILES, 2, HALF])
        slots = range(SLOTS)
        v_loaded = [tl.sem(f"ed_v_loaded{s}") for s in slots]
        a_loaded = [tl.sem(f"ed_a_loaded{s}") for s in slots]
        coef_ready = [tl.sem(f"ed_coef_ready{s}") for s in slots]
        hi_ready = [tl.sem(f"ed_hi_ready{s}") for s in slots]
        split = [tl.sem(f"ed_split{s}") for s in slots]
        used = [tl.sem(f"ed_used{s}") for s in slots]
        zeroed = tl.sem("ed_zeroed")
        h_loaded = tl.sem("ed_h_loaded")
        summed = tl.sem("ed_summed")
        added = tl.sem("ed_added")
        block = ctx.enter_context(nc.Block())
        ROUNDS = KEYS // SLOTS
        v_chunks = v_dram.rearrange("(a b) d -> b a d", b=KEYS)

        @block.sync
        def _(sp):
            sp.dma_start(h[:], h_dram.rearrange("(t p) d -> p t d", p=P)).then_inc(h_loaded, 16)
            for half in range(2):
                tokens = slice(half * HALF, (half + 1) * HALF)

                def load(i):
                    for s in slots:
                        b = i * SLOTS + s
                        sp.wait_ge(split[s], i + half * ROUNDS + FREE)
                        sp.dma_start(v_raw[:, s, :], v_chunks[b, :, :]).then_inc(v_loaded[s], 16)
                        sp.dma_start(act_in[:, s, :], act_dram[b, :, tokens]).then_inc(a_loaded[s], 16)
                        sp.dma_start(gate_in[:, s, :], gates_dram[b, :, tokens]).then_inc(a_loaded[s], 16)

                if half == 0:
                    sp.wait_ge(gates_stored, (NT // 2) * 32)
                    with sp.Fori(0, 2) as i:
                        load(i)
                    with sp.Fori(2, PIECES + 2) as i:
                        load(i)
                        piece = bass.ds((i - 2) * (KEYS // PIECES), KEYS // PIECES)
                        sp.dma_start(gates_dram[piece, :, T - SIDE:T].rearrange("b a t -> a b t"),
                                     dense_late[:, piece, :]).then_inc(gates_stored, 16)
                    with sp.Fori(PIECES + 2, ROUNDS) as i:
                        load(i)
                else:
                    sp.wait_ge(gates_stored, (NT - 1) * 32 + PIECES * 16)
                    with sp.Fori(0, ROUNDS) as i:
                        load(i)

        @block.vector
        def _(dve):
            for s in slots:
                dve.sem_inc(split[s], FREE)
            dve.sem_inc(added, FREE)
            dve.memset(zero[:], 0.0).then_inc(zeroed, 1)
            for half in range(2):
                with dve.Fori(0, ROUNDS) as i:
                    r = i + half * ROUNDS
                    for s in slots:
                        dve.wait_ge(a_loaded[s], (r + 1) * 32)
                        dve.tensor_tensor(coef[:, s, :], act_in[:, s, :], gate_in[:, s, :], ALU.mult) \
                            .then_inc(coef_ready[s], 1)
                        dve.wait_ge(hi_ready[s], (r + 1) * 2)
                        dve.tensor_tensor(v_lo[:, s, :], v_raw[:, s, :], v_hi[:, s, :].bitcast(F32), ALU.subtract)
                        dve.tensor_tensor(c_lo[:, s, :], coef[:, s, :], c_hi[:, s, :].bitcast(F32),
                                          ALU.subtract).then_inc(split[s], 1)
                dve.wait_ge(summed, half + 1)
                dve.wait_ge(h_loaded, 16)
                for t in range(TILES):
                    rows = h[:, half * TILES + t, :]
                    q = dve.tensor_tensor(rows, rows, y[:, t, :, :].rearrange("p a b -> p (a b)"), ALU.add)
                q.then_inc(added, 1)

        @block.scalar
        def _(act):
            for half in range(2):
                with act.Fori(0, ROUNDS) as i:
                    r = i + half * ROUNDS
                    for s in slots:
                        act.wait_ge(used[s], r + FREE)
                        act.wait_ge(v_loaded[s], (r + 1) * 16)
                        act.copy(v_hi[:, s, :], v_raw[:, s, :]).then_inc(hi_ready[s], 1)
                        act.wait_ge(coef_ready[s], r + 1)
                        act.copy(c_hi[:, s, :], coef[:, s, :]).then_inc(hi_ready[s], 1)

        @block.tensor
        def _(pe):
            for s in slots:
                pe.sem_inc(used[s], FREE)
            pe.wait_ge(zeroed, 1)

            def zeros(start):
                for t in range(TILES):
                    for n in range(2):
                        q = pe.matmul(y[:, t, n, :], zero[:, 0:P], zero[:], start=start, stop=not start)
                return q

            for half in range(2):
                pe.wait_ge(added, half + FREE)
                zeros(True)
                with pe.Fori(0, ROUNDS) as i:
                    r = i + half * ROUNDS
                    for s in slots:
                        pe.wait_ge(split[s], r + 1 + FREE)
                        for t in range(TILES):
                            rows = slice(t * P, (t + 1) * P)
                            for lhs, rhs in ((c_hi, v_hi), (c_hi, v_lo), (c_lo, v_hi)):
                                for n in range(2):
                                    q = pe.matmul(y[:, t, n, :], lhs[:, s, rows],
                                                  rhs[:, s, n * HALF:(n + 1) * HALF], start=False, stop=False)
                        q.then_inc(used[s], 1)
                zeros(False).then_inc(summed, 1)


def load_layer_input(nc, w_dram, pt_dram, gain_dram, pt, pw, gain, loaded):
    with nc.Block() as block:
        @block.sync
        def _(sp):
            sp.dma_start(pt[:], pt_dram.rearrange("(k p) t -> p k t", p=P)).then_inc(loaded, 16)
            sp.dma_start(pw[:], w_dram.rearrange("(k p) d -> p k d", p=P)).then_inc(loaded, 16)
            sp.dma_start(gain[:], gain_dram.partition_broadcast(P)).then_inc(loaded, 16)


def last_norm(nc, tl, h, gate_logit, pt, pw, gain, loaded, eps, out_dram):
    KP = 2
    with ExitStack() as ctx:
        part = tl.sb(ctx, "fs_part", [P, 2, D])
        square = tl.sb(ctx, "fs_square", [P, D])
        ssq = tl.sb(ctx, "fs_ssq", [P, NT])
        root = tl.sb(ctx, "fs_root", [P, NT])
        rstd = tl.sb(ctx, "fs_rstd", [P, NT])
        out = [tl.ps(ctx, f"fs_out{s}", [P, 2, HALF]) for s in range(2)]
        gate_ready = tl.sem("fs_gate_ready")
        out_ready = tl.sem("fs_out_ready")
        part_ready = tl.sem("fs_part_ready")
        h_ready = tl.sem("fs_h_ready")
        squared = tl.sem("fs_squared")
        root_ready = tl.sem("fs_root_ready")
        rstd_ready = tl.sem("fs_rstd_ready")
        row_ready = tl.sem("fs_row_ready")
        stored = tl.sem("fs_stored")
        block = ctx.enter_context(nc.Block())

        @block.tensor
        def _(pe):
            pe.wait_ge(loaded, 48)
            for t in range(NT):
                if t >= 2:
                    pe.wait_ge(part_ready, t - 1)
                for n in range(2):
                    for k in range(KP):
                        q = pe.matmul(out[t % 2][:, n, :], pt[:, k, t * P:(t + 1) * P],
                                      pw[:, k, n * HALF:(n + 1) * HALF], start=(k == 0), stop=(k == KP - 1))
                q.then_inc(out_ready, 1)

        @block.scalar
        def _(act):
            for t in range(NT):
                act.activation(gate_logit[:, t, :], gate_logit[:, t, :], ACT.Sigmoid).then_inc(gate_ready, 1)
            for t in range(NT):
                act.wait_ge(h_ready, t + 1)
                act.activation(square[:], h[:, t, :], ACT.Square, accum_out=ssq[:, t:t + 1]).then_inc(squared, 1)
                act.wait_ge(squared, t + 1)
                act.activation(root[:, t:t + 1], ssq[:, t:t + 1], ACT.Sqrt, scale=1.0 / D,
                               bias=eps[:, 0:1]).then_inc(root_ready, 1)

        @block.vector
        def _(dve):
            def normalize(t):
                dve.wait_ge(root_ready, t + 1)
                dve.reciprocal(rstd[:, t:t + 1], root[:, t:t + 1]).then_inc(rstd_ready, 1)
                dve.wait_ge(rstd_ready, t + 1)
                dve.scalar_tensor_tensor(out=h[:, t, :], in0=h[:, t, :], scalar=rstd[:, t:t + 1], in1=gain[:],
                                         op0=ALU.mult, op1=ALU.mult).then_inc(row_ready, 1)

            dve.wait_ge(loaded, 48)
            for t in range(NT):
                dve.wait_ge(gate_ready, t + 1)
                dve.wait_ge(out_ready, t + 1)
                if t >= 2:
                    dve.wait_ge(h_ready, t - 1)
                dve.tensor_tensor(part[:, t % 2, :], gate_logit[:, t, :],
                                  out[t % 2][:].rearrange("p a b -> p (a b)"), ALU.mult).then_inc(part_ready, 1)
                dve.wait_ge(part_ready, t + 1)
                dve.tensor_tensor(h[:, t, :], h[:, t, :], part[:, t % 2, :], ALU.add).then_inc(h_ready, 1)
                if t >= 1:
                    normalize(t - 1)
            normalize(NT - 1)

        @block.sync
        def _(sp):
            for t in range(NT):
                sp.wait_ge(row_ready, t + 1)
                sp.dma_start(out_dram[t * P:(t + 1) * P, :], h[:, t, :]).then_inc(stored, 16)
            sp.wait_ge(stored, 16 * NT)


def program(nc, d, out):
    with ExitStack() as top:
        tl = Tools(nc)
        whole = ExitStack()
        top.enter_context(whole)
        ident = tl.sb(whole, "ident", [P, P])
        gains = tl.sb(whole, "gains", [P, 4, DC])
        eps = tl.sb(whole, "eps", [P, 1])
        const_loaded = tl.sem("const_loaded")
        eps_ready = tl.sem("eps_ready")
        with nc.Block() as block:
            @block.sync
            def _(sp):
                sp.dma_start(ident[:], d["ident"][:, :]).then_inc(const_loaded, 16)
                sp.dma_start(gains[:], d["gains"][:, :, :]).then_inc(const_loaded, 16)
                sp.wait_ge(const_loaded, 32)

            @block.gpsimd
            def _(pool):
                pool.memset(eps[:], EPS).then_inc(eps_ready, 1)

        residual = top.enter_context(ExitStack())
        h = tl.sb(residual, "h", [P, NT, D])

        def gain(n):
            return {"t": gains[:, n, :], "eps": eps}

        att = ExitStack()
        v = tl.sb(att, "v", [P, NT, V_COLS])
        masks = tl.sb(att, "masks", [P, 2 * P], BF16)
        ident16 = tl.sb(att, "ident16", [P, P], BF16)
        perm = tl.sb(att, "perm", [P, P])
        key_rows = tl.sb(att, "key_rows", [4 * FOX_HEADS, T], F32R)
        query_rows = tl.sb(att, "query_rows", [4 * FOX_HEADS, T], F32R)
        head_pick = tl.sb(att, "head_pick", [4 * FOX_HEADS, FOX_HEADS])
        sinks = {"value": tl.sb(att, "sink_value", [P, PAIRS, 2]),
                 "negative": tl.sb(att, "sink_negative", [P, PAIRS, 2])}
        att_qk = ExitStack()
        acts = ExitStack()
        xt_hi = tl.sb(acts, "xt_hi", [P, DC, T], F32R, "right")
        xt_lo = tl.sb(acts, "xt_lo", [P, DC, T], F32R, "right")

        def keep_v(dve, s, t, o):
            return dve.tensor_copy(v[:, t, :].rearrange("p (n w) -> p n w", n=2), o[:, :, 0:V_PART])

        token_pass(nc, tl, "mix", h, d["x"], 1, gain(0), ident, (2, V_PART), d["w_v"], (xt_hi, xt_lo), keep_v)
        qk = tl.sb(att_qk, "qk", [P, QK_CHUNKS, T])
        feature_proj(nc, tl, d["w_qk"], xt_hi, xt_lo, qk)
        acts.close()
        with ExitStack() as ctx:
            mask_raw = tl.sb(ctx, "mask_raw", [P, 2 * P])
            loaded = tl.sem("small_loaded")
            block = ctx.enter_context(nc.Block())

            @block.sync
            def _(sp):
                sp.dma_start(mask_raw[:], d["masks"][:, :]).then_inc(loaded, 16)
                sp.dma_start(perm[:], d["perm"][:, :]).then_inc(loaded, 16)
                sp.dma_start(head_pick[:], d["head_pick"][:, :]).then_inc(loaded, 16)
                sp.dma_start(sinks["value"][:], d["sinks"].partition_broadcast(P)).then_inc(loaded, 16)

            @block.vector
            def _(dve):
                dve.wait_ge(loaded, 64)
                dve.tensor_copy(masks[:], mask_raw[:])
                dve.tensor_copy(ident16[:], ident[:])
                dve.tensor_scalar(sinks["negative"][:], sinks["value"][:], -1.0, None, ALU.mult)
        rotate(nc, tl, qk, perm, d["cos"], d["sin"])
        decay(nc, tl, v, d["b_forget"], d["tri"], key_rows, query_rows)
        mixing = ExitStack()
        mixed = tl.sb(mixing, "mixed", [P, NT, D], F32, "right")
        attention(nc, tl, qk, v, key_rows, query_rows, sinks, masks, head_pick, ident, ident16, mixed)
        att_qk.close()
        att.close()

        def add_out(dve, s, t, o):
            return dve.tensor_tensor(h[:, t, :], h[:, t, :], o[:].rearrange("p n w -> p (n w)"), ALU.add)

        token_pass(nc, tl, "out", mixed, None, 2, gain(1), ident, (2, HALF), d["w_out"], None, add_out)
        mixing.close()
        tl.recycle()
        experts = ExitStack()
        xn_hi = tl.sb(experts, "xn_hi", [P, DC, T], F32R, "right")
        xn_lo = tl.sb(experts, "xn_lo", [P, DC, T], F32R, "right")
        h_dram = nc.dram_tensor("residual", (T, D), F32, kind="Internal").ap()
        gates_dram = nc.dram_tensor("gates", (KEYS, KEYS, T), F32, kind="Internal").ap()
        act_dram = nc.dram_tensor("activations", (KEYS, KEYS, T), F32, kind="Internal").ap()
        token_pass(nc, tl, "ffn", h, None, 1, gain(2), ident, None, None, (xn_hi, xn_lo), None, h_dram)
        residual.close()
        late = ExitStack()
        dense_late = tl.sb(late, "dense_late", [P, KEYS, P // 2])
        lists = ExitStack()
        top_v = tl.sb(lists, "top_v", [P, NT, HC, TOPK])
        top_i = tl.sb(lists, "top_i", [P, NT, HC, TOPK], BF16)
        peer_scores(nc, tl, d["w_query"], d["sub_keys"], xn_hi, xn_lo, top_v, top_i)
        tl.recycle()
        dense_stored = tl.pair("dense_stored")
        experts_up(nc, tl, d["expert_u"], d["iota"], xn_hi, xn_lo, top_v, top_i, ident, act_dram, gates_dram,
                   dense_late, dense_stored)
        lists.close()
        experts.close()
        h = tl.sb(residual, "h_again", [P, NT, D], F32, "right")
        expert_down(nc, tl, d["expert_v"], act_dram, gates_dram, h, h_dram, dense_late,
                    dense_stored[1])
        late.close()
        last = ExitStack()
        pt = tl.sb(last, "pt", [P, 2, T])
        pw = tl.sb(last, "pw", [P, 2, D])
        final_gain = tl.sb(last, "final_gain", [P, D])
        input_loaded = tl.sem("input_loaded")
        load_layer_input(nc, d["w_ple_proj"], d["p_t"], d["norm_final_g"], pt, pw, final_gain, input_loaded)
        logit = tl.sb(last, "logit", [P, NT, D])

        def keep_logit(dve, s, t, o):
            return dve.tensor_copy(logit[:, t, :], o[:].rearrange("p n w -> p (n w)"))

        token_pass(nc, tl, "ple", h, None, 1, gain(3), ident, (2, HALF), d["w_ple_gate"], None, keep_logit)
        last_norm(nc, tl, h, logit, pt, pw, final_gain, input_loaded, eps, out)
        last.close()
        residual.close()



def layouts(i):
    def contiguous(a):
        return np.ascontiguousarray(a)

    w_in = np.asarray(i["w_in"])[0]
    swa_k0 = SWA_HEADS * HEAD
    swa_v0 = swa_k0 + SWA_KV * HEAD
    fox_q0 = swa_v0 + SWA_KV * HEAD
    fox_k0 = fox_q0 + FOX_HEADS * HEAD
    fox_v0 = fox_k0 + FOX_HEADS * HEAD
    forget0 = fox_v0 + FOX_HEADS * HEAD
    cols = []
    for c in range(PAIRS):
        for head in (c, c + SWA_HEADS // SWA_KV):
            cols += range(head * HEAD, (head + 1) * HEAD)
    cols += range(swa_k0, swa_v0)
    cols += range(fox_q0, fox_v0)
    v_cols = list(range(swa_v0, fox_q0)) + list(range(fox_v0, forget0 + FOX_HEADS))

    def chunked(w):
        return contiguous(w.reshape(DC, P, -1, P).transpose(2, 1, 0, 3))

    gains = [i["norm_mix_g"][0], np.concatenate([i["g_out_a"][0], i["g_out_b"][0]]), i["norm_ffn_g"][0],
             i["norm_ple_g"][0]]
    return {
        "x": contiguous(i["x"][0]),
        "gains": contiguous(np.stack([np.asarray(g).reshape(DC, P).T for g in gains], 1)),
        "w_v": contiguous(w_in[:, v_cols].reshape(DC, P, V_COLS)),
        "w_qk": chunked(w_in[:, cols]),
        "b_forget": contiguous(i["b_forget"][0]),
        "sinks": contiguous(np.asarray(i["sinks"])[0].reshape(2, PAIRS).T),
        "expert_u": contiguous(np.asarray(i["expert_u"])[0].reshape(KEYS, KEYS, DC, P).transpose(1, 3, 2, 0)),
        "expert_v": contiguous(np.asarray(i["expert_v"])[0]),
        "w_query": chunked(np.asarray(i["w_query"])[0]),
        "sub_keys": contiguous(np.asarray(i["sub_keys"])[0].transpose(0, 2, 1)),
        "w_ple_gate": contiguous(np.asarray(i["w_ple_gate"])[0].reshape(DC, P, D)),
        "w_ple_proj": contiguous(np.asarray(i["w_ple_proj"])[0]),
        "p_t": contiguous(np.asarray(i["p"])[0, 0].T),
        "norm_final_g": contiguous(i["norm_final_g"]),
        "w_out": contiguous(np.asarray(i["w_out"])[0].reshape(DC, P, D)),
    }


def constants():
    pos = np.arange(T, dtype=np.float32)
    freq = (np.float32(10000.0) ** (-np.arange(0, HEAD, 2, dtype=np.float32) / np.float32(HEAD))).astype(np.float32)
    ang = (pos[:, None] * freq[None, :]).astype(np.float32)
    feature = np.arange(P)
    cos = np.cos(ang).astype(np.float32).T[feature % (HEAD // 2)]
    sin = np.sin(ang).astype(np.float32).T[feature % (HEAD // 2)]
    first = (feature % HEAD) < HEAD // 2
    sin = np.where(first[:, None], -sin, sin).astype(np.float32)
    partner = np.where(first, feature + HEAD // 2, feature - HEAD // 2)
    perm = np.zeros((P, P), np.float32)
    perm[partner, feature] = 1.0
    q, k = np.arange(P)[:, None], np.arange(P)[None, :]
    masks = np.concatenate([np.where(k > q, 0.0, NEG), np.where(k <= q, 0.0, NEG)], 1).astype(np.float32)
    row = np.arange(4 * FOX_HEADS)
    return {
        "ident": np.eye(P, dtype=np.float32),
        "masks": masks,
        "iota": np.tile(np.arange(KEYS, dtype=np.float32), (P, 1)),
        "perm": perm,
        "head_pick": (row[:, None] % FOX_HEADS == np.arange(FOX_HEADS)[None, :]).astype(np.float32),
        "cos": np.ascontiguousarray(cos),
        "sin": np.ascontiguousarray(sin),
        "tri": (np.arange(P)[:, None] <= np.arange(-(T - P), T)[None, :]).astype(np.float32),
    }


def kernel(**inputs):
    import concourse.bacc as _bacc
    from concourse.bass_utils import run_bass_kernel_spmd as _run

    nc = _bacc.Bacc("TRN2", target_bir_lowering=False, num_devices=1)
    arrays = {**layouts({n: np.asarray(a) for n, a in inputs.items()}), **constants()}
    dram = {n: nc.dram_tensor(f"in_{n}", a.shape, mybir.dt.from_np(a.dtype), kind="ExternalInput").ap()
            for n, a in arrays.items()}
    out = nc.dram_tensor("out", (T, D), F32, kind="ExternalOutput").ap()
    program(nc, dram, out)
    r = _run(nc, [{f"in_{n}": a for n, a in arrays.items()}], core_ids=[0])
    return r.results[0]["out"].reshape(1, T, D)
```
